# Optimizing a Trainium2 kernel written in Bass

```python
import math
import jax, jax.numpy as jnp
from jax import lax
import numpy as np

D_MODEL = 1024
BATCH = 1
SEQ = 1024
DEPTH = 1
DEC_BATCH = 8
DEC_SEQ = 1
PAST_LEN = 4096
PAGE_SIZE = 128

HEAD_DIM = 64
N_HEADS = D_MODEL // HEAD_DIM
MIX_WIDTH = N_HEADS * HEAD_DIM
NSA_HEADS = N_HEADS // 2
SB_HEADS = N_HEADS - NSA_HEADS
NSA_KV_HEADS = 2
NSA_GROUP = NSA_HEADS // NSA_KV_HEADS
CMP_BLOCK = 32
CMP_STRIDE = 16
CMP_HIDDEN = 2 * HEAD_DIM
SEL_BLOCK = 64
N_SEL = 16
N_LOCAL_FORCED = 2
WINDOW = 512
Q_BLOCK = 128
SEL_Q_BLOCK = 64
D_FF = ((8 * D_MODEL + 3 * 256 - 1) // (3 * 256)) * 256
ROPE_THETA = 10000.0
EPS = 1e-6
NEG = -1e30

Q_NSA_W = NSA_HEADS * HEAD_DIM
KV_NSA_W = 3 * 2 * NSA_KV_HEADS * HEAD_DIM
GATE_W = 3 * NSA_HEADS
SB_W = 3 * SB_HEADS * HEAD_DIM
OFF_KV = Q_NSA_W
OFF_GATE = OFF_KV + KV_NSA_W
OFF_SB = OFF_GATE + GATE_W
PROJ_W = OFF_SB + SB_W

kernel_name = 'hymba_nsa_stickbreaking_decode_step'

def rms_norm(x, g):
    x32 = x.astype(jnp.float32)
    y = x32 * lax.rsqrt(jnp.mean(x32 * x32, axis=-1, keepdims=True) + EPS)
    return (y * g.astype(jnp.float32)).astype(x.dtype)

def rope(x, pos):
    half = HEAD_DIM // 2
    inv = jnp.exp(-math.log(ROPE_THETA) * jnp.arange(0, HEAD_DIM, 2, dtype=jnp.float32) / HEAD_DIM)
    ang = pos.astype(jnp.float32)[:, None] * inv[None, :]
    shape = (ang.shape[0],) + (1,) * (x.ndim - 3) + (half,)
    cos, sin = jnp.cos(ang).reshape(shape), jnp.sin(ang).reshape(shape)
    x32 = x.astype(jnp.float32)
    x1, x2 = x32[..., :half], x32[..., half:]
    return jnp.concatenate([x1 * cos - x2 * sin, x1 * sin + x2 * cos], axis=-1).astype(x.dtype)

def project(xn, pos, w_in, g_q, g_k):
    B, T, _ = xn.shape
    p = xn @ w_in
    q = p[..., :OFF_KV].reshape(B, T, NSA_HEADS, HEAD_DIM)
    kv = p[..., OFF_KV:OFF_GATE].reshape(B, T, 3, 2, NSA_KV_HEADS, HEAD_DIM)
    gates = jax.nn.sigmoid(p[..., OFF_GATE:OFF_SB]).reshape(B, T, NSA_HEADS, 3)
    sb = p[..., OFF_SB:].reshape(B, T, 3, SB_HEADS, HEAD_DIM)
    q = rope(rms_norm(q, g_q), pos)
    k = rope(rms_norm(kv[:, :, :, 0], g_k[:, None, :]), pos)
    v = kv[:, :, :, 1]
    nsa_rows = jnp.stack([k[:, :, 0], v[:, :, 0], k[:, :, 1], v[:, :, 1]], axis=2)
    win_rows = jnp.stack([k[:, :, 2], v[:, :, 2]], axis=2)
    return q, gates, nsa_rows, win_rows, sb[:, :, 0], sb[:, :, 1:]

def query_blocked(fn, q, q_pos, block):
    B, T = q.shape[:2]
    if T <= block or T % block:
        return fn(q, q_pos)
    n = T // block
    qb = q.reshape((B, n, block) + q.shape[2:]).swapaxes(0, 1)
    out = lax.map(lambda a: fn(a[0], a[1]), (qb, q_pos.reshape(n, block)))
    return jax.tree_util.tree_map(lambda o: o.swapaxes(0, 1).reshape((B, T) + o.shape[3:]), out)

def compress(rows, w1, w2, pe):
    B, L = rows.shape[:2]
    nc = (L - CMP_BLOCK) // CMP_STRIDE + 1
    idx = jnp.arange(nc)[:, None] * CMP_STRIDE + jnp.arange(CMP_BLOCK)[None, :]
    blk = rows[:, idx] + pe[:, None, :]
    blk = blk.transpose(0, 1, 3, 2, 4).reshape(B, nc, NSA_KV_HEADS, CMP_BLOCK * HEAD_DIM)
    return jax.nn.gelu(blk @ w1) @ w2

def to_blocks(rows, nb):
    B, L = rows.shape[:2]
    rows = jnp.pad(rows, ((0, 0), (0, nb * SEL_BLOCK - L), (0, 0), (0, 0)))
    return rows.reshape(B, nb, SEL_BLOCK, NSA_KV_HEADS, HEAD_DIM).transpose(0, 3, 1, 2, 4)

def overlap_matrix(nc, nb):
    c = jnp.arange(nc)[:, None] * CMP_STRIDE
    j = jnp.arange(nb)[None, :] * SEL_BLOCK
    return ((c < j + SEL_BLOCK) & (c + CMP_BLOCK > j)).astype(jnp.float32)

def nsa_query_block(q, q_pos, kc, vc, c_end, kb, vb, overlap):
    B, Tq = q.shape[:2]
    nb = kb.shape[2]
    scale = HEAD_DIM ** -0.5
    qg = q.reshape(B, Tq, NSA_KV_HEADS, NSA_GROUP, HEAD_DIM)
    s = jnp.einsum('btgqd,bcgd->bgqtc', qg, kc).astype(jnp.float32) * scale
    cmask = c_end[None, :] <= q_pos[:, None]
    p = jax.nn.softmax(jnp.where(cmask, s, NEG), axis=-1) * cmask
    o_cmp = jnp.einsum('bgqtc,bcgd->btgqd', p.astype(vc.dtype), vc)
    imp = jnp.einsum('bgqtc,cj->bgtj', p, overlap)
    qblk = q_pos // SEL_BLOCK
    j = jnp.arange(nb)
    future = j[None, :] > qblk[:, None]
    forced = (j[None, :] == 0) | (j[None, :] > qblk[:, None] - N_LOCAL_FORCED)
    score = jnp.where(future, -jnp.inf, jnp.where(forced, jnp.inf, imp))
    top_val, top_idx = lax.top_k(score, min(N_SEL, nb))
    valid = top_val > -jnp.inf
    gather = jax.vmap(jax.vmap(lambda blocks, ix: blocks[ix]))
    ks = gather(kb, top_idx)
    vs = gather(vb, top_idx)
    ss = jnp.einsum('btgqd,bgtksd->bgqtks', qg, ks).astype(jnp.float32) * scale
    kpos = top_idx[..., None] * SEL_BLOCK + jnp.arange(SEL_BLOCK)
    smask = ((kpos <= q_pos[None, None, :, None, None]) & valid[..., None])[:, :, None]
    ss = jnp.where(smask, ss, NEG)
    nk = ss.shape[-2]
    ps = jax.nn.softmax(ss.reshape(ss.shape[:-2] + (nk * SEL_BLOCK,)), axis=-1).reshape(ss.shape)
    o_slc = jnp.einsum('bgqtks,bgtksd->btgqd', ps.astype(vs.dtype), vs)
    return (o_cmp.reshape(B, Tq, NSA_HEADS, HEAD_DIM), o_slc.reshape(B, Tq, NSA_HEADS, HEAD_DIM))

def nsa_context(q, q_pos, rows, w_ck1, w_ck2, pe_ck, w_cv1, w_cv2, pe_cv):
    L = rows.shape[1]
    kc = compress(rows[:, :, 0], w_ck1, w_ck2, pe_ck)
    vc = compress(rows[:, :, 1], w_cv1, w_cv2, pe_cv)
    nc = kc.shape[1]
    c_end = jnp.arange(nc) * CMP_STRIDE + (CMP_BLOCK - 1)
    nb = -(-L // SEL_BLOCK)
    kb = to_blocks(rows[:, :, 2], nb)
    vb = to_blocks(rows[:, :, 3], nb)
    ov = overlap_matrix(nc, nb)
    return query_blocked(lambda qq, pp: nsa_query_block(qq, pp, kc, vc, c_end, kb, vb, ov), q, q_pos, SEL_Q_BLOCK)

def window_attend(q, q_pos, k, v, k_pos):
    B, Tq = q.shape[:2]
    qg = q.reshape(B, Tq, NSA_KV_HEADS, NSA_GROUP, HEAD_DIM)
    s = jnp.einsum('btgqd,bsgd->bgqts', qg, k).astype(jnp.float32) * HEAD_DIM ** -0.5
    kp, qp = k_pos[None, :], q_pos[:, None]
    mask = (kp <= qp) & (kp >= qp - WINDOW) & (kp >= 0)
    p = jax.nn.softmax(jnp.where(mask, s, NEG), axis=-1)
    return jnp.einsum('bgqts,bsgd->btgqd', p.astype(v.dtype), v).reshape(B, Tq, NSA_HEADS, HEAD_DIM)

def sb_attend(q, q_pos, k, v, k_pos):
    z = jnp.einsum('bthd,bshd->bhts', q, k).astype(jnp.float32) * HEAD_DIM ** -0.5
    mask = k_pos[None, :] < q_pos[:, None]
    log_1m = jnp.where(mask, jax.nn.log_sigmoid(-z), 0.0)
    suffix = lax.cumsum(log_1m, axis=3, reverse=True) - log_1m
    a = jnp.where(mask, jnp.exp(jax.nn.log_sigmoid(z) + suffix), 0.0)
    return jnp.einsum('bhts,bshd->bthd', a.astype(v.dtype), v)

def finish(x, gates, o_cmp, o_slc, o_win, o_sb, g_on, g_os, w_out, g_ffn, w_gu, w_down):
    B, T, _ = x.shape
    o_nsa = gates[..., 0:1] * o_cmp + gates[..., 1:2] * o_slc + gates[..., 2:3] * o_win
    mix = jnp.concatenate([rms_norm(o_nsa, g_on), rms_norm(o_sb, g_os)], axis=2).reshape(B, T, MIX_WIDTH)
    h = x + mix @ w_out
    gu = rms_norm(h, g_ffn) @ w_gu
    return h + (jax.nn.silu(gu[..., :D_FF]) * gu[..., D_FF:]) @ w_down

def gather_pages(pool, page_table):
    rows = pool[page_table]
    return rows.reshape((page_table.shape[0], -1) + pool.shape[2:])

def layer_step(xp, xs, c_nsa, c_sb, s_win, page_table, g_attn, w_in, g_q, g_k,
               w_ck1, w_ck2, pe_ck, w_cv1, w_cv2, pe_cv, g_on, g_os, w_out, g_ffn, w_gu, w_down):
    cmp_w = (w_ck1, w_ck2, pe_ck, w_cv1, w_cv2, pe_cv)
    out_w = (g_on, g_os, w_out, g_ffn, w_gu, w_down)
    seq = xp.shape[1]
    pos_p = jnp.arange(seq, dtype=jnp.int32)
    q, gates, nsa_p, win_p, q_sb, sb_p = project(rms_norm(xp, g_attn), pos_p, w_in, g_q, g_k)
    o_cmp, o_slc = nsa_context(q, pos_p, nsa_p, *cmp_w)
    kpad = jnp.pad(win_p, ((0, 0), (WINDOW, 0), (0, 0), (0, 0), (0, 0)))

    def win_block(qq, pp):
        n = WINDOW + qq.shape[1]
        kw = lax.dynamic_slice_in_dim(kpad, pp[0], n, axis=1)
        return window_attend(qq, pp, kw[:, :, 0], kw[:, :, 1], pp[0] - WINDOW + jnp.arange(n, dtype=jnp.int32))

    o_win = query_blocked(win_block, q, pos_p, Q_BLOCK)
    o_sb = query_blocked(lambda qq, pp: sb_attend(qq, pp, sb_p[:, :, 0], sb_p[:, :, 1], pos_p), q_sb, pos_p, Q_BLOCK)
    yp = finish(xp, gates, o_cmp, o_slc, o_win, o_sb, *out_w)
    win_keep_p = win_p[:, seq - min(WINDOW, seq):]
    dseq = xs.shape[1]
    pos_s = PAST_LEN + jnp.arange(dseq, dtype=jnp.int32)
    q_s, gates_s, nsa_s, win_s, q_sb_s, sb_s = project(rms_norm(xs, g_attn), pos_s, w_in, g_q, g_k)
    nsa_all = jnp.concatenate([gather_pages(c_nsa, page_table), nsa_s], axis=1)
    o_cmp_s, o_slc_s = nsa_context(q_s, pos_s, nsa_all, *cmp_w)
    wb = s_win.shape[1]
    win_all = jnp.concatenate([s_win, win_s], axis=1)
    o_win_s = window_attend(q_s, pos_s, win_all[:, :, 0], win_all[:, :, 1],
                            PAST_LEN - wb + jnp.arange(wb + dseq, dtype=jnp.int32))
    sb_all = jnp.concatenate([gather_pages(c_sb, page_table), sb_s], axis=1)
    k_pos_s = jnp.arange(PAST_LEN + dseq, dtype=jnp.int32)
    o_sb_s = query_blocked(lambda qq, pp: sb_attend(qq, pp, sb_all[:, :, 0], sb_all[:, :, 1], k_pos_s),
                           q_sb_s, pos_s, Q_BLOCK)
    ys = finish(xs, gates_s, o_cmp_s, o_slc_s, o_win_s, o_sb_s, *out_w)
    return (yp, ys, nsa_p, nsa_s, sb_p, sb_s, win_keep_p, win_all[:, dseq:])

def setup_inputs(seed: int = 0) -> dict:
    key = jax.random.key(seed)
    ks = jax.random.split(key, 24)
    n_pages = PAST_LEN // PAGE_SIZE
    n_pool = (DEC_BATCH * n_pages * 5) // 4
    wb = min(WINDOW, PAST_LEN)
    f32 = jnp.float32

    def w(k, shape, fan_in):
        return jax.random.normal(k, (DEPTH,) + shape, f32) * fan_in ** -0.5

    def g(k, shape):
        return 1.0 + 0.02 * jax.random.normal(k, (DEPTH,) + shape, f32)

    page_table = jax.random.permutation(ks[5], n_pool)[:DEC_BATCH * n_pages].reshape(DEC_BATCH, n_pages).astype(jnp.int32)
    return {
        'x_prompt': jax.random.normal(ks[0], (BATCH, SEQ, D_MODEL), f32),
        'x_sample': jax.random.normal(ks[1], (DEC_BATCH, DEC_SEQ, D_MODEL), f32),
        'cache_nsa_kv': jax.random.normal(ks[2], (DEPTH, n_pool, PAGE_SIZE, 4, NSA_KV_HEADS, HEAD_DIM), f32),
        'cache_sb_kv': jax.random.normal(ks[3], (DEPTH, n_pool, PAGE_SIZE, 2, SB_HEADS, HEAD_DIM), f32),
        'state_nsa_window': jax.random.normal(ks[4], (DEPTH, DEC_BATCH, wb, 2, NSA_KV_HEADS, HEAD_DIM), f32),
        'page_table': page_table,
        'g_attn': g(ks[6], (D_MODEL,)),
        'w_in': w(ks[7], (D_MODEL, PROJ_W), D_MODEL),
        'g_q': g(ks[8], (HEAD_DIM,)),
        'g_k': g(ks[9], (3, HEAD_DIM)),
        'w_cmp1_k': w(ks[10], (CMP_BLOCK * HEAD_DIM, CMP_HIDDEN), CMP_BLOCK * HEAD_DIM),
        'w_cmp2_k': w(ks[11], (CMP_HIDDEN, HEAD_DIM), CMP_HIDDEN),
        'pe_cmp_k': 0.02 * jax.random.normal(ks[12], (DEPTH, CMP_BLOCK, HEAD_DIM), f32),
        'w_cmp1_v': w(ks[13], (CMP_BLOCK * HEAD_DIM, CMP_HIDDEN), CMP_BLOCK * HEAD_DIM),
        'w_cmp2_v': w(ks[14], (CMP_HIDDEN, HEAD_DIM), CMP_HIDDEN),
        'pe_cmp_v': 0.02 * jax.random.normal(ks[15], (DEPTH, CMP_BLOCK, HEAD_DIM), f32),
        'g_out_nsa': g(ks[16], (NSA_HEADS, HEAD_DIM)),
        'g_out_sb': g(ks[17], (SB_HEADS, HEAD_DIM)),
        'w_out': w(ks[18], (MIX_WIDTH, D_MODEL), MIX_WIDTH),
        'g_ffn': g(ks[19], (D_MODEL,)),
        'w_gate_up': w(ks[20], (D_MODEL, 2 * D_FF), D_MODEL),
        'w_down': w(ks[21], (D_FF, D_MODEL), D_FF),
    }

def reference(x_prompt, x_sample, cache_nsa_kv, cache_sb_kv, state_nsa_window, page_table,
              g_attn, w_in, g_q, g_k, w_cmp1_k, w_cmp2_k, pe_cmp_k, w_cmp1_v, w_cmp2_v, pe_cmp_v,
              g_out_nsa, g_out_sb, w_out, g_ffn, w_gate_up, w_down):
    hp, hs = x_prompt, x_sample
    nsa_p_l, nsa_s_l, sb_p_l, sb_s_l, win_p_l, win_s_l = [], [], [], [], [], []
    for l in range(DEPTH):
        hp, hs, nsa_p, nsa_s, sb_p, sb_s, win_p, win_s = layer_step(
            hp, hs, cache_nsa_kv[l], cache_sb_kv[l], state_nsa_window[l], page_table,
            g_attn[l], w_in[l], g_q[l], g_k[l], w_cmp1_k[l], w_cmp2_k[l], pe_cmp_k[l],
            w_cmp1_v[l], w_cmp2_v[l], pe_cmp_v[l], g_out_nsa[l], g_out_sb[l], w_out[l],
            g_ffn[l], w_gate_up[l], w_down[l])
        nsa_p_l.append(nsa_p)
        nsa_s_l.append(nsa_s)
        sb_p_l.append(sb_p)
        sb_s_l.append(sb_s)
        win_p_l.append(win_p)
        win_s_l.append(win_s)
    return (hp, hs, jnp.stack(nsa_p_l), jnp.stack(nsa_s_l), jnp.stack(sb_p_l), jnp.stack(sb_s_l),
            jnp.stack(win_p_l), jnp.stack(win_s_l))


_drawn_inputs = setup_inputs


def setup_inputs(seed=0):
    import zlib

    import numpy as np

    out = dict(_drawn_inputs(seed))
    spreads = {}
    factors = {'g_q': 3.627,
     'g_k': 3.821,
     'pe_cmp_k': 5.545,
     'pe_cmp_v': 2.765,
     'g_out_nsa': 5.073,
     'g_out_sb': 5.381,
     'g_ffn': 5.072}
    for name, (base, spread) in spreads.items():
        noise = np.random.default_rng([zlib.crc32(name.encode()), seed]).standard_normal(out[name].shape)
        drawn = base * np.exp(spread * noise) if base else spread * noise
        out[name] = __import__('jax').numpy.asarray(drawn.astype(out[name].dtype))
    for name, factor in factors.items():
        out[name] = (out[name] * factor).astype(out[name].dtype)
    return out
```

```python
import math
from contextlib import ExitStack

import numpy as np
import concourse.bass as bass
from concourse import mybir

F32 = mybir.dt.float32
BF16 = mybir.dt.bfloat16
I32 = mybir.dt.int32
U32 = mybir.dt.uint32
ALU = mybir.AluOpType
ACT = mybir.ActivationFunctionType
AX = mybir.AxisListType

P = 128
D = 1024
SEQ = 1024
NB = 8
PAST = 4096
PAGE = 128
NPAGE = PAST // PAGE
NPOOL = NB * NPAGE * 5 // 4
HD = 64
NH = 8
KVH = 2
GRP = NH // KVH
WINDOW = 512
DFF = 2816
PROJ = 2840
KT = D // P
TILES = SEQ // P
NCP = (SEQ - 32) // 16 + 1
NCS = (PAST + 1 - 32) // 16 + 1
NBLK = PAST // 64
NSEL = 15
EPS = 1e-6
NEG = -1e30
SCALE = HD ** -0.5

COLS = [(0, 512), (512, 1024), (1024, 1304), (1304, 1816), (1816, 2328), (2328, 2840)]
GATE0, SBQ0, SBK0 = 1280, 1304, 1816
T_QN, T_KS, T_KW, T_QS, T_KB = 0, 8, 10, 12, 20
NT = 28
TOK = SEQ + NB


def constants():
    inv = np.exp(-math.log(10000.0) * np.arange(0, HD, 2, dtype=np.float32) / HD).astype(np.float32)
    pos = np.concatenate([np.arange(SEQ), np.full(P, PAST)]).astype(np.float32)
    ang = pos[:, None] * inv[None, :]
    rot = np.stack([np.cos(ang), np.sin(ang)], 1).astype(np.float32)
    i, j = np.arange(P)[:, None], np.arange(P)[None, :]
    masks = np.zeros((P, 3, P), np.float32)
    masks[:, 0] = np.where(j > i, NEG, 0)
    masks[:, 1] = np.where(j >= i, NEG, 0)
    masks[:, 2] = np.where(j < i, NEG, 0)
    cend = np.arange(64) * 16 + 31
    cmask = np.where(cend[None, :] <= np.arange(SEQ)[:, None], 0, NEG).astype(np.float32)
    cmask = cmask.reshape(TILES, P, 64).transpose(1, 0, 2)
    rowok = (np.arange(P) >= 31).astype(np.float32)[:, None]
    c = np.arange(256)[:, None] * 16
    b = np.arange(NBLK)[None, :] * 64
    ov = ((c < b + 64) & (c + 32 > b)).astype(np.float32)
    ov[NCS:] = 0
    ov = ov.reshape(2, P, NBLK).transpose(1, 0, 2)
    k, r = np.arange(NBLK), np.arange(16)
    sel = np.zeros((NBLK, 3, NBLK), np.float32)
    sel[:, 0] = np.eye(NBLK)
    sel[:, 1] = (k[None, :] < k[:, None])
    sel[:, 2] = np.where((k == 0) | (k == NBLK - 1), 1e30, 0)[None, :]
    ranks = np.broadcast_to(r, (NBLK, 16)).astype(np.float32)
    blk = np.stack([(k // 2), (k % 2)], 1).astype(np.float32)
    pageof = (np.arange(NPAGE)[:, None] == (k // 2)[None, :]).astype(np.float32)
    off = np.stack([(np.arange(P) < 64), (np.arange(P) >= 64), (np.arange(P) % 64) * 8], 1).astype(np.float32)
    tri = (i >= j).astype(np.float32)
    selrow = np.zeros((NB, NB, 512), np.float32)
    diag = np.zeros((NH, NH, HD), np.float32)
    for h in range(NH):
        diag[h, h] = 1
    return {
        "c_rot": rot.reshape(TILES + 1, P, 64), "c_ident": np.eye(P, dtype=np.float32),
        "c_masks": masks, "c_cmask": cmask, "c_rowok": rowok, "c_ov": ov, "c_sel": sel,
        "c_ranks": ranks, "c_blk": blk, "c_pageof": pageof, "c_off": off, "c_tri": tri, "c_diag": diag,
    }


def project(nc, io, g):
    with ExitStack() as ctx:
        sb = lambda n, s, t=F32: ctx.enter_context(nc.sbuf_tensor(n, s, t))
        ps = lambda n, s, t=F32: ctx.enter_context(nc.psum_tensor(n, s, t))
        sem = lambda n: g["sem"](n)
        w = sb("w_in_sb", [P, KT, PROJ])
        x = sb("x_sb", [P, 2, D])
        xn = sb("xn_sb", [P, 2, D])
        xT = sb("xT_sb", [P, 2, KT, P])
        pj = sb("proj_sb", [P, 2, PROJ])
        junk = sb("squares_sb", [P, D])
        ss = sb("ss_sb", [P, 2, 2])
        half = sb("minus_half", [P, 16])
        rot = sb("rot_sb", [P, 2, 64])
        gat = sb("g_attn_col", [P, KT])
        gqk = sb("g_qk_sb", [P, 14, HD])
        sq = sb("qk_squares", [P, 14, HD])
        hss = sb("head_ss", [P, 2, 16])
        r1 = sb("normed", [P, 14, HD])
        ra = sb("rot_a", [P, 14, HD])
        rb = sb("rot_b", [P, 14, HD])
        ro = sb("roped", [P, 2, 14, HD])
        kvo = sb("kv_out", [P, 2, 6, P])
        ts = sb("transposed", [P, 2, 14, P])
        sbq = sb("sb_q_scaled", [NB, 512])
        px = ps("px", [P, 2, 512])
        pp = ps("pp", [P, 4, 512])
        pt = ps("pt", [P, 2, 512])
        w_loaded = [sem(f"w_loaded{c}") for c in range(6)]
        c_loaded = sem("c_loaded")
        x_loaded = [sem("x_loaded0"), sem("x_loaded1")]
        x_squared, x_rstd, x_normed, x_turned, x_ready = map(sem, ("x_squared", "x_rstd", "x_normed", "x_turned", "x_ready"))
        proj_done, proj_saved = map(sem, ("proj_done", "proj_saved"))
        qk_squared, qk_summed, qk_rstd, roped, kv_copied = map(sem, ("qk_squared", "qk_summed", "qk_rstd", "roped", "kv_copied"))
        turned, turned_saved, sbq_scaled = map(sem, ("turned", "turned_saved", "sbq_scaled"))
        stored = [sem("stored0"), sem("stored1")]
        NTILE = TILES + 1
        rows = lambda n: P if n < TILES else NB
        ident = g["ident"]

        with nc.Block() as block:
            @block.sync
            def _(eng):
                eng.dma_start(gat[:, :], io["g_attn"].rearrange("a (k p) -> p (a k)", p=P), allow_slow_non_contiguous=True).then_inc(c_loaded, 16)
                for h in range(8):
                    eng.dma_start(gqk[:, h, :], io["g_q"][0].partition_broadcast(P)).then_inc(c_loaded, 16)
                for r in range(3):
                    for j in range(2):
                        eng.dma_start(gqk[:, 8 + 2 * r + j, :], io["g_k"][0, r].partition_broadcast(P)).then_inc(c_loaded, 16)
                def load(n):
                    R, u = rows(n), n % 2
                    if n >= 2:
                        eng.wait_ge(x_normed, n - 1)
                        eng.wait_ge(roped, n - 1)
                    src = io["x_prompt"][0, n * P:(n + 1) * P, :] if n < TILES else io["x_sample"].rearrange("b t d -> (b t) d")
                    eng.dma_start(x[0:R, u, :], src).then_inc(x_loaded[u], 16)
                    eng.dma_start(rot[0:R, u, :], io["c_rot"][n, 0:R]).then_inc(x_loaded[u], 16)

                def store(n):
                    R, u, t0 = rows(n), n % 2, n * P
                    k4 = kvo[0:R, u, 0:4, :].rearrange("p r e -> p (r e)")
                    k2 = kvo[0:R, u, 4:6, :].rearrange("p r e -> p (r e)")
                    last = n == TILES
                    eng.wait_ge(kv_copied, n + 1)
                    eng.dma_start(io["nsa_s"] if last else io["nsa_p"][t0:t0 + R, :], k4).then_inc(stored[u], 16)
                    eng.dma_start(io["win_new"] if last else io["win_p"][t0:t0 + R, :], k2).then_inc(stored[u], 16)
                    eng.wait_ge(proj_saved, 6 * n + 6)
                    eng.dma_start(io["sb_s"] if last else io["sb_p"][t0:t0 + R, :], pj[0:R, u, SBK0:PROJ]).then_inc(stored[u], 16)
                    eng.wait_ge(turned_saved, 4 * n + 4)
                    if last:
                        eng.dma_start(io["Ts"].rearrange("(m p) t -> p m t", p=P), ts[:, u, :, 0:R], allow_slow_non_contiguous=True).then_inc(stored[u], 16)
                        eng.wait_ge(sbq_scaled, 1)
                        eng.dma_start(io["sbq_s"], sbq[:, :]).then_inc(stored[u], 16)
                    else:
                        eng.dma_start(io["T"].rearrange("(m p) t -> p m t", p=P)[:, :, t0:t0 + R], ts[:, u, :, :]).then_inc(stored[u], 16)

                load(0)
                wv = io["w_in"][0].rearrange("(k p) n -> p k n", p=P)
                for c, (a, b) in enumerate(COLS):
                    eng.dma_start(w[:, :, a:b], wv[:, :, a:b]).then_inc(w_loaded[c], 16)
                load(1)
                for n in range(NTILE):
                    if n + 2 < NTILE:
                        load(n + 2)
                    store(n)
                eng.wait_ge(stored[0], 64 * 5 + 16)
                eng.wait_ge(stored[1], 64 * 4)

            @block.gpsimd
            def _(eng):
                eng.memset(half[:, :], -0.5)
                eng.drain()

                def head_norm(n):
                    R, u = rows(n), n % 2
                    eng.wait_ge(qk_summed, n + 1)
                    eng.tensor_scalar(hss[0:R, u, 0:14], hss[0:R, u, 0:14], 1.0 / HD, EPS, ALU.mult, ALU.add)
                    eng.drain()
                    eng.tensor_tensor(hss[0:R, u, 0:14], hss[0:R, u, 0:14], half[0:R, 0:14], ALU.pow).then_inc(qk_rstd, 1)

                def join_rows(n):
                    R, u = rows(n), n % 2
                    eng.wait_ge(roped, n + 1)
                    eng.wait_ge(proj_saved, 6 * n + 6)
                    if n >= 2:
                        eng.wait_ge(stored[u], 64 * (n // 2))
                    rv = ro[0:R, u, 8:14, :].rearrange("p (r j) d -> p r (j d)", j=2)
                    kv = kvo[0:R, u, :, :].rearrange("p (r c) e -> p r c e", c=2)
                    pv = pj[0:R, u, 512:1280].rearrange("p (r c e) -> p r c e", r=3, c=2)
                    eng.tensor_copy(kv[:, :, 0, :], rv)
                    eng.tensor_copy(kv[:, :, 1, :], pv[:, :, 1, :]).then_inc(kv_copied, 1)

                for n in range(NTILE):
                    R, u = rows(n), n % 2
                    eng.wait_ge(x_squared, n + 1)
                    eng.tensor_scalar(ss[0:R, u, 1:2], ss[0:R, u, 0:1], 1.0 / D, EPS, ALU.mult, ALU.add)
                    eng.drain()
                    eng.tensor_tensor(ss[0:R, u, 1:2], ss[0:R, u, 1:2], half[0:R, 0:1], ALU.pow).then_inc(x_rstd, 1)
                    if n >= 1:
                        head_norm(n - 1)
                        join_rows(n - 1)
                head_norm(TILES)
                join_rows(TILES)

            @block.scalar
            def _(eng):
                def square(n):
                    R, u = rows(n), n % 2
                    eng.wait_ge(x_loaded[u], 32 * (n // 2 + 1))
                    eng.drain()
                    eng.activation(junk[0:R, :], x[0:R, u, :], ACT.Square, accum_out=ss[0:R, u, 0:1]).then_inc(x_squared, 1)
                square(0)
                for n in range(NTILE):
                    R, u = rows(n), n % 2
                    if n + 1 < NTILE:
                        if n >= 1:
                            eng.wait_ge(x_normed, n)
                        square(n + 1)
                    for c, (a, b) in enumerate(COLS):
                        if n >= 2 and c == 0:
                            eng.wait_ge(stored[u], 64 * (n // 2))
                            eng.wait_ge(turned, 4 * (n - 1))
                            eng.wait_ge(roped, n - 1)
                        eng.wait_ge(proj_done, 6 * n + c + 1)
                        eng.activation(pj[0:R, u, a:b], pp[0:R, (6 * n + c) % 4, 0:b - a], ACT.Copy).then_inc(proj_saved, 1)
                    eng.drain()
                    if n >= 1:
                        eng.wait_ge(qk_summed, n)
                    eng.activation(sq[0:R, 0:8, :].rearrange("p h d -> p (h d)"), pj[0:R, u, 0:512], ACT.Square)
                    kk = pj[0:R, u, 512:1280].rearrange("p (r c e) -> p r c e", r=3, c=2)[:, :, 0, :]
                    eng.activation(sq[0:R, 8:14, :].rearrange("p (r j) d -> p r (j d)", j=2), kk, ACT.Square).then_inc(qk_squared, 1)
                    eng.activation(g["gates"][0:R, n, :], pj[0:R, u, GATE0:GATE0 + 24], ACT.Sigmoid)
                    if n == TILES:
                        eng.activation(sbq[:, :], pj[0:R, u, SBQ0:SBK0], ACT.Copy, scale=SCALE).then_inc(sbq_scaled, 1)

            @block.tensor
            def _(eng):
                def x_transposes(n):
                    R, u = rows(n), n % 2
                    eng.wait_ge(x_normed, n + 1)
                    for b in range(2):
                        if n >= 1:
                            eng.wait_ge(x_ready, 2 * (n - 1) + b + 1)
                        for k in range(4):
                            mm = eng.transpose(px[:, b, k * P:k * P + R], xn[0:R, u, (4 * b + k) * P:(4 * b + k + 1) * P], ident[0:R, 0:R])
                        mm.then_inc(x_turned, 1)

                def head_transposes(n):
                    R, u = rows(n), n % 2
                    eng.wait_ge(roped, n + 1)
                    for b in range(4):
                        m = 4 * n + b
                        if m >= 2:
                            eng.wait_ge(turned_saved, m - 1)
                        for k in range(4 * b, min(4 * b + 4, 14)):
                            if k < 4:
                                src = ro[0:R, u, 2 * k:2 * k + 2, :]
                            elif k < 6:
                                src = ro[0:R, u, 2 * k + 2:2 * k + 4, :]
                            else:
                                a = SBQ0 + (k - 6) * P
                                src = pj[0:R, u, a:a + P]
                            if k < 6:
                                src = src.rearrange("p h d -> p (h d)")
                            mm = eng.transpose(pt[:, m % 2, (k % 4) * P:(k % 4) * P + R], src, ident[0:R, 0:R])
                        mm.then_inc(turned, 1)

                for n in range(NTILE):
                    R, u = rows(n), n % 2
                    x_transposes(n) if n == 0 else None
                    for c, (a, b) in enumerate(COLS):
                        m = 6 * n + c
                        if c == 0:
                            eng.wait_ge(x_ready, 2 * n + 2)
                        if c == 3 and n >= 1:
                            head_transposes(n - 1)
                        if c == 4 and n + 1 < NTILE:
                            x_transposes(n + 1)
                        if n == 0:
                            eng.wait_ge(w_loaded[c], 16)
                        if m >= 4:
                            eng.wait_ge(proj_saved, m - 3)
                        for k in range(KT):
                            mm = eng.matmul(pp[0:R, m % 4, 0:b - a], xT[:, u, k, 0:R], w[:, k, a:b], start=(k == 0), stop=(k == KT - 1))
                        mm.then_inc(proj_done, 1)
                head_transposes(TILES)

            @block.vector
            def _(eng):
                eng.wait_ge(c_loaded, 16 * 15)

                def norm_x(n):
                    R, u = rows(n), n % 2
                    eng.wait_ge(x_rstd, n + 1)
                    if n >= 2:
                        eng.wait_ge(x_turned, 2 * (n - 1))
                    eng.tensor_scalar(xn[0:R, u, :], x[0:R, u, :], ss[0:R, u, 1:2], None, ALU.mult).then_inc(x_normed, 1)

                def save_xT(n):
                    R, u = rows(n), n % 2
                    if n >= 2:
                        eng.wait_ge(proj_done, 6 * (n - 1))
                    for b in range(2):
                        eng.wait_ge(x_turned, 2 * n + b + 1)
                        eng.tensor_tensor(xT[:, u, 4 * b:4 * b + 4, 0:R], px[:, b, :].rearrange("p (k r) -> p k r", k=4)[:, :, 0:R],
                                          gat[:, 4 * b:4 * b + 4].to_broadcast([P, 4, R]), ALU.mult).then_inc(x_ready, 1)

                def rotate(n):
                    R, u = rows(n), n % 2
                    eng.wait_ge(qk_squared, n + 1)
                    eng.tensor_reduce(hss[0:R, u, 0:14], sq[0:R, :, :], AX.X, ALU.add).then_inc(qk_summed, 1)
                    eng.wait_ge(qk_rstd, n + 1)
                    rs = hss[0:R, u, 0:14].to_broadcast([R, 14, HD])
                    kk = pj[0:R, u, 512:1280].rearrange("p (r c j d) -> p r c j d", r=3, c=2, j=2)
                    eng.tensor_tensor(r1[0:R, 0:8, :], pj[0:R, u, 0:512].rearrange("p (h d) -> p h d", d=HD), rs[:, 0:8, :], ALU.mult)
                    for r in range(3):
                        eng.tensor_tensor(r1[0:R, 8 + 2 * r:10 + 2 * r, :], kk[:, r, 0, :, :], rs[:, 8 + 2 * r:10 + 2 * r, :], ALU.mult)
                    eng.drain()
                    eng.tensor_tensor(r1[0:R], r1[0:R], gqk[0:R], ALU.mult)
                    eng.drain()
                    cos = rot[0:R, u:u + 1, 0:32].to_broadcast([R, 14, 32])
                    sin = rot[0:R, u:u + 1, 32:64].to_broadcast([R, 14, 32])
                    for o in (0, 32):
                        eng.tensor_tensor(ra[0:R, :, o:o + 32], r1[0:R, :, o:o + 32], cos, ALU.mult)
                        eng.tensor_tensor(rb[0:R, :, o:o + 32], r1[0:R, :, 32 - o:64 - o], sin, ALU.mult)
                    if n >= 2:
                        eng.wait_ge(turned, 4 * (n - 1))
                        eng.wait_ge(kv_copied, n - 1)
                    eng.drain()
                    eng.tensor_tensor(ro[0:R, u, :, 0:32], ra[0:R, :, 0:32], rb[0:R, :, 0:32], ALU.subtract)
                    eng.tensor_tensor(ro[0:R, u, :, 32:64], ra[0:R, :, 32:64], rb[0:R, :, 32:64], ALU.add).then_inc(roped, 1)

                def save_turned(n):
                    R, u = rows(n), n % 2
                    if n >= 2:
                        eng.wait_ge(stored[u], 64 * (n // 2))
                    for b in range(4):
                        eng.wait_ge(turned, 4 * n + b + 1)
                        cnt = min(4, 14 - 4 * b)
                        for a, e, s in ([(0, 4, SCALE)], [(0, 2, 1.0), (2, 4, SCALE)], [(0, 2, SCALE), (2, 4, 1.0)], [(0, 2, 1.0)])[b]:
                            ins = eng.tensor_scalar(ts[:, u, 4 * b + a:4 * b + e, 0:R], pt[:, b % 2, :].rearrange("p (k r) -> p k r", k=4)[:, a:e, 0:R],
                                                    s, None, ALU.mult)
                        ins.then_inc(turned_saved, 1)

                norm_x(0)
                save_xT(0)
                for n in range(NTILE):
                    if n + 1 < NTILE:
                        norm_x(n + 1)
                    if n >= 1:
                        save_turned(n - 1)
                    if n + 1 < NTILE:
                        save_xT(n + 1)
                    rotate(n)
                save_turned(TILES)


def compress(nc, io, g):
    with ExitStack() as ctx:
        sb = lambda n, s, t=F32: ctx.enter_context(nc.sbuf_tensor(n, s, t))
        ps = lambda n, s, t=F32: ctx.enter_context(nc.psum_tensor(n, s, t))
        sem = lambda n: g["sem"](n)
        RING, PAIRS = 8, NPAGE // 2
        w1 = sb("w_cmp1", [P, 2, 2, 8, P])
        w2 = sb("w_cmp2", [P, 2, HD])
        pe = sb("pe_rows", [16, 2, P])
        peT = sb("pe_cols", [P, 2, 16])
        peb = sb("pe_bias", [P, 2])
        pg = g["late"][:, 0:RING * 512].rearrange("p (s r e) -> p s r e", s=RING, r=2)
        xt = sb("rows_turned", [P, 2, 4, PAST // 2])
        hid = sb("hidden", [P, 2, 2 * NCS])
        px = ps("px_c", [P, 2, 512])
        ph = ps("ph_c", [P, 2, 512])
        pk = ps("pk_c", [HD, 512])
        pv = ps("pv_c", [P, 512])
        w_loaded = sem("cmp_w_loaded")
        table_ready = sem("page_table_loaded")
        pair_loaded = [sem(f"pair_loaded{r}") for r in range(RING)]
        turned, hidden_done, gelu_done, block_done, keys_saved, values_saved = map(
            sem, ("rows_turned_s", "hidden_done", "gelu_done", "block_done", "keys_saved", "values_saved"))
        saved = [sem("turned_saved_v"), sem("turned_saved_a")]
        pe_turned, pe_saved, bias_saved = map(sem, ("pe_turned", "pe_saved", "bias_saved"))
        ident, pt, kcT, vc, kcTp, vcp = (g[k] for k in ("ident", "pt", "kcT", "vc", "kcTp", "vcp"))

        with nc.Block() as block:
            @block.sync
            def _(eng):
                for kk, s in enumerate("kv"):
                    eng.dma_start(pe[:, kk, :], io[f"pe_cmp_{s}"][0].rearrange("(m r) d -> m (r d)", r=2)).then_inc(w_loaded, 16)
                    eng.dma_start(w1[:, kk], io[f"w_cmp1_{s}"][0].rearrange("(a j p) n -> p a j n", a=2, p=P)).then_inc(w_loaded, 16)
                    eng.dma_start(w2[:, kk], io[f"w_cmp2_{s}"][0]).then_inc(w_loaded, 16)
                eng.dma_start(pt[:, :], io["page_table"].rearrange("b (o n) -> o (b n)", o=1)).then_inc(table_ready, 16)
                for q in range(4):
                    for a in range(2):
                        rows = io["nsa_p"][(2 * q + a) * P:(2 * q + a + 1) * P, 0:256].rearrange("(p r) e -> p r e", r=2)
                        eng.dma_start(pg[64 * a:64 * a + 64, q], rows).then_inc(pair_loaded[q], 16)
                eng.wait_ge(table_ready, 16)
                with eng.Fori(0, NB) as b:
                    for q in range(PAIRS):
                        slot = (4 + q) % RING
                        if q >= 4:
                            eng.wait_ge(turned, b * PAIRS + q - 3)
                        else:
                            eng.wait_ge(turned, b * PAIRS + 1)
                        for a in range(2):
                            page = eng.value_load(pt[0:1, bass.ds(b * NPAGE + 2 * q + a, 1)], min_val=0, max_val=NPOOL - 1)
                            rows = io["cache_nsa"][bass.ds(page * (PAGE // 2), PAGE // 2), :, 0:256]
                            eng.dma_start(pg[64 * a:64 * a + 64, slot], rows).then_inc(pair_loaded[slot], 16)

            def sequence_loop(eng, body):
                body(0, 1, 4, NCP, None)
                with eng.Fori(0, NB // 2) as i:
                    for u in range(2):
                        body(i * 2 + u + 1, u, PAIRS, NCS, i * 2 + u)

            def pair_number(b, q):
                return q if b is None else b * PAIRS + 4 + q

            @block.tensor
            def _(eng):
                eng.wait_ge(w_loaded, 16 * 6)
                for kk in range(2):
                    mm = eng.transpose(pv[:, kk * 16:kk * 16 + 16], pe[:, kk, :], ident[0:16, 0:16])
                mm.then_inc(pe_turned, 1)
                eng.wait_ge(pe_saved, 1)
                for kk in range(2):
                    for m in range(16):
                        mm = eng.matmul(ph[:, 0, kk:kk + 1], w1[:, kk, m // 8, m % 8, :], peT[:, kk, m:m + 1], start=(m == 0), stop=(m == 15))
                mm.then_inc(hidden_done, 1)
                eng.wait_ge(bias_saved, 1)

                def body(s, u, pairs, blocks, b):
                    for q in range(pairs):
                        slot = q if b is None else (4 + q) % RING
                        k = 0 if b is None else (4 + q) // RING
                        eng.wait_ge(pair_loaded[slot], 32 if b is None else b * 64 + 32 * (k + 1))
                        if not (b is None and q < 2):
                            eng.wait_ge(saved[q % 2], 1 if b is None else b * 8 + 2 + q // 2)
                        for v in range(4):
                            mm = eng.transpose(px[:, q % 2, v * P:(v + 1) * P], pg[:, slot, v % 2, (v // 2) * P:(v // 2 + 1) * P], ident[:, :])
                        mm.then_inc(turned, 1)
                    for kk in range(2):
                        for e in range(2):
                            eng.wait_ge(saved[e], 2 if b is None else b * 8 + 10)
                        if b is not None:
                            eng.wait_ge(gelu_done, b * 2 + kk + 1)
                        out = ph[:, kk, 0:2 * blocks].rearrange("p (v c) -> p v c", v=2)
                        for m in range(16):
                            half, j = m // 8, m % 8
                            src = xt[:, u, 2 * kk:2 * kk + 2, :].rearrange("p v (c j) -> p v c j", j=8)[:, :, half:half + blocks, j]
                            mm = eng.matmul(out, w1[:, kk, half, j, :], src, start=(m == 0), stop=(m == 15))
                        mm.then_inc(hidden_done, 1)
                    gd = 0 if b is None else b * 2 + 2
                    eng.wait_ge(gelu_done, gd + 1)
                    if b is not None:
                        eng.wait_ge(keys_saved, b + 1)
                    eng.matmul(pk[:, 0:2 * blocks], w2[:, 0, :], hid[:, 0, 0:2 * blocks], start=True, stop=True).then_inc(block_done, 1)
                    eng.wait_ge(gelu_done, gd + 2)
                    if b is not None:
                        eng.wait_ge(values_saved, b + 1)
                    for v in range(2):
                        for c in range((blocks + P - 1) // P):
                            r = min(P, blocks - c * P)
                            mm = eng.matmul(pv[0:r, (2 * v + c) * HD:(2 * v + c + 1) * HD], hid[:, 1, v * blocks + c * P:v * blocks + c * P + r], w2[:, 1, :], start=True, stop=True)
                    mm.then_inc(block_done, 1)

                sequence_loop(eng, body)

            def save_turned(eng, e, u, pairs, b):
                for q in range(e, pairs, 2):
                    eng.wait_ge(turned, pair_number(b, q) + 1)
                    if q < 2 and b is not None:
                        eng.wait_ge(hidden_done, b * 2 + 1)
                    for r in range(2):
                        for j in range(2):
                            out = xt[64 * r:64 * r + 64, u, j:4:2, q * P:(q + 1) * P]
                            src = px[64 * j:64 * j + 64, q % 2, :].rearrange("p (k r c) -> p k r c", k=2, r=2)[:, :, r, :]
                            ins = eng.tensor_copy(out, src) if e == 0 else eng.activation(out, src, ACT.Copy)
                    ins.then_inc(saved[e], 1)

            @block.vector
            def _(eng):
                eng.memset(vcp[:, :, HD:HD + 1], 1.0)
                eng.wait_ge(pe_turned, 1)
                eng.tensor_copy(peT[:, :, :], pv[:, 0:32].rearrange("p (k m) -> p k m", k=2)).then_inc(pe_saved, 1)
                eng.wait_ge(hidden_done, 1)
                eng.tensor_copy(peb[:, :], ph[:, 0, 0:2]).then_inc(bias_saved, 1)

                def body(s, u, pairs, blocks, b):
                    save_turned(eng, 0, u, pairs, b)
                    bd = 0 if b is None else b * 2 + 2
                    eng.wait_ge(block_done, bd + 1)
                    keys = pk[:, 0:2 * blocks].rearrange("p (v c) -> p v c", v=2)
                    eng.tensor_copy(kcTp[:, :, :] if b is None else kcT[:, bass.ds(b * 2, 2), :], keys).then_inc(keys_saved, 1)
                    eng.wait_ge(block_done, bd + 2)
                    if b is None:
                        src = pv[0:NCP, 0:256].rearrange("p (v c d) -> p v c d", v=2, c=2)[:, :, 0, :]
                        eng.tensor_copy(vcp[0:NCP, :, 0:HD], src).then_inc(values_saved, 1)
                    else:
                        vals = pv[:, 0:256].rearrange("p (v c d) -> p v c d", v=2, c=2)
                        eng.tensor_copy(vc[:, bass.ds(b * 2, 2), 0, :], vals[:, :, 0, :])
                        eng.tensor_copy(vc[0:P - 1, bass.ds(b * 2, 2), 1, :], vals[0:P - 1, :, 1, :]).then_inc(values_saved, 1)

                sequence_loop(eng, body)

            @block.scalar
            def _(eng):
                eng.wait_ge(bias_saved, 1)

                def body(s, u, pairs, blocks, b):
                    save_turned(eng, 1, u, pairs, b)
                    for kk in range(2):
                        eng.wait_ge(hidden_done, 2 + kk if b is None else b * 2 + 4 + kk)
                        if b is not None:
                            eng.wait_ge(block_done, b * 2 + 1 + kk)
                        eng.activation(hid[:, kk, 0:2 * blocks], ph[:, kk, 0:2 * blocks], ACT.Gelu_apprx_tanh, bias=peb[:, kk:kk + 1]).then_inc(gelu_done, 1)

                sequence_loop(eng, body)


def attend(nc, io, g):
    with ExitStack() as ctx:
        sb = lambda n, s, t=F32: ctx.enter_context(nc.sbuf_tensor(n, s, t))
        ps = lambda n, s, t=F32: ctx.enter_context(nc.psum_tensor(n, s, t))
        sem = lambda n: g["sem"](n)
        kT = sb("kT_sel_win", [HD, 2, KVH, SEQ])
        vx = sb("v_sel_win", [P, 2, TILES, KVH, HD + 1])
        qn = sb("q_nsa", [HD, 2, SEQ])
        qs = sb("q_sb", [HD, 2, SEQ])
        ks = sb("k_sb", [HD, 2, SEQ])
        vs = sb("v_sb", [P, 2, TILES, HD])
        masksf = sb("masks_f", [P, 3, P])
        cmaskf = sb("cmask_f", [P, TILES, 64])
        masks = sb("masks_b", [P, 3, P], BF16)
        cmask = sb("cmask_b", [P, TILES, 64], BF16)
        identb = sb("ident_b", [P, P], BF16)
        rowok = sb("rowok", [P, 1])
        nm = sb("minus_max", [P, 64])
        pr = sb("probs", [P, 2, SEQ])
        prT = sb("probs_turned", [P, 2, TILES, P])
        lg = sb("log_part", [P, SEQ])
        rl = sb("relu_part", [P, SEQ])
        dd = sb("log_weight", [P, SEQ])
        fac = sb("factor", [P, 64, 2])
        S = ps("scores", [P, 2, 1024])
        PT = ps("turned_ps", [P, 2, 512])
        O = ps("out_ps", [P, 2, 512])
        const_loaded, masks_set = sem("const_loaded"), sem("masks_set")
        head_loaded = [sem("head_loaded0"), sem("head_loaded1")]
        qk_done, abs_done, log_done, stat_done, exp_done, turned, pv_done, out_done = map(
            sem, ("qk_done", "abs_done", "log_done", "stat_done", "exp_done", "turned_a", "pv_done", "out_done"))
        saved = [sem("p_saved_v"), sem("p_saved_a")]
        stored, steps = sem("window_stored"), sem("steps_a")
        ident, gates, mix, kcTp, vcp = (g[k] for k in ("ident", "gates", "mix", "kcTp", "vcp"))

        units = []
        for u in range(2):
            for t in range(TILES):
                for kind in ("sb", "cmp", "sel", "win"):
                    lo = max(0, t - 4) if kind == "win" else 0
                    tiles = 1 if kind == "cmp" else t + 1 - lo
                    units.append((u, t, kind, lo, tiles))
        U = len(units)
        G0 = [0]
        for x in units:
            G0.append(G0[-1] + (x[4] + 3) // 4)
        assert G0[-1] % 2 == 0
        SBU = 2 * TILES
        width = lambda n: NCP if units[n][2] == "cmp" else units[n][4] * P
        sbs = [n for n in range(U) if units[n][2] == "sb"]

        with nc.Block() as block:
            @block.sync
            def _(eng):
                Tr = io["T"].rearrange("(h d) t -> d h t", d=HD)
                eng.dma_start(kT[:, 0], Tr[:, T_KS:T_KS + 2, :]).then_inc(const_loaded, 16)
                eng.dma_start(kT[:, 1], Tr[:, T_KW:T_KW + 2, :]).then_inc(const_loaded, 16)
                for j in range(2):
                    eng.dma_start(vx[:, 0, :, j, 0:HD], io["nsa_p"].rearrange("(t p) e -> p t e", p=P)[:, :, 384 + j * HD:448 + j * HD]).then_inc(const_loaded, 16)
                    eng.dma_start(vx[:, 1, :, j, 0:HD], io["win_p"].rearrange("(t p) e -> p t e", p=P)[:, :, 128 + j * HD:192 + j * HD]).then_inc(const_loaded, 16)
                eng.dma_start(masksf[:, :, :], io["c_masks"]).then_inc(const_loaded, 16)
                eng.dma_start(cmaskf[:, :, :], io["c_cmask"]).then_inc(const_loaded, 16)
                eng.dma_start(rowok[:, :], io["c_rowok"]).then_inc(const_loaded, 16)
                for kv in range(KVH):
                    with eng.Fori(0, 2) as i:
                        for u in range(2):
                            h = i * 2 + 4 * kv + u
                            if not kv:
                                pass
                            eng.wait_ge(masks_set, i * 1 + 2 * kv + 1)
                            Th = io["T3"]
                            eng.dma_start(qn[:, u], Th[bass.ds(h + T_QN, 1)].rearrange("o d t -> d (o t)")).then_inc(head_loaded[u], 16)
                            eng.dma_start(qs[:, u], Th[bass.ds(h + T_QS, 1)].rearrange("o d t -> d (o t)")).then_inc(head_loaded[u], 16)
                            eng.dma_start(ks[:, u], Th[bass.ds(h + T_KB, 1)].rearrange("o d t -> d (o t)")).then_inc(head_loaded[u], 16)
                            eng.dma_start(vs[:, u], io["sb_p"].rearrange("(t p) (c h d) -> c p t h d", p=P, c=2, h=NH)[1][:, :, bass.ds(h, 1), :].rearrange("p t o d -> p t (o d)")).then_inc(head_loaded[u], 16)
                eng.dma_start(io["win_p_out"], io["win_p"][SEQ - WINDOW:SEQ, :]).then_inc(stored, 16)
                eng.dma_start(io["win_s_out"][:, 0:WINDOW - 1, :], io["state"][:, 1:WINDOW, :]).then_inc(stored, 16)
                eng.dma_start(io["win_s_out"][:, WINDOW - 1, :], io["win_new"]).then_inc(stored, 16)
                eng.wait_ge(stored, 48)

            def turns(eng, body):
                for kv in range(KVH):
                    with eng.Fori(0, 2) as i:
                        body(kv, i + 2 * kv)

            @block.tensor
            def _(eng):
                eng.wait_ge(const_loaded, 16 * 9)
                eng.wait_ge(masks_set, 1)

                def body(kv, N):
                    def qk(n):
                        u, t, kind, lo, tiles = units[n]
                        if n % (U // 2) == 0:
                            eng.wait_ge(head_loaded[u], (N + 1) * 64)
                        if n >= 2:
                            eng.wait_ge(exp_done, N * U + n - 1)
                        q = (qs if kind == "sb" else qn)[:, u, t * P:(t + 1) * P]
                        if kind == "cmp":
                            eng.matmul(S[:, n % 2, 0:NCP], q, kcTp[:, kv, :], start=True, stop=False)
                            mm = eng.matmul(S[:, n % 2, 0:NCP], identb[:, :], cmask[:, t, 0:NCP], start=False, stop=True)
                        else:
                            k = {"sb": ks[:, u], "sel": kT[:, 0, kv], "win": kT[:, 1, kv]}[kind][:, lo * P:(t + 1) * P]
                            w = tiles * P
                            edges = [((tiles - 1) * P, 1 if kind == "sb" else 0)]
                            if kind == "win" and t >= 4:
                                edges.append((0, 2))
                            for a in range(0, w, 512):
                                e = min(w, a + 512)
                                own = [x for x in edges if a <= x[0] < e]
                                mm = eng.matmul(S[:, n % 2, a:e], q, k[:, a:e], start=True, stop=not own)
                                for z, (at, m) in enumerate(own):
                                    mm = eng.matmul(S[:, n % 2, at:at + P], identb[:, :], masks[:, m, :], start=False, stop=z == len(own) - 1)
                        mm.then_inc(qk_done, 1)

                    def transposes(n):
                        tiles = units[n][4]
                        eng.wait_ge(exp_done, N * U + n + 1)
                        for b in range(G0[n], G0[n + 1]):
                            if b >= 2:
                                eng.wait_ge(saved[b % 2], N * (G0[-1] // 2) + b // 2)
                            if units[n][2] == "cmp":
                                eng.sem_inc(steps, 1)
                            for c in range(4 * (b - G0[n]), min(tiles, 4 * (b - G0[n]) + 4)):
                                w = min(P, width(n) - c * P)
                                mm = eng.transpose(PT[0:w, b % 2, (c % 4) * P:(c % 4 + 1) * P], pr[:, n % 2, c * P:c * P + w], ident[:, :])
                            mm.then_inc(turned, 1)

                    def pv(n):
                        u, t, kind, lo, tiles = units[n]
                        for b in range(G0[n], G0[n + 1]):
                            eng.wait_ge(saved[b % 2], N * (G0[-1] // 2) + b // 2 + 1)
                        if n >= 2:
                            eng.wait_ge(out_done, N * U + n - 1)
                        for c in range(tiles):
                            if kind == "cmp":
                                l, r = prT[0:NCP, n % 2, 0, :], vcp[0:NCP, kv, :]
                            elif kind == "sb":
                                l, r = prT[:, n % 2, c, :], vs[:, u, c, :]
                            else:
                                l, r = prT[:, n % 2, c, :], vx[:, 0 if kind == "sel" else 1, lo + c, kv, :]
                            mm = eng.matmul(O[:, n % 2, 0:HD if kind == "sb" else HD + 1], l, r, start=c == 0, stop=c == tiles - 1)
                        mm.then_inc(pv_done, 1)

                    qk(0)
                    for n in range(U + 1):
                        if n + 1 < U:
                            qk(n + 1)
                        if n < U:
                            transposes(n)
                        if n >= 1:
                            pv(n - 1)
                    eng.wait_ge(out_done, (N + 1) * U)
                turns(eng, body)

            def save_groups(eng, N, n, e):
                tiles = units[n][4]
                for b in range(G0[n], G0[n + 1]):
                    if b % 2 != e:
                        continue
                    eng.wait_ge(turned, N * G0[-1] + b + 1)
                    if n >= 2:
                        eng.wait_ge(pv_done, N * U + n - 1)
                    c = 4 * (b - G0[n])
                    m, w = min(4, tiles - c), min(P, width(n))
                    out = prT[0:w, n % 2, c:c + m, :]
                    src = PT[0:w, b % 2, 0:m * P].rearrange("p (c q) -> p c q", q=P)
                    if e == 0:
                        eng.tensor_copy(out, src).then_inc(saved[0], 1)
                    else:
                        eng.activation(out, src, ACT.Copy).then_inc(saved[1], 1)

            @block.scalar
            def _(eng):
                def body(kv, N):
                    def prepare(n):
                        w = width(n)
                        eng.wait_ge(qk_done, N * U + n + 1)
                        eng.activation(lg[:, 0:w], S[:, n % 2, 0:w], ACT.Abs).then_inc(abs_done, 1)
                        eng.drain()
                        eng.activation(lg[:, 0:w], lg[:, 0:w], ACT.Exp, scale=-1.0)
                        eng.drain()
                        eng.activation(lg[:, 0:w], lg[:, 0:w], ACT.Ln, bias=1.0).then_inc(log_done, 1)

                    def exps(n):
                        w, kind = width(n), units[n][2]
                        if kind == "sb":
                            prepare(n)
                        eng.wait_ge(stat_done, N * U + n + 1)
                        if n >= 2:
                            eng.wait_ge(turned, N * G0[-1] + G0[n - 1])
                        if kind == "sb":
                            eng.activation(pr[:, n % 2, 0:w], dd[:, 0:w], ACT.Exp).then_inc(exp_done, 1)
                        else:
                            eng.activation(pr[:, n % 2, 0:w], S[:, n % 2, 0:w], ACT.Exp, bias=nm[:, n:n + 1]).then_inc(exp_done, 1)

                    exps(0)
                    for n in range(U):
                        if n + 1 < U:
                            exps(n + 1)
                        save_groups(eng, N, n, 1)
                    eng.wait_ge(pv_done, (N + 1) * U)
                turns(eng, body)

            @block.vector
            def _(eng):
                eng.wait_ge(const_loaded, 16 * 9)
                eng.memset(vx[:, :, :, :, HD:HD + 1], 1.0)
                eng.tensor_copy(identb[:, :], ident[:, :])
                eng.tensor_copy(masks[:, :, :], masksf[:, :, :])
                eng.tensor_copy(cmask[:, :, :], cmaskf[:, :, :]).then_inc(masks_set, 1)

                def body(kv, N):
                    def stat(n):
                        w, kind = width(n), units[n][2]
                        eng.wait_ge(qk_done, N * U + n + 1)
                        z = S[:, n % 2, 0:w]
                        if kind != "sb":
                            eng.tensor_reduce(nm[:, n:n + 1], z, AX.X, ALU.max, negate=True).then_inc(stat_done, 1)
                            return
                        k = sbs.index(n)
                        eng.wait_ge(abs_done, N * SBU + k + 1)
                        eng.tensor_scalar(rl[:, 0:w], z, 0.0, None, ALU.max)
                        eng.drain()
                        if k >= 1:
                            eng.wait_ge(exp_done, N * U + sbs[k - 1] + 1)
                        eng.wait_ge(log_done, N * SBU + k + 1)
                        rev = (lambda a: a[:, w - 1::-1] if w == SEQ else a[:, w - 1::-1])
                        eng.tensor_tensor_scan(rev(dd), rev(lg), rev(rl), 0.0, ALU.add, ALU.add)
                        eng.drain()
                        eng.tensor_tensor(dd[:, 0:w], z, dd[:, 0:w], ALU.subtract).then_inc(stat_done, 1)

                    def out(n):
                        u, t, kind, lo, tiles = units[n]
                        o = O[:, n % 2, 0:HD]
                        h = N * 2 + u
                        eng.wait_ge(pv_done, N * U + n + 1)
                        if kind == "sb":
                            eng.tensor_copy(mix[:, t, bass.ds(h * HD + 512, HD)], o).then_inc(out_done, 1)
                            return
                        br = ("cmp", "sel", "win").index(kind)
                        f, f2 = fac[:, n, 0:1], fac[:, n, 1:2]
                        eng.reciprocal(f, O[:, n % 2, HD:HD + 1])
                        eng.drain()
                        eng.tensor_tensor(f2, f, gates[:, t, bass.ds(h * 3 + br, 1)], ALU.mult)
                        eng.drain()
                        if kind == "cmp" and t == 0:
                            eng.tensor_tensor(f2, f2, rowok[:, :], ALU.mult)
                            eng.drain()
                        m = mix[:, t, bass.ds(h * HD, HD)]
                        if kind == "cmp":
                            eng.tensor_scalar(m, o, f2, None, ALU.mult).then_inc(out_done, 1)
                        else:
                            eng.scalar_tensor_tensor(m, o, f2, m, ALU.mult, ALU.add).then_inc(out_done, 1)

                    stat(0)
                    for n in range(U + 1):
                        if n + 1 < U:
                            stat(n + 1)
                        if n < U:
                            save_groups(eng, N, n, 0)
                        if n >= 1:
                            out(n - 1)
                    eng.memset(fac[:, 0, 0:1], 0.0).then_inc(masks_set, 1)
                turns(eng, body)


def decode_sb(nc, io, g):
    with ExitStack() as ctx:
        sb = lambda n, s, t=F32: ctx.enter_context(nc.sbuf_tensor(n, s, t))
        ps = lambda n, s, t=F32: ctx.enter_context(nc.psum_tensor(n, s, t))
        sem = lambda n: g["sem"](n)
        RING = 8
        kr = sb("k_ring", [P, RING, 512])
        vr = sb("v_ring", [P, RING, 512])
        qb = sb("q_rows", [P, 2, 512])
        pr = sb("products", [P, 4, 512])
        z = sb("z_dec", [P, NH, NPAGE])
        lg = sb("log_dec", [P, NH * NPAGE])
        rl = sb("relu_dec", [P, NH * NPAGE])
        later = sb("later_pages", [P, NH * NPAGE])
        keep = sb("keep", [P, NH, NPAGE])
        dd = sb("logw_dec", [P, NH * NPAGE])
        aw = sb("weights_dec", [P, NH, NPAGE])
        tri = sb("tri", [P, P])
        ones = sb("ones_dec", [P, P])
        diag = sb("diag", [NH, 512])
        om = sb("o_masked", [NH, 512])
        orow = sb("o_row", [1, 512])
        cum = ps("cum_dec", [P, 512])
        ov = ps("o_dec", [NH, 512])
        os_ = ps("o_row_ps", [1, 512])
        k_loaded = [sem(f"k_loaded{r}") for r in range(RING)]
        v_loaded = [sem(f"v_loaded{r}") for r in range(RING)]
        q_loaded = [sem("q_loaded0"), sem("q_loaded1")]
        multiplied = [sem("k_times_q_v"), sem("k_times_q_p")]
        names = ("c_loaded_d", "reduced", "z_absed", "z_logged", "softplus_done", "cum_done", "logw_done", "weights_done",
                 "v_used", "o_masked_s", "o_row_done", "o_row_saved", "c_set")
        c_loaded, reduced, absed, logged, sp_done, cum_done, logw_done, weights_done, v_used, masked, row_done, row_saved, c_set = map(sem, names)
        stored = [sem("o_row_stored0"), sem("o_row_stored1")]
        pt = g["pt"]
        page_steps = sem("page_steps")

        def steps(eng, body):
            body(0, 0, True, False)
            body(1, 1, True, True)
            with eng.Fori(0, (NB - 2) // 2) as i:
                body(i * 2 + 2, 0, True, True)
                body(i * 2 + 3, 1, True, True)
            body(NB, 0, False, True)

        def first_turns(b, n):
            return isinstance(b, int) and b < n

        with nc.Block() as block:
            @block.sync
            def _(eng):
                eng.dma_start(tri[:, :], io["c_tri"]).then_inc(c_loaded, 16)
                eng.dma_start(diag[:, :], io["c_diag"].rearrange("a h d -> a (h d)")).then_inc(c_loaded, 16)

                def body(b, u, keys, values):
                    if keys:
                        if not first_turns(b, 2):
                            eng.wait_ge(reduced, b * NPAGE - NPAGE)
                        eng.dma_start(qb[:, u], io["sbq_s"][bass.ds(b, 1), :].rearrange("o n -> (o n)").partition_broadcast(P)).then_inc(q_loaded[u], 16)
                    for p in range(NPAGE):
                        r = p % RING
                        if keys:
                            if not (first_turns(b, 1) and p < RING):
                                eng.wait_ge(multiplied[p % 2], b * (NPAGE // 2) + (p - RING) // 2 + 1)
                            page = eng.value_load(pt[0:1, bass.ds(b * NPAGE + p, 1)], min_val=0, max_val=NPOOL - 1)
                            eng.dma_start(kr[:, r], io["cache_sb"][bass.ds(page * P, P), 0, :]).then_inc(k_loaded[r], 16)
                        if values:
                            if not (first_turns(b, 2) and p < RING):
                                eng.wait_ge(v_used, (b - 1) * NPAGE + p - RING + 1)
                            page = eng.value_load(pt[0:1, bass.ds((b - 1) * NPAGE + p, 1)], min_val=0, max_val=NPOOL - 1)
                            eng.dma_start(vr[:, r], io["cache_sb"][bass.ds(page * P, P), 1, :]).then_inc(v_loaded[r], 16)
                    if values:
                        eng.wait_ge(row_saved, b)
                        eng.dma_start(io["osb_s"][bass.ds(b - 1, 1), :], orow[:, :]).then_inc(stored[u], 16)
                steps(eng, body)
                eng.wait_ge(stored[0], 16 * NB // 2)
                eng.wait_ge(stored[1], 16 * NB // 2)

            def page_ready(eng, b, u, p):
                if p == 0:
                    eng.wait_ge(q_loaded[u], (b - u) * 8 + 16)
                eng.wait_ge(k_loaded[p % RING], b * 64 + 16 * (p // RING) + 16)

            @block.gpsimd
            def _(eng):
                def body(b, u, keys, values):
                    if not keys:
                        return
                    for p in range(1, NPAGE, 2):
                        if p == 1:
                            eng.wait_ge(q_loaded[u], (b - u) * 8 + 16)
                        page_ready(eng, b, u, p)
                        if not (first_turns(b, 1) and p < 4):
                            eng.wait_ge(reduced, b * NPAGE + p - 3)
                        eng.tensor_tensor(pr[:, 2 + p // 2 % 2], kr[:, p % RING], qb[:, u], ALU.mult).then_inc(multiplied[1], 1)
                steps(eng, body)

            @block.vector
            def _(eng):
                eng.memset(ones[:, :], 1.0)
                eng.memset(keep[:, :, 1:NPAGE], 1.0)
                eng.memset(keep[:, :, 0:1], 0.0).then_inc(c_set, 1)
                eng.wait_ge(c_loaded, 32)
                zf = z[:, :, :].rearrange("p h n -> p (h n)")

                def body(b, u, keys, values):
                    if keys:
                        for p in range(NPAGE):
                            if p % 2 == 0:
                                page_ready(eng, b, u, p)
                                buf = pr[:, p // 2 % 2]
                                eng.tensor_tensor(buf, kr[:, p % RING], qb[:, u], ALU.mult).then_inc(multiplied[0], 1)
                                eng.drain()
                            else:
                                buf = pr[:, 2 + p // 2 % 2]
                                eng.wait_ge(multiplied[1], b * (NPAGE // 2) + p // 2 + 1)
                            eng.tensor_reduce(z[:, :, NPAGE - 1 - p], buf.rearrange("p (h d) -> p h d", h=NH), AX.X, ALU.add).then_inc(reduced, 1)
                    if values:
                        eng.wait_ge(v_used, b * NPAGE)
                        if not first_turns(b, 2):
                            eng.wait_ge(row_done, b - 1)
                        eng.tensor_tensor(om[:, :], ov[:, :], diag[:, :], ALU.mult).then_inc(masked, 1)
                    if keys:
                        eng.drain()
                        if not first_turns(b, 1):
                            eng.wait_ge(cum_done, b)
                        eng.tensor_scalar(rl[:, :], zf, 0.0, None, ALU.max)
                        eng.drain()
                        eng.wait_ge(logged, b + 1)
                        eng.tensor_tensor(rl[:, :], rl[:, :], lg[:, :], ALU.add)
                        eng.drain()
                        eng.tensor_tensor_scan(later[:, :], keep[:, :, :].rearrange("p h n -> p (h n)"), rl[:, :], 0.0, ALU.mult, ALU.add)
                        eng.drain()
                        eng.tensor_tensor(later[:, :], later[:, :], rl[:, :], ALU.subtract).then_inc(sp_done, 1)
                        if not first_turns(b, 1):
                            eng.wait_ge(weights_done, b)
                        eng.wait_ge(cum_done, b + 1)
                        eng.tensor_tensor(dd[:, :], zf, cum[:, 0:NH * NPAGE], ALU.subtract).then_inc(logw_done, 1)
                steps(eng, body)

            @block.scalar
            def _(eng):
                def body(b, u, keys, values):
                    if keys:
                        eng.wait_ge(reduced, b * NPAGE + NPAGE)
                        eng.activation(lg[:, :], z[:, :, :].rearrange("p h n -> p (h n)"), ACT.Abs)
                        eng.drain()
                        eng.activation(lg[:, :], lg[:, :], ACT.Exp, scale=-1.0)
                        eng.drain()
                        eng.activation(lg[:, :], lg[:, :], ACT.Ln, bias=1.0).then_inc(logged, 1)
                    if values:
                        eng.wait_ge(row_done, b)
                        if not first_turns(b, 2):
                            eng.wait_ge(stored[1 - u], b * 8 if u == 0 else b * 8 - 8)
                        eng.activation(orow[:, :], os_[:, :], ACT.Copy).then_inc(row_saved, 1)
                    if keys:
                        eng.wait_ge(logw_done, b + 1)
                        if not first_turns(b, 1):
                            eng.wait_ge(v_used, b * NPAGE)
                        eng.activation(aw[:, :, :].rearrange("p h n -> p (h n)"), dd[:, :], ACT.Exp).then_inc(weights_done, 1)
                steps(eng, body)

            @block.tensor
            def _(eng):
                eng.wait_ge(c_loaded, 32)
                eng.wait_ge(c_set, 1)

                def body(b, u, keys, values):
                    if values:
                        eng.wait_ge(weights_done, b)
                        if not first_turns(b, 2):
                            eng.wait_ge(masked, b - 1)
                        for p in range(NPAGE):
                            eng.wait_ge(v_loaded[p % RING], b * 64 - 64 + 16 * (p // RING) + 16)
                            eng.matmul(ov[:, :], aw[:, :, NPAGE - 1 - p], vr[:, p % RING], start=p == 0, stop=p == NPAGE - 1).then_inc(v_used, 1)
                        eng.wait_ge(masked, b)
                        if not first_turns(b, 2):
                            eng.wait_ge(row_saved, b - 1)
                        eng.sem_inc(page_steps, 1)
                        eng.matmul(os_[:, :], ones[0:NH, 0:1], om[:, :], start=True, stop=True).then_inc(row_done, 1)
                    if keys:
                        eng.wait_ge(sp_done, b + 1)
                        if not first_turns(b, 1):
                            eng.wait_ge(logw_done, b)
                        eng.matmul(cum[:, 0:NH * NPAGE], tri[:, :], rl[:, :], start=True, stop=False)
                        eng.matmul(cum[:, 0:NH * NPAGE], ones[:, :], later[:, :], start=False, stop=True).then_inc(cum_done, 1)
                steps(eng, body)


def decode_nsa(nc, io, g):
    with ExitStack() as ctx:
        sb = lambda n, s, t=F32: ctx.enter_context(nc.sbuf_tensor(n, s, t))
        sem = lambda n: g["sem"](n)
        X = NB * KVH
        ident, pt, kcT, vc = (g[k] for k in ("ident", "pt", "kcT", "vc"))
        qT = sb("q_dec", [HD, NH, NB])
        oC = sb("o_cmp_dec", [GRP, X, HD])
        oS = sb("o_sel_dec", [GRP, X, HD])
        oW = sb("o_win_dec", [GRP, X, HD])
        block_id = sb("block_id", [1, X * 16], I32)
        with ExitStack() as c2:
            sb2 = lambda n, s, t=F32: c2.enter_context(nc.sbuf_tensor(n, s, t))
            ps2 = lambda n, s: c2.enter_context(nc.psum_tensor(n, s, F32))
            sc = sb2("sc_dec", [GRP, X, NCS])
            st = sb2("st_dec", [GRP, 4, X])
            pT = sb2("p_turned", [P, X * 2, GRP])
            pS = sb2("p_summed", [P, X * 2])
            pB = sb2("p_bcast", [P, X * 2, NBLK])
            ovl = sb2("overlap", [P, 2, NBLK])
            selc = sb2("sel_consts", [NBLK, 3, NBLK])
            ranks = sb2("ranks", [NBLK, 16])
            blk = sb2("blk", [NBLK, 2])
            pageof = sb2("pageof", [NPAGE, NBLK])
            pti = sb2("pt_int", [NPAGE, NB], I32)
            ptf = sb2("pt_float", [NPAGE, NB])
            ones = sb2("ones_sel", [NBLK, 2])
            R = sb2("score_rows", [NBLK, X, NBLK])
            Q1 = sb2("sel_tmp1", [NBLK, X, NBLK])
            Q2 = sb2("sel_tmp2", [NBLK, X, NBLK])
            col = sb2("score_col", [NBLK, X])
            rank = sb2("rank", [NBLK, X])
            base = sb2("block_addr", [NBLK, NB])
            OH = sb2("one_hot", [NBLK, X, 16])
            S4 = ps2("S4", [GRP, 4, 512])
            PA = ps2("PA", [P, 512])
            PB = ps2("PB", [P, 512])
            PR = ps2("PR", [NBLK, 2, 512])
            c_loaded, scored, copied, shifted, exped, probs, turned, turned_saved, summed, rows_done, bases_done, oh_done, ids_done, pt_set = map(
                lambda n: g["sem"](n),
                ("cd_loaded", "scored", "copied", "shifted", "exped", "probs", "p_turned_s", "p_turned_saved", "p_summed_s",
                 "rows_done", "bases_done", "oh_done", "ids_done", "pt_set"))
            with nc.Block() as block:
                @block.sync
                def _(eng):
                    for dst, src in ((qT[:, :, :], io["Ts"].rearrange("(h d) b -> d h b", d=HD)[:, 0:NH, :]), (ovl[:, :, :], io["c_ov"]),
                                     (selc[:, :, :], io["c_sel"]), (ranks[:, :], io["c_ranks"]), (blk[:, :], io["c_blk"]),
                                     (pageof[:, :], io["c_pageof"]), (pti[:, :], io["page_table"].rearrange("b n -> n b"))):
                        eng.dma_start(dst, src, allow_slow_non_contiguous=True).then_inc(c_loaded, 16)

                @block.tensor
                def _(eng):
                    eng.wait_ge(c_loaded, 16 * 7)
                    for x in range(X):
                        b, j = x // 2, x % 2
                        if x == 8:
                            eng.wait_ge(copied, 1)
                        mm = eng.matmul(S4[:, x // 2 % 4, j * NCS:(j + 1) * NCS], qT[:, GRP * j:GRP * j + GRP, b], kcT[:, x, :], start=True, stop=True)
                        if x % 8 == 7:
                            mm.then_inc(scored, 1)
                    eng.wait_ge(pt_set, 1)
                    eng.matmul(PB[0:NBLK, 0:NB], pageof[:, :], ptf[:, :], start=True, stop=True).then_inc(bases_done, 1)
                    eng.wait_ge(probs, 1)
                    for x in range(X):
                        for c in range(2):
                            w = P - c
                            mm = eng.transpose(PA[0:w, (2 * x + c) * GRP:(2 * x + c + 1) * GRP], sc[:, x, c * P:c * P + w], ident[0:GRP, 0:GRP])
                    mm.then_inc(turned, 1)
                    eng.wait_ge(turned_saved, 1)
                    for x in range(X):
                        for c in range(2):
                            w = P - c
                            mm = eng.matmul(S4[:, x // 8, x % 8 * HD:(x % 8 + 1) * HD], pT[0:w, 2 * x + c, :], vc[0:w, x, c, :], start=c == 0, stop=c == 1)
                    mm.then_inc(scored, 1)
                    eng.wait_ge(summed, 1)
                    for x in range(X):
                        for c in range(2):
                            w = P - c
                            mm = eng.matmul(PR[:, x // 8, x % 8 * HD:(x % 8 + 1) * HD], pB[0:w, 2 * x + c, :], ovl[0:w, c, :], start=c == 0, stop=c == 1)
                    mm.then_inc(rows_done, 1)
                    eng.wait_ge(oh_done, 1)
                    eng.matmul(PB[0:1, 0:X * 16], ones[:, 0:1], OH[:, :, :].rearrange("p x r -> p (x r)"), start=True, stop=True).then_inc(ids_done, 1)

                @block.scalar
                def _(eng):
                    eng.wait_ge(shifted, 1)
                    scf = sc[:, :, :].rearrange("p x c -> p (x c)")
                    eng.activation(scf, scf, ACT.Exp).then_inc(exped, 1)

                @block.vector
                def _(eng):
                    eng.memset(ones[:, :], 1.0)
                    eng.memset(pT[96:P, :, :], 0.0)
                    eng.wait_ge(c_loaded, 16 * 7)
                    eng.tensor_copy(ptf[:, :], pti[:, :]).then_inc(pt_set, 1)
                    for h in range(2):
                        eng.wait_ge(scored, h + 1)
                        eng.tensor_copy(sc[:, 8 * h:8 * h + 8, :].rearrange("p (a j) c -> p a (j c)", j=2), S4[:, :, 0:2 * NCS]).then_inc(copied, 1)
                    eng.drain()
                    bc = lambda a: a.unsqueeze(2).broadcast_to([GRP, X, NCS])
                    eng.tensor_reduce(st[:, 0, :], sc[:, :, :], AX.X, ALU.max)
                    eng.drain()
                    eng.tensor_tensor(sc[:, :, :], sc[:, :, :], bc(st[:, 0, :]), ALU.subtract).then_inc(shifted, 1)
                    eng.wait_ge(exped, 1)
                    eng.tensor_reduce(st[:, 1, :], sc[:, :, :], AX.X, ALU.add)
                    eng.drain()
                    eng.reciprocal(st[:, 2, :], st[:, 1, :])
                    eng.drain()
                    eng.tensor_tensor(sc[:, :, :], sc[:, :, :], bc(st[:, 2, :]), ALU.mult).then_inc(probs, 1)
                    eng.wait_ge(turned, 1)
                    pa = PA[:, 0:2 * X * GRP].rearrange("p (x c h) -> p x c h", c=2, h=GRP)
                    pt4 = pT[:, :, :].rearrange("p (x c) h -> p x c h", c=2)
                    eng.tensor_copy(pt4[:, :, 0, :], pa[:, :, 0, :])
                    eng.tensor_copy(pt4[0:P - 1, :, 1, :], pa[0:P - 1, :, 1, :]).then_inc(turned_saved, 1)
                    eng.drain()
                    eng.tensor_reduce(pS[:, :], pT[:, :, :], AX.X, ALU.add)
                    eng.drain()
                    eng.tensor_copy(pB[:, :, :], pS[:, :].unsqueeze(2).broadcast_to([P, 2 * X, NBLK])).then_inc(summed, 1)
                    eng.wait_ge(scored, 3)
                    eng.tensor_copy(oC[:, :, :].rearrange("p (a x) d -> p a (x d)", a=2), S4[:, 0:2, :])
                    eng.wait_ge(bases_done, 1)
                    eng.tensor_scalar(base[:, :], PB[0:NBLK, 0:NB], 2.0, None, ALU.mult)
                    eng.drain()
                    eng.tensor_scalar(base[:, :], base[:, :], blk[:, 1:2], None, ALU.add)
                    eng.wait_ge(rows_done, 1)
                    over = lambda a, n=NBLK: a.unsqueeze(1).broadcast_to([NBLK, X, n])
                    each = lambda a, n=NBLK: a.unsqueeze(2).broadcast_to([NBLK, X, n])
                    eng.tensor_tensor(R[:, :, :], PR[:, :, :].rearrange("p a (x j) -> p (a x) j", j=NBLK), over(selc[:, 2, :]), ALU.add)
                    eng.drain()
                    eng.tensor_tensor(Q1[:, :, :], R[:, :, :], over(selc[:, 0, :]), ALU.mult)
                    eng.drain()
                    eng.tensor_reduce(col[:, :], Q1[:, :, :], AX.X, ALU.add)
                    eng.drain()
                    eng.tensor_tensor(Q1[:, :, :], R[:, :, :], each(col[:, :]), ALU.is_gt)
                    eng.tensor_tensor(Q2[:, :, :], R[:, :, :], each(col[:, :]), ALU.is_equal)
                    eng.drain()
                    eng.tensor_tensor(Q2[:, :, :], Q2[:, :, :], over(selc[:, 1, :]), ALU.mult)
                    eng.drain()
                    eng.tensor_tensor(Q1[:, :, :], Q1[:, :, :], Q2[:, :, :], ALU.add)
                    eng.drain()
                    eng.tensor_reduce(rank[:, :], Q1[:, :, :], AX.X, ALU.add)
                    eng.drain()
                    eng.tensor_tensor(OH[:, :, :], each(rank[:, :], 16), over(ranks[:, :], 16), ALU.is_equal)
                    eng.drain()
                    b4 = base[:, :].unsqueeze(2).broadcast_to([NBLK, NB, 32])
                    o4 = OH[:, :, :].rearrange("p (b j) r -> p b (j r)", j=2)
                    eng.tensor_tensor(o4, o4, b4, ALU.mult).then_inc(oh_done, 1)
                    eng.wait_ge(ids_done, 1)
                    eng.tensor_copy(block_id[:, :], PB[0:1, 0:X * 16])

        ps = lambda n, s: ctx.enter_context(nc.psum_tensor(n, s, F32))
        kv = sb("kv_sel", [P, 2, 8, 2, HD])
        wk = sb("kv_win", [P, 2, 5, 256])
        qst = sb("q_now", [HD, 2, GRP])
        ksb = sb("keys_turned", [HD, 2, 1536])
        pd = sb("probs_dec", [GRP, 1536])
        nmx = sb("nmx_dec", [GRP, 2])
        sums = sb("sums_dec", [GRP, 4])
        pTs = sb("probs_dec_turned", [P, 13, GRP])
        KT = ps("KT", [HD, 2, 512])
        SD = ps("SD", [GRP, 4, 512])
        PT = ps("PTd", [P, 512])
        OD = ps("OD", [GRP, 512])
        kv_loaded = [sem("kv_loaded0"), sem("kv_loaded1")]
        wk_loaded = sem("wk_loaded")
        names = ("q_staged", "k_turned", "k_saved", "scores_done", "max_done", "exps_done", "pd_turned", "pd_saved", "od_done", "od_saved")
        q_staged, k_turned, k_saved, scores_done, max_done, exps_done, pd_turned, pd_saved, od_done, od_saved = map(sem, names)
        o_stored, steps = sem("o_stored"), sem("steps_d")
        NS, NW = NSEL * 64 + 1, WINDOW + 1
        KEYT = [(c, 64 * c * 2, P) for c in range(7)] + [(7, 896, 65)]

        def turns(eng, body):
            for j in range(2):
                body(0, j)
            with eng.Fori(1, NB) as b:
                for j in range(2):
                    body(b, j)

        with nc.Block() as block:
            @block.sync
            def _(eng):
                def body(b, j):
                    first = isinstance(b, int)
                    x = b * 2 + j
                    if not first:
                        eng.wait_ge(od_done, x - 1)
                    for r in range(NSEL):
                        bid = eng.value_load(block_id[0:1, bass.ds(x * 16 + r, 1)], min_val=0, max_val=2 * NPOOL - 1)
                        src = io["cache_blocks"][bass.ds(bid, 1)].rearrange("o s u d -> (o s) u d")[:, 4 + j:8:2, :]
                        eng.dma_start(kv[64 * (r % 2):64 * (r % 2) + 64, j, r // 2], src).then_inc(kv_loaded[j], 16)
                    new = io["nsa_s"][bass.ds(b, 1), :].rearrange("o (u d) -> o u d", d=HD)[:, 4 + j:8:2, :]
                    eng.dma_start(kv[64:65, j, 7], new).then_inc(kv_loaded[j], 16)
                    eng.dma_start(wk[:, j, 0:4, :], io["state"][bass.ds(b, 1)].rearrange("o (t p) e -> p (o t) e", p=P)).then_inc(kv_loaded[j], 16)
                    eng.dma_start(wk[0:1, j, 4, :], io["win_new"][bass.ds(b, 1), :]).then_inc(kv_loaded[j], 16)
                turns(eng, body)
                eng.wait_ge(od_saved, 2 * X)
                for br, o in enumerate((oC, oS, oW)):
                    dst = io["o_s"][br].rearrange("b (j h d) -> h (b j) d", j=2, h=GRP)
                    eng.dma_start(dst, o[:, :, :]).then_inc(o_stored, 16)
                eng.wait_ge(o_stored, 48)

            @block.tensor
            def _(eng):
                def steady(eng):
                    eng.sem_inc(steps, 1)

                def body(b, j):
                    first = isinstance(b, int)
                    x = b * 2 + j
                    eng.wait_ge(kv_loaded[j], b * 16 * 18 + 16 * 18)
                    for go in range(4):
                        k = x * 4 + go
                        if first and j == 0 and go < 2:
                            pass
                        else:
                            eng.wait_ge(k_saved, k - 1)
                        steady(eng)
                        if go < 2:
                            for c in range(4 * go, 4 * go + 4):
                                w = P if c < 7 else 65
                                mm = eng.transpose(KT[:, go % 2, c % 4 * P:c % 4 * P + w], kv[0:w, j, c, 0, :], ident[0:w, 0:w])
                        elif go == 2:
                            for c in range(4):
                                mm = eng.transpose(KT[:, 0, c * P:(c + 1) * P], wk[:, j, c, j * HD:(j + 1) * HD], ident[:, :])
                        else:
                            mm = eng.transpose(KT[:, 1, 0:1], wk[0:1, j, 4, j * HD:(j + 1) * HD], ident[0:1, 0:1])
                        mm.then_inc(k_turned, 1)
                    eng.wait_ge(k_saved, x * 4 + 4)
                    eng.wait_ge(q_staged, x + 1)
                    if not (first and j == 0):
                        eng.wait_ge(exps_done, x * 2)
                    steady(eng)
                    for a, e in ((0, 512), (512, NS), (1024, 1536)):
                        eng.matmul(SD[:, a // 512, 0:e - a], qst[:, j], ksb[:, j, a:e], start=True, stop=True)
                    eng.matmul(SD[:, 3, 0:1], qst[:, j], ksb[:, j, 1000:1001], start=True, stop=True).then_inc(scores_done, 1)
                    eng.wait_ge(exps_done, x * 2 + 2)
                    if not (first and j == 0):
                        eng.wait_ge(pd_saved, x)
                    steady(eng)
                    for c in range(13):
                        a, w = (c * P, P if c < 7 else 65) if c < 8 else (1000 + (c - 8) * P, P if c < 12 else 1)
                        mm = eng.transpose(PT[0:w, c * GRP:(c + 1) * GRP], pd[:, a:a + w], ident[0:GRP, 0:GRP])
                    mm.then_inc(pd_turned, 1)
                    eng.wait_ge(pd_saved, x + 1)
                    if not (first and j == 0):
                        eng.wait_ge(od_saved, x * 2)
                    steady(eng)
                    for c in range(8):
                        w = P if c < 7 else 65
                        eng.matmul(OD[:, 0:HD], pTs[0:w, c, :], kv[0:w, j, c, 1, :], start=c == 0, stop=c == 7)
                    for c in range(5):
                        w = P if c < 4 else 1
                        mm = eng.matmul(OD[:, HD:2 * HD], pTs[0:w, 8 + c, :], wk[0:w, j, c, (2 + j) * HD:(3 + j) * HD], start=c == 0, stop=c == 4)
                    mm.then_inc(od_done, 1)
                turns(eng, body)

            @block.vector
            def _(eng):
                eng.memset(pTs[:, :, :], 0.0)

                def body(b, j):
                    first = isinstance(b, int)
                    x = b * 2 + j
                    if not first:
                        eng.wait_ge(scores_done, x - 1)
                    eng.tensor_copy(qst[:, j], qT[:, GRP * j:GRP * j + GRP, bass.ds(b, 1)].rearrange("p h o -> p (h o)")).then_inc(q_staged, 1)
                    for go, (a, e) in enumerate(((0, 512), (512, NS), (1024, 1536), (1000, 1001))):
                        eng.wait_ge(k_turned, x * 4 + go + 1)
                        eng.tensor_copy(ksb[:, j, a:e], KT[:, go % 2, 0:e - a]).then_inc(k_saved, 1)
                    eng.wait_ge(scores_done, x + 1)
                    if not (first and j == 0):
                        eng.wait_ge(exps_done, x * 2)
                    eng.tensor_reduce(nmx[:, 0:1], SD[:, 0:2, :].rearrange("p a c -> p (a c)")[:, 0:NS], AX.X, ALU.max, negate=True)
                    eng.tensor_reduce(nmx[:, 1:2], SD[:, 2:4, :].rearrange("p a c -> p (a c)")[:, 0:NW], AX.X, ALU.max, negate=True).then_inc(max_done, 1)
                    eng.wait_ge(pd_turned, x + 1)
                    if not (first and j == 0):
                        eng.wait_ge(od_done, x)
                    p3 = PT[:, 0:13 * GRP].rearrange("p (c h) -> p c h", h=GRP)
                    eng.tensor_copy(pTs[:, 0:7, :], p3[:, 0:7, :])
                    eng.tensor_copy(pTs[0:65, 7, :], p3[0:65, 7, :])
                    eng.tensor_copy(pTs[:, 8:12, :], p3[:, 8:12, :])
                    eng.drain()
                    eng.tensor_copy(pTs[0:1, 12, :], p3[0:1, 12, :]).then_inc(pd_saved, 1)
                    eng.reciprocal(sums[:, 2:4], sums[:, 0:2])
                    eng.drain()
                    eng.wait_ge(od_done, x + 1)
                    for k, o in enumerate((oS, oW)):
                        eng.tensor_scalar(o[:, bass.ds(x, 1), :].rearrange("p o d -> p (o d)"), OD[:, k * HD:(k + 1) * HD], sums[:, 2 + k:3 + k], None, ALU.mult).then_inc(od_saved, 1)
                turns(eng, body)

            @block.scalar
            def _(eng):
                def body(b, j):
                    first = isinstance(b, int)
                    x = b * 2 + j
                    eng.wait_ge(max_done, x + 1)
                    if not (first and j == 0):
                        eng.wait_ge(pd_turned, x)
                        eng.wait_ge(od_saved, x * 2)
                    eng.activation(pd[:, 0:NS], SD[:, 0:2, :].rearrange("p a c -> p (a c)")[:, 0:NS], ACT.Exp, bias=nmx[:, 0:1], accum_out=sums[:, 0:1]).then_inc(exps_done, 1)
                    eng.activation(pd[:, 1000:1000 + NW], SD[:, 2:4, :].rearrange("p a c -> p (a c)")[:, 0:NW], ACT.Exp, bias=nmx[:, 1:2], accum_out=sums[:, 1:2]).then_inc(exps_done, 1)
                turns(eng, body)


def mix_out(nc, io, g):
    with ExitStack() as ctx:
        sb = lambda n, s, t=F32: ctx.enter_context(nc.sbuf_tensor(n, s, t))
        ps = lambda n, s, t=F32: ctx.enter_context(nc.psum_tensor(n, s, t))
        sem = lambda n: g["sem"](n)
        NTILE = TILES + 1
        rows = lambda n: P if n < TILES else NB
        mix, ident, gates = g["mix"], g["ident"], g["gates"]
        hT = g["late"][:, 0:KT * TOK].rearrange("p (k t) -> p k t", k=KT)
        w = sb("w_out_sb", [P, KT, D])
        gout = sb("g_out_rows", [P, D])
        gffn = sb("g_ffn_col", [P, KT])
        x = sb("x_again", [P, 2, D])
        h = sb("h_rows", [P, 2, D])
        sq = sb("mix_squares", [P, D])
        junk = sb("h_squares", [P, D])
        half = sb("minus_half2", [P, 16])
        s16 = sb("mix_ss", [P, 2, 16])
        ss = sb("h_ss", [P, 2, 2])
        mn = sb("mix_normed", [P, 2, D])
        mT = sb("mix_turned", [P, 2, KT, P])
        hn = sb("h_normed", [P, 2, D])
        o3 = sb("o_dec_rows", [NB, 3, 512])
        px = ps("px2", [P, 2, 512])
        py = ps("py2", [P, 2, 512])
        ph = ps("ph2", [P, 2, 2, 512])
        c_loaded, w_loaded, dec_loaded = map(sem, ("c_loaded2", "w_out_loaded", "dec_loaded"))
        x_loaded = [sem("x_again0"), sem("x_again1")]
        stored = [sem("h_stored0"), sem("h_stored1")]
        names = ("mix_ready", "squared", "summed2", "rstd16", "mix_normed_s", "mix_turned_s", "mix_saved", "projected",
                 "h_done", "h_squared", "h_rstd", "h_normed_s", "h_turned", "h_saved")
        mix_ready, squared, summed, rstd16, normed, turned, mT_saved, projected, h_done, h_squared, h_rstd, h_normed, h_turned, h_saved = map(sem, names)

        with nc.Block() as block:
            @block.sync
            def _(eng):
                def store(eng, n):
                    R, u = rows(n), n % 2
                    eng.wait_ge(h_done, n + 1)
                    eng.dma_start(io["h_s"][n * P:n * P + R, :], h[0:R, u, :]).then_inc(stored[u], 16)

                eng.dma_start(gout[:, 0:512], io["g_out_nsa"][0].rearrange("h d -> (h d)").partition_broadcast(P)).then_inc(c_loaded, 16)
                eng.dma_start(gout[:, 512:D], io["g_out_sb"][0].rearrange("h d -> (h d)").partition_broadcast(P)).then_inc(c_loaded, 16)
                eng.dma_start(gffn[:, :], io["g_ffn"].rearrange("a (k p) -> p (a k)", p=P), allow_slow_non_contiguous=True).then_inc(c_loaded, 16)
                eng.dma_start(w[:, :, :], io["w_out"][0].rearrange("(k p) n -> p k n", p=P)).then_inc(w_loaded, 16)
                eng.dma_start(o3[:, :, :], io["o_s"].rearrange("c b n -> b c n")).then_inc(dec_loaded, 16)
                eng.dma_start(mix[0:NB, TILES, 512:D], io["osb_s"]).then_inc(dec_loaded, 16)
                for n in range(NTILE):
                    R, u = rows(n), n % 2
                    if n >= 2:
                        eng.wait_ge(h_done, n - 1)
                    src = io["x_prompt"][0, n * P:(n + 1) * P, :] if n < TILES else io["x_sample"].rearrange("b t d -> (b t) d")
                    eng.dma_start(x[0:R, u, :], src).then_inc(x_loaded[u], 16)
                    if n >= 1:
                        store(eng, n - 1)
                store(eng, TILES)
                eng.wait_ge(stored[0], 80)
                eng.wait_ge(stored[1], 64)

            @block.gpsimd
            def _(eng):
                eng.memset(half[:, :], -0.5)
                eng.drain()
                for n in range(NTILE + 1):
                    if n < NTILE:
                        R, u = rows(n), n % 2
                        eng.wait_ge(summed, n + 1)
                        eng.tensor_scalar(s16[0:R, u, :], s16[0:R, u, :], 1.0 / HD, EPS, ALU.mult, ALU.add)
                        eng.drain()
                        eng.tensor_tensor(s16[0:R, u, :], s16[0:R, u, :], half[0:R, :], ALU.pow).then_inc(rstd16, 1)
                    if n >= 1:
                        R, u = rows(n - 1), (n - 1) % 2
                        eng.wait_ge(h_squared, n)
                        eng.tensor_scalar(ss[0:R, u, 1:2], ss[0:R, u, 0:1], 1.0 / D, EPS, ALU.mult, ALU.add)
                        eng.drain()
                        eng.tensor_tensor(ss[0:R, u, 1:2], ss[0:R, u, 1:2], half[0:R, 0:1], ALU.pow).then_inc(h_rstd, 1)

            @block.scalar
            def _(eng):
                def square_mix(n):
                    R = rows(n)
                    if n == TILES:
                        eng.wait_ge(mix_ready, 1)
                        eng.wait_ge(dec_loaded, 32)
                    if n >= 1:
                        eng.wait_ge(summed, n)
                    eng.activation(sq[0:R, :], mix[0:R, n, :], ACT.Square).then_inc(squared, 1)

                def save_mT(n):
                    R, u = rows(n), n % 2
                    if n >= 2:
                        eng.wait_ge(projected, n - 1)
                    for b in range(2):
                        eng.wait_ge(turned, 2 * n + b + 1)
                        eng.activation(mT[:, u, 4 * b:4 * b + 4, 0:R], px[:, b, :].rearrange("p (k r) -> p k r", k=4)[:, :, 0:R], ACT.Copy).then_inc(mT_saved, 1)

                square_mix(0)
                save_mT(0)
                for n in range(NTILE):
                    R, u = rows(n), n % 2
                    if n + 1 < NTILE:
                        square_mix(n + 1)
                        save_mT(n + 1)
                    eng.wait_ge(h_done, n + 1)
                    if n >= 2:
                        eng.wait_ge(h_normed, n - 1)
                    eng.drain()
                    eng.activation(junk[0:R, :], h[0:R, u, :], ACT.Square, accum_out=ss[0:R, u, 0:1]).then_inc(h_squared, 1)

            @block.tensor
            def _(eng):
                def turn(n, src, ready, bank, saved, done):
                    R, u = rows(n), n % 2
                    eng.wait_ge(ready, n + 1)
                    for b in range(2):
                        if n >= 1:
                            eng.wait_ge(saved, 2 * (n - 1) + b + 1)
                        for k in range(4):
                            c = (4 * b + k) * P
                            mm = eng.transpose(bank[:, b, k * P:k * P + R], src[0:R, u, c:c + P], ident[0:R, 0:R])
                        mm.then_inc(done, 1)

                eng.wait_ge(w_loaded, 16)
                turn(0, mn, normed, px, mT_saved, turned)
                for n in range(NTILE + 1):
                    if n < NTILE:
                        R, u = rows(n), n % 2
                        eng.wait_ge(mT_saved, 2 * n + 2)
                        if n >= 2:
                            eng.wait_ge(h_done, n - 1)
                        for c in range(2):
                            for k in range(KT):
                                mm = eng.matmul(ph[0:R, u, c, :], mT[:, u, k, 0:R], w[:, k, c * 512:(c + 1) * 512], start=k == 0, stop=k == KT - 1)
                            if c == 0 and n + 1 < NTILE:
                                turn(n + 1, mn, normed, px, mT_saved, turned)
                        mm.then_inc(projected, 1)
                    if n >= 1:
                        turn(n - 1, hn, h_normed, py, h_saved, h_turned)

            @block.vector
            def _(eng):
                eng.wait_ge(c_loaded, 48)
                eng.wait_ge(dec_loaded, 32)
                m = mix[0:NB, TILES, 0:512].rearrange("b (h d) -> b h d", h=NH)
                for br in range(3):
                    o = o3[:, br, :].rearrange("b (h d) -> b h d", h=NH)
                    gt = gates[0:NB, TILES, br:24:3].unsqueeze(2).broadcast_to([NB, NH, HD])
                    eng.tensor_tensor(o, o, gt, ALU.mult)
                eng.drain()
                o = [o3[:, br, :].rearrange("b (h d) -> b h d", h=NH) for br in range(3)]
                eng.tensor_tensor(m, o[0], o[1], ALU.add)
                eng.drain()
                eng.tensor_tensor(m, m, o[2], ALU.add).then_inc(mix_ready, 1)

                def norm_mix(n):
                    R, u = rows(n), n % 2
                    eng.wait_ge(squared, n + 1)
                    if n >= 2:
                        eng.wait_ge(turned, 2 * (n - 1))
                    eng.tensor_reduce(s16[0:R, u, :], sq[0:R, :].rearrange("p (h d) -> p h d", h=16), AX.X, ALU.add).then_inc(summed, 1)
                    eng.wait_ge(rstd16, n + 1)
                    eng.drain()
                    eng.tensor_tensor(mn[0:R, u, :].rearrange("p (h d) -> p h d", h=16), mix[0:R, n, :].rearrange("p (h d) -> p h d", h=16),
                                      s16[0:R, u, :].unsqueeze(2).broadcast_to([R, 16, HD]), ALU.mult)
                    eng.drain()
                    eng.tensor_tensor(mn[0:R, u, :], mn[0:R, u, :], gout[0:R, :], ALU.mult).then_inc(normed, 1)

                norm_mix(0)
                norm_mix(1)
                for n in range(NTILE + 1):
                    if n < NTILE:
                        R, u = rows(n), n % 2
                        eng.wait_ge(projected, n + 1)
                        eng.wait_ge(x_loaded[u], 16 * (n // 2) + 16)
                        if n >= 2:
                            eng.wait_ge(stored[u], 16 * (n // 2))
                            eng.wait_ge(h_squared, n - 1)
                        eng.tensor_tensor(h[0:R, u, :], ph[0:R, u, :, :].rearrange("p c n -> p (c n)"), x[0:R, u, :], ALU.add).then_inc(h_done, 1)
                        if n + 2 < NTILE:
                            norm_mix(n + 2)
                        eng.wait_ge(h_rstd, n + 1)
                        if n >= 2:
                            eng.wait_ge(h_turned, 2 * (n - 1))
                        eng.tensor_scalar(hn[0:R, u, :], h[0:R, u, :], ss[0:R, u, 1:2], None, ALU.mult).then_inc(h_normed, 1)
                    if n >= 1:
                        R = rows(n - 1)
                        for b in range(2):
                            eng.wait_ge(h_turned, 2 * (n - 1) + b + 1)
                            out = hT[:, 4 * b:4 * b + 4, (n - 1) * P:(n - 1) * P + R]
                            eng.tensor_tensor(out, py[:, b, :].rearrange("p (k r) -> p k r", k=4)[:, :, 0:R],
                                              gffn[:, 4 * b:4 * b + 4].unsqueeze(2).broadcast_to([P, 4, R]), ALU.mult).then_inc(h_saved, 1)


def swiglu(nc, io, g):
    NF, NC, CW = DFF // P, 3, TOK // 3
    NTILE = TILES + 1
    rows = lambda n: P if n < TILES else NB
    with ExitStack() as ctx:
        sb = lambda n, s, t=F32: ctx.enter_context(nc.sbuf_tensor(n, s, t))
        late = g["late"]
        hT = late[:, 0:KT * TOK].rearrange("p (k t) -> p k t", k=KT)
        ring = late[:, KT * TOK:KT * TOK + 4096].rearrange("p (u k c f) -> p u k c f", u=2, k=KT, c=2)
        act = sb("swiglu_act", [P, NF, TOK])
        wd0 = sb("w_down0", [P, NF, 512])
        wd1 = late[:, 0:NF * 512].rearrange("p (f n) -> p f n", f=NF)
        wd_loaded = g["sem"]("wd_loaded")
        wdv = io["w_down"][0].rearrange("(f p) n -> p f n", p=P)
        with ExitStack() as c2:
            sem = lambda n: g["sem"](n)
            pg = c2.enter_context(nc.psum_tensor("pg", [P, NC, 2, 512], F32))
            sg = c2.enter_context(nc.sbuf_tensor("silu_gate", [P, 2, CW], F32))
            w_loaded = [sem("wgu_loaded0"), sem("wgu_loaded1")]
            up_done, silu_done, act_done = map(sem, ("up_done", "silu_done", "act_done"))
            with nc.Block() as block:
                @block.sync
                def _(eng):
                    wv = io["w_gate_up"][0].rearrange("(k p) (c f) -> p k c f", p=P, c=2)

                    def load(f, u):
                        for c in range(2):
                            eng.dma_start(ring[:, u, :, c], wv[:, :, c, bass.ds(f * P, P)]).then_inc(w_loaded[u], 16)
                    load(0, 0)
                    load(1, 1)
                    eng.dma_start(wd0[:, :, :], wdv[:, :, 0:512]).then_inc(wd_loaded, 16)
                    with eng.Fori(1, NF // 2) as i:
                        for u in range(2):
                            eng.wait_ge(up_done, (i * 2 + u - 1) * NC)
                            load(i * 2 + u, u)

                @block.tensor
                def _(eng):
                    def body(i, u):
                        eng.wait_ge(w_loaded[u], i * 32 + 32)
                        for c in range(NC):
                            if not (isinstance(i, int) and u == 0):
                                eng.wait_ge(act_done, (i * 2 + u - 1) * NC + c + 1)
                            for e in range(2):
                                for k in range(KT):
                                    mm = eng.matmul(pg[:, c, e, 0:CW], ring[:, u, k, e, :], hT[:, k, c * CW:(c + 1) * CW], start=k == 0, stop=k == KT - 1)
                            mm.then_inc(up_done, 1)
                    body(0, 0)
                    body(0, 1)
                    with eng.Fori(1, NF // 2) as i:
                        body(i, 0)
                        body(i, 1)

                @block.scalar
                def _(eng):
                    def body(i, u):
                        for c in range(NC):
                            m = (i * 2 + u) * NC + c
                            eng.wait_ge(up_done, m + 1)
                            s = (u * NC + c) % 2
                            if not (isinstance(i, int) and m < 2):
                                eng.wait_ge(act_done, m - 1)
                            eng.activation(sg[:, s, :], pg[:, c, 0, 0:CW], ACT.Silu).then_inc(silu_done, 1)
                    body(0, 0)
                    body(0, 1)
                    with eng.Fori(1, NF // 2) as i:
                        body(i, 0)
                        body(i, 1)

                @block.vector
                def _(eng):
                    with eng.Fori(0, NF // 2) as i:
                        for u in range(2):
                            for c in range(NC):
                                m = (i * 2 + u) * NC + c
                                eng.wait_ge(silu_done, m + 1)
                                out = act[:, bass.ds(i * 2 + u, 1), c * CW:(c + 1) * CW].rearrange("p o t -> p (o t)")
                                eng.tensor_tensor(out, sg[:, (u * NC + c) % 2, :], pg[:, c, 1, 0:CW], ALU.mult).then_inc(act_done, 1)
        with ExitStack() as c2:
            sem = lambda n: g["sem"](n)
            py = c2.enter_context(nc.psum_tensor("py3", [P, 4, 512], F32))
            hr = c2.enter_context(nc.sbuf_tensor("h_back", [P, 4, 512], F32))
            y = c2.enter_context(nc.sbuf_tensor("y_rows", [P, 2, 512], F32))
            h_loaded = [sem(f"h_back{r}") for r in range(4)]
            down_done, y_done = sem("down_done"), sem("y_done")
            stored = [sem("y_stored0"), sem("y_stored1")]
            jobs = [(c, n) for c in range(2) for n in range(NTILE)]
            with nc.Block() as block:
                @block.sync
                def _(eng):
                    eng.dma_start(wd1, wdv[:, :, 512:D]).then_inc(wd_loaded, 16)
                    for m, (c, n) in enumerate(jobs):
                        R = rows(n)
                        if m >= 4:
                            eng.wait_ge(y_done, m - 3)
                        eng.dma_start(hr[0:R, m % 4], io["h_s"][n * P:n * P + R, c * 512:c * 512 + 512]).then_inc(h_loaded[m % 4], 16)

                @block.scalar
                def _(eng):
                    for m, (c, n) in enumerate(jobs):
                        R = rows(n)
                        dst = io["y_prompt"][n * P:(n + 1) * P] if n < TILES else io["y_sample"]
                        eng.wait_ge(y_done, m + 1)
                        eng.dma_start(dst[:, c * 512:c * 512 + 512], y[0:R, m % 2]).then_inc(stored[m % 2], 16)
                    for s in stored:
                        eng.wait_ge(s, 16 * len(jobs) // 2)

                @block.tensor
                def _(eng):
                    eng.wait_ge(wd_loaded, 16)
                    for m, (c, n) in enumerate(jobs):
                        R = rows(n)
                        if m == NTILE:
                            eng.wait_ge(wd_loaded, 32)
                        if m >= 4:
                            eng.wait_ge(y_done, m - 3)
                        for f in range(NF):
                            mm = eng.matmul(py[0:R, m % 4, :], act[:, f, n * P:n * P + R], (wd0, wd1)[c][:, f, :], start=f == 0, stop=f == NF - 1)
                        mm.then_inc(down_done, 1)

                @block.vector
                def _(eng):
                    for m, (c, n) in enumerate(jobs):
                        R = rows(n)
                        eng.wait_ge(down_done, m + 1)
                        eng.wait_ge(h_loaded[m % 4], 16 * (m // 4) + 16)
                        if m >= 2:
                            eng.wait_ge(stored[m % 2], 16 * (m // 2))
                        eng.tensor_tensor(y[0:R, m % 2], py[0:R, m % 4], hr[0:R, m % 4], ALU.add).then_inc(y_done, 1)


_INS = ["x_prompt", "x_sample", "cache_nsa_kv", "cache_sb_kv", "state_nsa_window", "page_table", "g_attn", "w_in",
        "g_q", "g_k", "w_cmp1_k", "w_cmp2_k", "pe_cmp_k", "w_cmp1_v", "w_cmp2_v", "pe_cmp_v", "g_out_nsa",
        "g_out_sb", "w_out", "g_ffn", "w_gate_up", "w_down"]

_OUTS = [("y_prompt", (1, SEQ, D)), ("y_sample", (NB, 1, D)), ("nsa_p", (1, 1, SEQ, 4, KVH, HD)), ("nsa_s", (1, NB, 1, 4, KVH, HD)),
         ("sb_p", (1, 1, SEQ, 2, NH, HD)), ("sb_s", (1, NB, 1, 2, NH, HD)),
         ("win_p_out", (1, 1, WINDOW, 2, KVH, HD)), ("win_s_out", (1, NB, WINDOW, 2, KVH, HD))]


def build(nc, io):
    with ExitStack() as ctx:
        sb = lambda n, s, t=F32: ctx.enter_context(nc.sbuf_tensor(n, s, t))
        taken = []

        def new_sem(name):
            taken.append(nc.alloc_semaphore(name))
            return taken[-1]

        def give_back():
            nc.all_engine_barrier()
            nc.clear_and_free_semaphores(taken)
            nc.all_engine_barrier()
            taken.clear()

        g = {"sem": new_sem, "ident": sb("ident", [P, P]), "gates": sb("gates", [P, TILES + 1, 24])}
        loaded = nc.alloc_semaphore("ident_loaded")
        with nc.Block() as block:
            @block.sync
            def _(eng):
                eng.dma_start(g["ident"][:, :], io["c_ident"]).then_inc(loaded, 16)
                eng.wait_ge(loaded, 16)
        project(nc, io, g)
        g["late"] = sb("late", [P, KT * TOK + 4096])
        with ExitStack() as mid:
            sm = lambda n, s, t=F32: mid.enter_context(nc.sbuf_tensor(n, s, t))
            g["mix"] = sm("mix", [P, TILES + 1, D])
            with ExitStack() as inner:
                si = lambda n, s, t=F32: inner.enter_context(nc.sbuf_tensor(n, s, t))
                g.update({"pt": si("page_table_sb", [1, NB * NPAGE], I32),
                          "kcT": si("kc_turned", [HD, NB * KVH, NCS]), "vc": si("vc_rows", [P, NB * KVH, 2, HD]),
                          "kcTp": si("kc_prompt", [HD, KVH, NCP]), "vcp": si("vc_prompt", [64, KVH, HD + 1])})
                compress(nc, io, g)
                give_back()
                attend(nc, io, g)
                decode_sb(nc, io, g)
                decode_nsa(nc, io, g)
                give_back()
            mix_out(nc, io, g)
        swiglu(nc, io, g)


def kernel(**inputs):
    import concourse.bacc as _bacc
    from concourse.bass_utils import run_bass_kernel_spmd as _run

    nc = _bacc.Bacc("TRN2", target_bir_lowering=False, num_devices=1)
    arrays, io = {}, {}
    for name in _INS:
        a = np.ascontiguousarray(inputs[name])
        if a.dtype.kind in "iu":
            a = a.astype(np.int32)
        arrays["in_" + name] = a
        io[name] = nc.dram_tensor("in_" + name, a.shape, mybir.dt.from_np(a.dtype), kind="ExternalInput").ap()
    for name, a in constants().items():
        arrays[name] = np.ascontiguousarray(a)
        io[name] = nc.dram_tensor(name, a.shape, F32, kind="ExternalInput").ap()
    outs = {n: nc.dram_tensor("out_" + n, s, F32, kind="ExternalOutput").ap() for n, s in _OUTS}
    flat = lambda ap: ap.rearrange("a b t c j d -> (a b t) (c j d)")
    for n in ("nsa_p", "nsa_s", "sb_p", "sb_s"):
        io[n] = flat(outs[n])
    io["y_prompt"] = outs["y_prompt"][0]
    io["y_sample"] = outs["y_sample"].rearrange("b t d -> (b t) d")
    io["win_p_out"] = flat(outs["win_p_out"])
    io["win_s_out"] = outs["win_s_out"][0].rearrange("b t c j d -> b t (c j d)")
    scratch = lambda n, s: nc.dram_tensor("scratch_" + n, s, F32, kind="Internal").ap()
    io["win_p"] = scratch("win_p", (SEQ, 256))
    io["win_new"] = scratch("win_new", (NB, 256))
    io["T"] = scratch("T", (NT * HD, SEQ))
    io["Ts"] = scratch("Ts", (NT * HD, NB))
    io["sbq_s"] = scratch("sbq_s", (NB, 512))
    io["osb_s"] = scratch("osb_s", (NB, 512))
    io["h_s"] = scratch("h_s", (TOK, D))
    io["cache_blocks"] = io["cache_nsa_kv"][0].rearrange("n (a s) f j d -> (n a) s (f j) d", a=2)
    io["o_s"] = scratch("o_s", (3, NB, 512))
    io["T3"] = io["T"].rearrange("(h d) t -> h d t", d=HD)
    io["cache_nsa"] = io["cache_nsa_kv"][0].rearrange("n (s r) f j d -> (n s) r (f j d)", r=2)
    io["cache_sb"] = io["cache_sb_kv"][0].rearrange("n s c h d -> (n s) c (h d)")
    io["state"] = io["state_nsa_window"][0].rearrange("b t c j d -> b t (c j d)")
    nc.disable_value_cache = True
    build(nc, io)
    r = _run(nc, [arrays], core_ids=[0])
    return tuple(r.results[0]["out_" + n] for n, _ in _OUTS)
```

```python
import math
from contextlib import ExitStack

import numpy as np
import concourse.bass as bass
from concourse import mybir

F32 = mybir.dt.float32
F32R = mybir.dt.float32r
BF16 = mybir.dt.bfloat16
I32 = mybir.dt.int32
U32 = mybir.dt.uint32
ALU = mybir.AluOpType
ACT = mybir.ActivationFunctionType
AX = mybir.AxisListType

P = 128
D = 1024
SEQ = 1024
NB = 8
PAST = 4096
PAGE = 128
NPAGE = PAST // PAGE
NPOOL = NB * NPAGE * 5 // 4
HD = 64
NH = 8
KVH = 2
GRP = NH // KVH
WINDOW = 512
DFF = 2816
PROJ = 2840
KT = D // P
TILES = SEQ // P
NCP = (SEQ - 32) // 16 + 1
NCS = (PAST + 1 - 32) // 16 + 1
NBLK = PAST // 64
NSEL = 15
EPS = 1e-6
NEG = -1e30
SCALE = HD ** -0.5

COLS = [(0, 512), (512, 1024), (1024, 1304), (1304, 1816), (1816, 2328), (2328, 2840)]
GATE0, SBQ0, SBK0 = 1280, 1304, 1816
T_QN, T_KS, T_KW, T_QS, T_KB = 0, 8, 10, 12, 20
NT = 28
TOK = SEQ + NB


def constants():
    inv = np.exp(-math.log(10000.0) * np.arange(0, HD, 2, dtype=np.float32) / HD).astype(np.float32)
    pos = np.concatenate([np.arange(SEQ), np.full(P, PAST)]).astype(np.float32)
    ang = pos[:, None] * inv[None, :]
    rot = np.stack([np.cos(ang), np.sin(ang)], 1).astype(np.float32)
    i, j = np.arange(P)[:, None], np.arange(P)[None, :]
    masks = np.zeros((P, 3, P), np.float32)
    masks[:, 0] = np.where(j > i, NEG, 0)
    masks[:, 1] = np.where(j >= i, NEG, 0)
    masks[:, 2] = np.where(j < i, NEG, 0)
    cend = np.arange(64) * 16 + 31
    cmask = np.where(cend[None, :] <= np.arange(SEQ)[:, None], 0, NEG).astype(np.float32)
    cmask = cmask.reshape(TILES, P, 64).transpose(1, 0, 2)
    rowok = (np.arange(P) >= 31).astype(np.float32)[:, None]
    c = np.arange(256)[:, None] * 16
    b = np.arange(NBLK)[None, :] * 64
    ov = ((c < b + 64) & (c + 32 > b)).astype(np.float32)
    ov[NCS:] = 0
    ov = ov.reshape(2, P, NBLK).transpose(1, 0, 2)
    k, r = np.arange(NBLK), np.arange(16)
    sel = np.zeros((NBLK, 3, NBLK), np.float32)
    sel[:, 0] = np.eye(NBLK)
    sel[:, 1] = (k[None, :] < k[:, None])
    sel[:, 2] = np.where((k == 0) | (k == NBLK - 1), 1e30, 0)[None, :]
    ranks = np.broadcast_to(r, (NBLK, 16)).astype(np.float32)
    blk = np.stack([(k // 2), (k % 2)], 1).astype(np.float32)
    pageof = (np.arange(NPAGE)[:, None] == (k // 2)[None, :]).astype(np.float32)
    off = np.stack([(np.arange(P) < 64), (np.arange(P) >= 64), (np.arange(P) % 64) * 8], 1).astype(np.float32)
    tri = (i >= j).astype(np.float32)
    diag = np.zeros((NH, NH, HD), np.float32)
    for h in range(NH):
        diag[h, h] = 1
    return {
        "c_rot": rot.reshape(TILES + 1, P, 64), "c_ident": np.eye(P, dtype=np.float32),
        "c_masks": masks, "c_cmask": cmask, "c_rowok": rowok, "c_ov": ov, "c_sel": sel,
        "c_ranks": ranks, "c_blk": blk, "c_pageof": pageof, "c_off": off, "c_tri": tri, "c_diag": diag,
    }


def project(nc, io, g):
    with ExitStack() as ctx:
        sb = lambda n, s, t=F32: ctx.enter_context(nc.sbuf_tensor(n, s, t))
        ps = lambda n, s, t=F32: ctx.enter_context(nc.psum_tensor(n, s, t))
        sem = lambda n: g["sem"](n)
        w = sb("w_in_sb", [P, KT, PROJ])
        x = sb("x_sb", [P, 2, D])
        xn = sb("xn_sb", [P, 2, D])
        xT = sb("xT_sb", [P, 2, KT, P])
        pj = sb("proj_sb", [P, 2, PROJ])
        junk = sb("squares_sb", [P, D])
        ss = sb("ss_sb", [P, 2, 2])
        half = sb("minus_half", [P, 16])
        rot = sb("rot_sb", [P, 2, 64])
        gat = sb("g_attn_col", [P, KT])
        gqk = sb("g_qk_sb", [P, 14, HD])
        sq = sb("qk_squares", [P, 14, HD])
        hss = sb("head_ss", [P, 2, 16])
        r1 = sb("normed", [P, 14, HD])
        ra = sb("rot_a", [P, 14, HD])
        rb = sb("rot_b", [P, 14, HD])
        ro = sb("roped", [P, 2, 14, HD])
        kvo = sb("kv_out", [P, 2, 6, P])
        ts = sb("transposed", [P, 2, 14, P])
        sbq = sb("sb_q_scaled", [NB, 512])
        px = ps("px", [P, 2, 512])
        pp = ps("pp", [P, 4, 512])
        pt = ps("pt", [P, 2, 512])
        w_loaded = [sem(f"w_loaded{c}") for c in range(6)]
        c_loaded = sem("c_loaded")
        x_loaded = [sem("x_loaded0"), sem("x_loaded1")]
        x_squared, x_rstd, x_normed, x_turned, x_ready = map(sem, ("x_squared", "x_rstd", "x_normed", "x_turned", "x_ready"))
        proj_done, proj_saved = map(sem, ("proj_done", "proj_saved"))
        qk_squared, qk_summed, qk_rstd, roped, kv_copied = map(sem, ("qk_squared", "qk_summed", "qk_rstd", "roped", "kv_copied"))
        turned, turned_saved, sbq_scaled = map(sem, ("turned", "turned_saved", "sbq_scaled"))
        stored = [sem("stored0"), sem("stored1")]
        NTILE = TILES + 1
        rows = lambda n: P if n < TILES else NB
        ident = g["ident"]

        with nc.Block() as block:
            @block.sync
            def _(eng):
                eng.dma_start(gat[:, :], io["g_attn"].rearrange("a (k p) -> p (a k)", p=P), allow_slow_non_contiguous=True).then_inc(c_loaded, 16)
                for h in range(8):
                    eng.dma_start(gqk[:, h, :], io["g_q"][0].partition_broadcast(P)).then_inc(c_loaded, 16)
                for r in range(3):
                    for j in range(2):
                        eng.dma_start(gqk[:, 8 + 2 * r + j, :], io["g_k"][0, r].partition_broadcast(P)).then_inc(c_loaded, 16)
                def load(n):
                    R, u = rows(n), n % 2
                    if n >= 2:
                        eng.wait_ge(x_normed, n - 1)
                        eng.wait_ge(roped, n - 1)
                    src = io["x_prompt"][0, n * P:(n + 1) * P, :] if n < TILES else io["x_sample"].rearrange("b t d -> (b t) d")
                    eng.dma_start(x[0:R, u, :], src).then_inc(x_loaded[u], 16)
                    eng.dma_start(rot[0:R, u, :], io["c_rot"][n, 0:R]).then_inc(x_loaded[u], 16)

                def store(n):
                    R, u, t0 = rows(n), n % 2, n * P
                    k4 = kvo[0:R, u, 0:4, :].rearrange("p r e -> p (r e)")
                    k2 = kvo[0:R, u, 4:6, :].rearrange("p r e -> p (r e)")
                    last = n == TILES
                    eng.wait_ge(kv_copied, n + 1)
                    eng.dma_start(io["nsa_s"] if last else io["nsa_p"][t0:t0 + R, :], k4).then_inc(stored[u], 16)
                    eng.dma_start(io["win_new"] if last else io["win_p"][t0:t0 + R, :], k2).then_inc(stored[u], 16)
                    eng.wait_ge(proj_saved, 6 * n + 6)
                    eng.dma_start(io["sb_s"] if last else io["sb_p"][t0:t0 + R, :], pj[0:R, u, SBK0:PROJ]).then_inc(stored[u], 16)
                    eng.wait_ge(turned_saved, 4 * n + 4)
                    if last:
                        eng.dma_start(io["Ts"].rearrange("(m p) t -> p m t", p=P), ts[:, u, :, 0:R], allow_slow_non_contiguous=True).then_inc(stored[u], 16)
                        eng.wait_ge(sbq_scaled, 1)
                        eng.dma_start(io["sbq_s"], sbq[:, :]).then_inc(stored[u], 16)
                    else:
                        eng.dma_start(io["T"].rearrange("(m p) t -> p m t", p=P)[:, :, t0:t0 + R], ts[:, u, :, :]).then_inc(stored[u], 16)

                load(0)
                wv = io["w_in"][0].rearrange("(k p) n -> p k n", p=P)
                for c, (a, b) in enumerate(COLS):
                    eng.dma_start(w[:, :, a:b], wv[:, :, a:b]).then_inc(w_loaded[c], 16)
                load(1)
                for n in range(NTILE):
                    if n + 2 < NTILE:
                        load(n + 2)
                    store(n)
                eng.wait_ge(stored[0], 64 * 5 + 16)
                eng.wait_ge(stored[1], 64 * 4)

            @block.gpsimd
            def _(eng):
                eng.memset(half[:, :], -0.5)
                eng.drain()

                def head_norm(n):
                    R, u = rows(n), n % 2
                    eng.wait_ge(qk_summed, n + 1)
                    eng.tensor_scalar(hss[0:R, u, 0:14], hss[0:R, u, 0:14], 1.0 / HD, EPS, ALU.mult, ALU.add)
                    eng.drain()
                    eng.tensor_tensor(hss[0:R, u, 0:14], hss[0:R, u, 0:14], half[0:R, 0:14], ALU.pow).then_inc(qk_rstd, 1)

                def join_rows(n):
                    R, u = rows(n), n % 2
                    eng.wait_ge(roped, n + 1)
                    eng.wait_ge(proj_saved, 6 * n + 6)
                    if n >= 2:
                        eng.wait_ge(stored[u], 64 * (n // 2))
                    rv = ro[0:R, u, 8:14, :].rearrange("p (r j) d -> p r (j d)", j=2)
                    kv = kvo[0:R, u, :, :].rearrange("p (r c) e -> p r c e", c=2)
                    pv = pj[0:R, u, 512:1280].rearrange("p (r c e) -> p r c e", r=3, c=2)
                    eng.tensor_copy(kv[:, :, 0, :], rv)
                    eng.tensor_copy(kv[:, :, 1, :], pv[:, :, 1, :]).then_inc(kv_copied, 1)

                for n in range(NTILE):
                    R, u = rows(n), n % 2
                    eng.wait_ge(x_squared, n + 1)
                    eng.tensor_scalar(ss[0:R, u, 1:2], ss[0:R, u, 0:1], 1.0 / D, EPS, ALU.mult, ALU.add)
                    eng.drain()
                    eng.tensor_tensor(ss[0:R, u, 1:2], ss[0:R, u, 1:2], half[0:R, 0:1], ALU.pow).then_inc(x_rstd, 1)
                    if n >= 1:
                        head_norm(n - 1)
                        join_rows(n - 1)
                head_norm(TILES)
                join_rows(TILES)

            @block.scalar
            def _(eng):
                def square(n):
                    R, u = rows(n), n % 2
                    eng.wait_ge(x_loaded[u], 32 * (n // 2 + 1))
                    eng.drain()
                    eng.activation(junk[0:R, :], x[0:R, u, :], ACT.Square, accum_out=ss[0:R, u, 0:1]).then_inc(x_squared, 1)
                square(0)
                for n in range(NTILE):
                    R, u = rows(n), n % 2
                    if n + 1 < NTILE:
                        if n >= 1:
                            eng.wait_ge(x_normed, n)
                        square(n + 1)
                    for c, (a, b) in enumerate(COLS):
                        if n >= 2 and c == 0:
                            eng.wait_ge(stored[u], 64 * (n // 2))
                            eng.wait_ge(turned, 4 * (n - 1))
                            eng.wait_ge(roped, n - 1)
                        eng.wait_ge(proj_done, 6 * n + c + 1)
                        eng.activation(pj[0:R, u, a:b], pp[0:R, (6 * n + c) % 4, 0:b - a], ACT.Copy).then_inc(proj_saved, 1)
                    eng.drain()
                    if n >= 1:
                        eng.wait_ge(qk_summed, n)
                    eng.activation(sq[0:R, 0:8, :].rearrange("p h d -> p (h d)"), pj[0:R, u, 0:512], ACT.Square)
                    kk = pj[0:R, u, 512:1280].rearrange("p (r c e) -> p r c e", r=3, c=2)[:, :, 0, :]
                    eng.activation(sq[0:R, 8:14, :].rearrange("p (r j) d -> p r (j d)", j=2), kk, ACT.Square).then_inc(qk_squared, 1)
                    eng.activation(g["gates"][0:R, n, :], pj[0:R, u, GATE0:GATE0 + 24], ACT.Sigmoid)
                    if n == TILES:
                        eng.activation(sbq[:, :], pj[0:R, u, SBQ0:SBK0], ACT.Copy, scale=SCALE).then_inc(sbq_scaled, 1)

            @block.tensor
            def _(eng):
                def x_transposes(n):
                    R, u = rows(n), n % 2
                    eng.wait_ge(x_normed, n + 1)
                    for b in range(2):
                        if n >= 1:
                            eng.wait_ge(x_ready, 2 * (n - 1) + b + 1)
                        for k in range(4):
                            mm = eng.transpose(px[:, b, k * P:k * P + R], xn[0:R, u, (4 * b + k) * P:(4 * b + k + 1) * P], ident[0:R, 0:R])
                        mm.then_inc(x_turned, 1)

                def head_transposes(n):
                    R, u = rows(n), n % 2
                    eng.wait_ge(roped, n + 1)
                    for b in range(4):
                        m = 4 * n + b
                        if m >= 2:
                            eng.wait_ge(turned_saved, m - 1)
                        for k in range(4 * b, min(4 * b + 4, 14)):
                            if k < 4:
                                src = ro[0:R, u, 2 * k:2 * k + 2, :]
                            elif k < 6:
                                src = ro[0:R, u, 2 * k + 2:2 * k + 4, :]
                            else:
                                a = SBQ0 + (k - 6) * P
                                src = pj[0:R, u, a:a + P]
                            if k < 6:
                                src = src.rearrange("p h d -> p (h d)")
                            mm = eng.transpose(pt[:, m % 2, (k % 4) * P:(k % 4) * P + R], src, ident[0:R, 0:R])
                        mm.then_inc(turned, 1)

                for n in range(NTILE):
                    R, u = rows(n), n % 2
                    x_transposes(n) if n == 0 else None
                    for c, (a, b) in enumerate(COLS):
                        m = 6 * n + c
                        if c == 0:
                            eng.wait_ge(x_ready, 2 * n + 2)
                        if c == 3 and n >= 1:
                            head_transposes(n - 1)
                        if c == 4 and n + 1 < NTILE:
                            x_transposes(n + 1)
                        if n == 0:
                            eng.wait_ge(w_loaded[c], 16)
                        if m >= 4:
                            eng.wait_ge(proj_saved, m - 3)
                        for k in range(KT):
                            mm = eng.matmul(pp[0:R, m % 4, 0:b - a], xT[:, u, k, 0:R], w[:, k, a:b], start=(k == 0), stop=(k == KT - 1))
                        mm.then_inc(proj_done, 1)
                head_transposes(TILES)

            @block.vector
            def _(eng):
                eng.wait_ge(c_loaded, 16 * 15)

                def norm_x(n):
                    R, u = rows(n), n % 2
                    eng.wait_ge(x_rstd, n + 1)
                    if n >= 2:
                        eng.wait_ge(x_turned, 2 * (n - 1))
                    eng.tensor_scalar(xn[0:R, u, :], x[0:R, u, :], ss[0:R, u, 1:2], None, ALU.mult).then_inc(x_normed, 1)

                def save_xT(n):
                    R, u = rows(n), n % 2
                    if n >= 2:
                        eng.wait_ge(proj_done, 6 * (n - 1))
                    for b in range(2):
                        eng.wait_ge(x_turned, 2 * n + b + 1)
                        eng.tensor_tensor(xT[:, u, 4 * b:4 * b + 4, 0:R], px[:, b, :].rearrange("p (k r) -> p k r", k=4)[:, :, 0:R],
                                          gat[:, 4 * b:4 * b + 4].to_broadcast([P, 4, R]), ALU.mult).then_inc(x_ready, 1)

                def rotate(n):
                    R, u = rows(n), n % 2
                    eng.wait_ge(qk_squared, n + 1)
                    eng.tensor_reduce(hss[0:R, u, 0:14], sq[0:R, :, :], AX.X, ALU.add).then_inc(qk_summed, 1)
                    eng.wait_ge(qk_rstd, n + 1)
                    rs = hss[0:R, u, 0:14].to_broadcast([R, 14, HD])
                    kk = pj[0:R, u, 512:1280].rearrange("p (r c j d) -> p r c j d", r=3, c=2, j=2)
                    eng.tensor_tensor(r1[0:R, 0:8, :], pj[0:R, u, 0:512].rearrange("p (h d) -> p h d", d=HD), rs[:, 0:8, :], ALU.mult)
                    for r in range(3):
                        eng.tensor_tensor(r1[0:R, 8 + 2 * r:10 + 2 * r, :], kk[:, r, 0, :, :], rs[:, 8 + 2 * r:10 + 2 * r, :], ALU.mult)
                    eng.drain()
                    eng.tensor_tensor(r1[0:R], r1[0:R], gqk[0:R], ALU.mult)
                    eng.drain()
                    cos = rot[0:R, u:u + 1, 0:32].to_broadcast([R, 14, 32])
                    sin = rot[0:R, u:u + 1, 32:64].to_broadcast([R, 14, 32])
                    for o in (0, 32):
                        eng.tensor_tensor(ra[0:R, :, o:o + 32], r1[0:R, :, o:o + 32], cos, ALU.mult)
                        eng.tensor_tensor(rb[0:R, :, o:o + 32], r1[0:R, :, 32 - o:64 - o], sin, ALU.mult)
                    if n >= 2:
                        eng.wait_ge(turned, 4 * (n - 1))
                        eng.wait_ge(kv_copied, n - 1)
                    eng.drain()
                    eng.tensor_tensor(ro[0:R, u, :, 0:32], ra[0:R, :, 0:32], rb[0:R, :, 0:32], ALU.subtract)
                    eng.tensor_tensor(ro[0:R, u, :, 32:64], ra[0:R, :, 32:64], rb[0:R, :, 32:64], ALU.add).then_inc(roped, 1)

                def save_turned(n):
                    R, u = rows(n), n % 2
                    if n >= 2:
                        eng.wait_ge(stored[u], 64 * (n // 2))
                    for b in range(4):
                        eng.wait_ge(turned, 4 * n + b + 1)
                        cnt = min(4, 14 - 4 * b)
                        for a, e, s in ([(0, 4, SCALE)], [(0, 2, 1.0), (2, 4, SCALE)], [(0, 2, SCALE), (2, 4, 1.0)], [(0, 2, 1.0)])[b]:
                            ins = eng.tensor_scalar(ts[:, u, 4 * b + a:4 * b + e, 0:R], pt[:, b % 2, :].rearrange("p (k r) -> p k r", k=4)[:, a:e, 0:R],
                                                    s, None, ALU.mult)
                        ins.then_inc(turned_saved, 1)

                norm_x(0)
                save_xT(0)
                for n in range(NTILE):
                    if n + 1 < NTILE:
                        norm_x(n + 1)
                    if n >= 1:
                        save_turned(n - 1)
                    if n + 1 < NTILE:
                        save_xT(n + 1)
                    rotate(n)
                save_turned(TILES)


def compress(nc, io, g):
    with ExitStack() as ctx:
        sb = lambda n, s, t=F32: ctx.enter_context(nc.sbuf_tensor(n, s, t))
        ps = lambda n, s, t=F32: ctx.enter_context(nc.psum_tensor(n, s, t))
        sem = lambda n: g["sem"](n)
        RING, PAIRS = 8, NPAGE // 2
        w1 = sb("w_cmp1", [P, 2, 2, 8, P])
        w2 = sb("w_cmp2", [P, 2, HD])
        pe = sb("pe_rows", [16, 2, P])
        peT = sb("pe_cols", [P, 2, 16])
        peb = sb("pe_bias", [P, 2])
        pg = g["late"][:, 0:RING * 512].rearrange("p (s r e) -> p s r e", s=RING, r=2)
        xt = sb("rows_turned", [P, 2, 4, PAST // 2])
        hid = sb("hidden", [P, 2, 2 * NCS])
        px = ps("px_c", [P, 2, 512])
        ph = ps("ph_c", [P, 2, 512])
        pk = ps("pk_c", [HD, 512])
        pv = ps("pv_c", [P, 512])
        w_loaded = sem("cmp_w_loaded")
        table_ready = sem("page_table_loaded")
        pair_loaded = [sem(f"pair_loaded{r}") for r in range(RING)]
        second_loaded = [sem(f"second_loaded{r}") for r in range(RING)]
        turned, hidden_done, gelu_done, block_done, keys_saved, values_saved = map(
            sem, ("rows_turned_s", "hidden_done", "gelu_done", "block_done", "keys_saved", "values_saved"))
        saved = [sem("turned_saved_v"), sem("turned_saved_a")]
        pe_turned, pe_saved, bias_saved = map(sem, ("pe_turned", "pe_saved", "bias_saved"))
        ident, pt, kcTp, vcp = (g[k] for k in ("ident", "pt", "kcTp", "vcp"))
        kcT = sb("kc_turned", [HD, NB * KVH, NCS])
        vc = sb("vc_rows", [P, NB * KVH, 2, HD])
        parked = sem("compressed_parked")

        def load_pages(eng, a):
            with eng.Fori(0, NB) as b:
                for q in range(PAIRS):
                    slot = (4 + q) % RING
                    if q >= 4:
                        eng.wait_ge(turned, b * PAIRS + q - 3)
                    else:
                        eng.wait_ge(turned, b * PAIRS + 1)
                    page = eng.value_load(pt[0:1, bass.ds(b * NPAGE + 2 * q + a, 1)], min_val=0, max_val=NPOOL - 1)
                    rows = io["cache_nsa"][bass.ds(page * (PAGE // 2), PAGE // 2), :, 0:256]
                    eng.dma_start(pg[64 * a:64 * a + 64, slot], rows).then_inc((pair_loaded, second_loaded)[a][slot], 16)

        with nc.Block() as block:
            @block.gpsimd
            def _(eng):
                eng.wait_ge(table_ready, 16)
                load_pages(eng, 1)

            @block.sync
            def _(eng):
                for kk, s in enumerate("kv"):
                    eng.dma_start(pe[:, kk, :], io[f"pe_cmp_{s}"][0].rearrange("(m r) d -> m (r d)", r=2)).then_inc(w_loaded, 16)
                    eng.dma_start(w1[:, kk], io[f"w_cmp1_{s}"][0].rearrange("(a j p) n -> p a j n", a=2, p=P)).then_inc(w_loaded, 16)
                    eng.dma_start(w2[:, kk], io[f"w_cmp2_{s}"][0]).then_inc(w_loaded, 16)
                eng.dma_start(pt[:, :], io["page_table"].rearrange("b (o n) -> o (b n)", o=1)).then_inc(table_ready, 16)
                for q in range(4):
                    for a in range(2):
                        rows = io["nsa_p"][(2 * q + a) * P:(2 * q + a + 1) * P, 0:256].rearrange("(p r) e -> p r e", r=2)
                        eng.dma_start(pg[64 * a:64 * a + 64, q], rows).then_inc(pair_loaded[q], 16)
                eng.wait_ge(table_ready, 16)
                load_pages(eng, 0)
                eng.wait_ge(keys_saved, NB + 1)
                eng.dma_start(io["kcT_s"], kcT[:, :, :].rearrange("p x c -> p (x c)")).then_inc(parked, 16)
                eng.wait_ge(values_saved, NB + 1)
                eng.dma_start(io["vc_s"][:, :, 0, :], vc[:, :, 0, :]).then_inc(parked, 16)
                eng.dma_start(io["vc_s"][0:P - 1, :, 1, :], vc[0:P - 1, :, 1, :]).then_inc(parked, 16)
                eng.wait_ge(parked, 48)

            def phases(eng, first, phase, last):
                first()
                phase(None, 1, 0, 0, False)
                phase(0, 0, 1, 1, None)
                with eng.Fori(0, NB // 2 - 1) as i:
                    for u in (1, 0):
                        b = i * 2 + 2 - u
                        phase(b, u, b + 1, 1 - u, b - 1)
                phase(NB - 1, 1, None, None, NB - 2)
                last(NB - 1)

            blocks_of = lambda b: NCP if b is None else NCS

            @block.tensor
            def _(eng):
                eng.wait_ge(w_loaded, 16 * 6)
                for kk in range(2):
                    mm = eng.transpose(pv[:, kk * 16:kk * 16 + 16], pe[:, kk, :], ident[0:16, 0:16])
                mm.then_inc(pe_turned, 1)
                eng.wait_ge(pe_saved, 1)
                for kk in range(2):
                    for m in range(16):
                        mm = eng.matmul(ph[:, 0, kk:kk + 1], w1[:, kk, m // 8, m % 8, :], peT[:, kk, m:m + 1], start=(m == 0), stop=(m == 15))
                mm.then_inc(hidden_done, 1)
                eng.wait_ge(bias_saved, 1)

                def turn_pair(b, q):
                    slot = q if b is None else (4 + q) % RING
                    if b is None:
                        eng.wait_ge(pair_loaded[slot], 32)
                    else:
                        k = b * 32 + 16 * ((4 + q) // RING + (0 if slot < 4 else 1))
                        eng.wait_ge(pair_loaded[slot], k + (32 if slot < 4 else 0))
                        eng.wait_ge(second_loaded[slot], k)
                    if not (b is None and q < 2):
                        eng.wait_ge(saved[q % 2], 1 if b is None else b * 8 + 2 + q // 2)
                    for v in range(4):
                        mm = eng.transpose(px[:, q % 2, v * P:(v + 1) * P], pg[:, slot, v % 2, (v // 2) * P:(v // 2 + 1) * P], ident[:, :])
                    mm.then_inc(turned, 1)

                def keys_product(b):
                    n = 2 * blocks_of(b)
                    eng.wait_ge(gelu_done, 1 if b is None else b * 2 + 3)
                    if b is not None:
                        eng.wait_ge(keys_saved, b + 1)
                    eng.matmul(pk[:, 0:n], w2[:, 0, :], hid[:, 0, 0:n], start=True, stop=True).then_inc(block_done, 1)

                def values_product(b):
                    blocks = blocks_of(b)
                    eng.wait_ge(gelu_done, 2 if b is None else b * 2 + 4)
                    if b is not None:
                        eng.wait_ge(values_saved, b + 1)
                    for v in range(2):
                        for c in range((blocks + P - 1) // P):
                            r = min(P, blocks - c * P)
                            mm = eng.matmul(pv[0:r, (2 * v + c) * HD:(2 * v + c + 1) * HD], hid[:, 1, v * blocks + c * P:v * blocks + c * P + r], w2[:, 1, :], start=True, stop=True)
                    mm.then_inc(block_done, 1)

                def phase(b, u, nb, nu, before):
                    blocks = blocks_of(b)
                    for kk in range(2):
                        for e in range(2):
                            eng.wait_ge(saved[e], 2 if b is None else b * 8 + 10)
                        if b is not None:
                            eng.wait_ge(gelu_done, b * 2 + kk + 1)
                        out = ph[:, kk, 0:2 * blocks].rearrange("p (v c) -> p v c", v=2)
                        for m in range(16):
                            half, j = m // 8, m % 8
                            src = xt[:, u, 2 * kk:2 * kk + 2, :].rearrange("p v (c j) -> p v c j", j=8)[:, :, half:half + blocks, j]
                            mm = eng.matmul(out, w1[:, kk, half, j, :], src, start=(m == 0), stop=(m == 15))
                            if m == 15:
                                mm.then_inc(hidden_done, 1)
                            if m % 2 == 1 and nb is not None:
                                turn_pair(nb, 8 * kk + m // 2)
                            if (kk, m) == (0, 3) and before is not False:
                                values_product(before)
                            if (kk, m) == (1, 7):
                                keys_product(b)

                def first():
                    for q in range(4):
                        turn_pair(None, q)
                phases(eng, first, phase, values_product)

            def save_pair(eng, b, u, q):
                eng.wait_ge(turned, (q if b is None else b * PAIRS + 4 + q) + 1)
                if q < 2 and b is not None:
                    eng.wait_ge(hidden_done, b * 2 + 1)
                for r in range(2):
                    for j in range(2):
                        out = xt[64 * r:64 * r + 64, u, j:4:2, q * P:(q + 1) * P]
                        src = px[64 * j:64 * j + 64, q % 2, :].rearrange("p (k r c) -> p k r c", k=2, r=2)[:, :, r, :]
                        ins = eng.tensor_copy(out, src) if q % 2 == 0 else eng.activation(out, src, ACT.Copy)
                ins.then_inc(saved[q % 2], 1)

            @block.vector
            def _(eng):
                eng.memset(vcp[:, :, HD:HD + 1], 1.0)
                eng.wait_ge(pe_turned, 1)
                eng.tensor_copy(peT[:, :, :], pv[:, 0:32].rearrange("p (k m) -> p k m", k=2)).then_inc(pe_saved, 1)
                eng.wait_ge(hidden_done, 1)
                eng.tensor_copy(peb[:, :], ph[:, 0, 0:2]).then_inc(bias_saved, 1)

                def save_keys(b):
                    eng.wait_ge(block_done, 1 if b is None else b * 2 + 3)
                    keys = pk[:, 0:2 * blocks_of(b)].rearrange("p (v c) -> p v c", v=2)
                    eng.tensor_copy(kcTp[:, :, :] if b is None else kcT[:, bass.ds(b * 2, 2), :], keys).then_inc(keys_saved, 1)

                def save_values(b):
                    eng.wait_ge(block_done, 2 if b is None else b * 2 + 4)
                    if b is None:
                        src = pv[0:NCP, 0:256].rearrange("p (v c d) -> p v c d", v=2, c=2)[:, :, 0, :]
                        eng.tensor_copy(vcp[0:NCP, :, 0:HD], src).then_inc(values_saved, 1)
                    else:
                        vals = pv[:, 0:256].rearrange("p (v c d) -> p v c d", v=2, c=2)
                        eng.tensor_copy(vc[:, bass.ds(b * 2, 2), 0, :], vals[:, :, 0, :])
                        eng.tensor_copy(vc[0:P - 1, bass.ds(b * 2, 2), 1, :], vals[0:P - 1, :, 1, :]).then_inc(values_saved, 1)

                def phase(b, u, nb, nu, before):
                    for q in range(0, PAIRS, 2):
                        if nb is not None:
                            save_pair(eng, nb, nu, q)
                        if q == 0 and before is not False:
                            save_values(before)
                        if q == 10:
                            save_keys(b)

                def first():
                    for q in (0, 2):
                        save_pair(eng, None, 1, q)
                phases(eng, first, phase, save_values)

            @block.scalar
            def _(eng):
                eng.wait_ge(bias_saved, 1)

                def phase(b, u, nb, nu, before):
                    for q in range(1, PAIRS, 2):
                        if nb is not None:
                            save_pair(eng, nb, nu, q)
                        if q in (7, 15):
                            kk, n = q // 8, 2 * blocks_of(b)
                            eng.wait_ge(hidden_done, 2 + kk if b is None else b * 2 + 4 + kk)
                            if b is not None:
                                eng.wait_ge(block_done, b * 2 + 1 + kk)
                            eng.activation(hid[:, kk, 0:n], ph[:, kk, 0:n], ACT.Gelu_apprx_tanh, bias=peb[:, kk:kk + 1]).then_inc(gelu_done, 1)

                def first():
                    for q in (1, 3):
                        save_pair(eng, None, 1, q)
                phases(eng, first, phase, lambda b: None)


def attend(nc, io, g):
    with ExitStack() as ctx:
        sb = lambda n, s, t=F32: ctx.enter_context(nc.sbuf_tensor(n, s, t))
        ps = lambda n, s, t=F32: ctx.enter_context(nc.psum_tensor(n, s, t))
        sem = g["sem"]
        RING, NPR = 8, 4
        kT = sb("kT_sel_win", [HD, 2, KVH, SEQ])
        vx = sb("v_sel_win", [P, 2, TILES, KVH, HD + 1])
        qn = sb("q_nsa", [HD, 2, SEQ])
        qs = sb("q_sb", [HD, 2, SEQ])
        ks = sb("k_sb", [HD, 2, SEQ])
        vs = sb("v_sb", [P, 2, TILES, HD])
        masksf = sb("masks_f", [P, 3, P])
        cmaskf = sb("cmask_f", [P, TILES, 64])
        masks = sb("masks_b", [P, 3, P], BF16)
        cmask = sb("cmask_b", [P, TILES, 64], BF16)
        identb = sb("ident_b", [P, P], BF16)
        rowok = sb("rowok", [P, 1])
        nm = sb("minus_max", [P, 64])
        pr = sb("probs", [P, 2, SEQ])
        prs = sb("stick_weights", [P, SEQ])
        prT = sb("probs_turned", [P, 2, TILES, P])
        zs = sb("stick_logits", [P, SEQ])
        lg = sb("log_part", [P, SEQ])
        rl = sb("relu_part", [P, SEQ])
        dd = sb("log_weight", [P, SEQ])
        fac = sb("factor", [P, 64, 2])
        S = ps("scores", [P, 2, 1024])
        PT = ps("turned_ps", [P, 2, 512])
        O = ps("out_ps", [P, 512])
        DB = ps("decode_ps", [P, 512])

        late = g["late"]
        kr = late[:, 0:4096].rearrange("p (r n) -> p r n", r=RING)
        vr = late[:, 4096:8192].rearrange("p (r n) -> p r n", r=RING)
        prod = late[:, 8192:10240].rearrange("p (r n) -> p r n", r=NPR)
        qb = late[:, 10240:11264].rearrange("p (r n) -> p r n", r=2)
        zd = sb("z_dec", [P, 2, NH, NPAGE])
        lgd = sb("log_dec", [P, NH * NPAGE])
        rld = sb("relu_dec", [P, NH * NPAGE])
        later = sb("later_pages", [P, NH * NPAGE])
        keep = sb("keep", [P, NH, NPAGE])
        ddd = sb("logw_dec", [P, NH * NPAGE])
        aw = sb("weights_dec", [P, NH, NPAGE])
        tri = sb("tri", [P, P])
        ones = sb("ones_dec", [P, P])
        diag = sb("diag", [NH, 512])
        om = sb("o_masked", [NH, 512])
        orow = sb("o_row", [1, 512])
        const_loaded, consts_set, pool_steps = sem("const_loaded"), sem("consts_set"), sem("pool_steps")
        head_loaded = [sem("head_loaded0"), sem("head_loaded1")]
        names = ("qk_done", "max_done_a", "z_copied", "log_done", "relu_done", "scan_done", "logw_ready", "exp_done", "stick_done",
                 "turned_a", "pv_done", "out_done", "steps_a")
        qk_done, max_done, z_copied, log_done, relu_done, scan_done, logw_ready, exp_done, stick_done, turned, pv_done, out_done, steps = map(sem, names)
        saved = [sem("p_saved_v"), sem("p_saved_a")]
        k_loaded = [sem(f"k_loaded{r}") for r in range(RING)]
        v_loaded = [sem(f"v_loaded{r}") for r in range(RING)]
        q_loaded = [sem("q_loaded0"), sem("q_loaded1")]
        names = ("multiplied", "reduced", "logged", "softplus_done", "cum_done", "logw_done", "weights_done",
                 "v_used", "o_masked_s", "o_row_done", "o_row_saved", "row_stored")
        multiplied, reduced, logged, sp_done, cum_done, logw_done, weights_done, v_used, masked, row_done, row_saved, row_stored = map(sem, names)
        ident, gates, mix, kcTp, vcp, pt = (g[k] for k in ("ident", "gates", "mix", "kcTp", "vcp", "pt"))

        FRONT = []
        for u in range(2):
            for t in range(TILES):
                for kind in ("sb", "cmp", "sel", "win"):
                    lo = max(0, t - 4) if kind == "win" else 0
                    FRONT.append((u, t, kind, lo, 1 if kind == "cmp" else t + 1 - lo))
        U = len(FRONT)
        H = U // 2
        front_of = lambda m: m + 1 if m % 4 < 3 else m - 3
        back_of = lambda f: f - 1 if f % 4 else f + 3
        BACK = [FRONT[front_of(m)] for m in range(U)]
        G0 = [0]
        for x in BACK:
            G0.append(G0[-1] + (x[4] + 3) // 4)
        G = G0[-1]
        assert G % 2 == 0
        soft = lambda f: f - (f // 4 + 1)
        NSOFT, NSTICK = U * 3 // 4, U // 4
        width = lambda x: NCP if x[2] == "cmp" else x[4] * P

        def spread(counts):
            ends = [sum(counts[:s // 4]) + -(-counts[s // 4] * (s % 4 + 1) // 4) for s in range(H)]
            return [list(range(([0] + ends)[s], ends[s])) for s in range(H)]
        KPAGES, VPAGES = spread((2, 2, 3, 4, 5, 5, 5, 6)), spread((0, 3, 3, 4, 5, 5, 6, 6))
        zero = lambda N: isinstance(N, int) and N == 0

        def turns(eng, body, tail):
            body(0, 0)
            with eng.Fori(1, 3) as i:
                body(i, i - 1)
            body(3, 1)
            for s in range(H):
                tail(s)

        with nc.Block() as block:
            @block.sync
            def _(eng):
                Tr = io["T"].rearrange("(h d) t -> d h t", d=HD)
                Th = io["T3"]

                def load_head(h, u):
                    for dst, t in ((qs, T_QS), (ks, T_KB), (qn, T_QN)):
                        eng.dma_start(dst[:, u], Th[bass.ds(h + t, 1)].rearrange("o d t -> d (o t)")).then_inc(head_loaded[u], 16)
                    v = io["sb_p"].rearrange("(t p) (c h d) -> c p t h d", p=P, c=2, h=NH)[1][:, :, bass.ds(h, 1), :]
                    eng.dma_start(vs[:, u], v.rearrange("p t o d -> p t (o d)")).then_inc(head_loaded[u], 16)

                eng.dma_start(masksf[:, :, :], io["c_masks"]).then_inc(const_loaded, 16)
                eng.dma_start(cmaskf[:, :, :], io["c_cmask"]).then_inc(const_loaded, 16)
                eng.dma_start(rowok[:, :], io["c_rowok"]).then_inc(const_loaded, 16)
                load_head(0, 0)
                eng.dma_start(kT[:, 0], Tr[:, T_KS:T_KS + 2, :]).then_inc(const_loaded, 16)
                eng.dma_start(kT[:, 1], Tr[:, T_KW:T_KW + 2, :]).then_inc(const_loaded, 16)
                for j in range(2):
                    eng.dma_start(vx[:, 0, :, j, 0:HD], io["nsa_p"].rearrange("(t p) e -> p t e", p=P)[:, :, 384 + j * HD:448 + j * HD]).then_inc(const_loaded, 16)
                    eng.dma_start(vx[:, 1, :, j, 0:HD], io["win_p"].rearrange("(t p) e -> p t e", p=P)[:, :, 128 + j * HD:192 + j * HD]).then_inc(const_loaded, 16)
                eng.dma_start(tri[:, :], io["c_tri"]).then_inc(const_loaded, 16)
                eng.dma_start(diag[:, :], io["c_diag"].rearrange("a h d -> a (h d)")).then_inc(const_loaded, 16)
                load_head(1, 1)
                eng.dma_start(io["win_p_out"], io["win_p"][SEQ - WINDOW:SEQ, :]).then_inc(row_stored, 16)

                def key_page(h, u, p):
                    if p == 0:
                        if not zero(h // 2 if isinstance(h, int) else h):
                            eng.wait_ge(reduced, h * NPAGE - NPAGE)
                        eng.dma_start(qb[:, u], io["sbq_s"][bass.ds(h, 1), :].rearrange("o n -> (o n)").partition_broadcast(P)).then_inc(q_loaded[u], 16)
                    if not (zero(h) and p < RING):
                        eng.wait_ge(multiplied, h * NPAGE + p - RING + 1)
                    page = eng.value_load(pt[0:1, bass.ds(h * NPAGE + p, 1)], min_val=0, max_val=NPOOL - 1)
                    eng.dma_start(kr[:, p % RING], io["cache_sb"][bass.ds(page * P, P), 0, :]).then_inc(k_loaded[p % RING], 16)

                def value_page(b, p):
                    if not (zero(b) and p < RING):
                        eng.wait_ge(v_used, b * NPAGE + p - RING + 1)
                    page = eng.value_load(pt[0:1, bass.ds(b * NPAGE + p, 1)], min_val=0, max_val=NPOOL - 1)
                    eng.dma_start(vr[:, p % RING], io["cache_sb"][bass.ds(page * P, P), 1, :]).then_inc(v_loaded[p % RING], 16)

                def store_row(b):
                    eng.wait_ge(row_saved, b + 1)
                    eng.dma_start(io["osb_s"][bass.ds(b, 1), :], orow[:, :]).then_inc(row_stored, 16)

                def body(N, kv):
                    for u in range(2):
                        h = N * 2 + u
                        for p in range(NPAGE):
                            key_page(h, u, p)
                            if not zero(h):
                                value_page(h - 1, p)
                            if p == 5 and not zero(N):
                                store_row(h - 2)
                            if p == 6 and not zero(h) and not (isinstance(h, int) and h == NH - 1):
                                eng.wait_ge(pv_done, h * H)
                                load_head(h + 1, 1 - u)

                def tail(s):
                    value_page(NH - 1, s)
                    if s == 5:
                        store_row(NH - 2)

                turns(eng, body, tail)
                store_row(NH - 1)
                eng.wait_ge(row_stored, 16 * (NH + 1))

            @block.gpsimd
            def _(eng):
                def multiply(h, u, p):
                    if p == 0:
                        eng.wait_ge(q_loaded[u], (h - u) * 8 + 16)
                    eng.wait_ge(k_loaded[p % RING], h * 64 + 16 * (p // RING) + 16)
                    if not (zero(h) and p < NPR):
                        eng.wait_ge(reduced, h * NPAGE + p - NPR + 1)
                    eng.tensor_tensor(prod[:, p % NPR], kr[:, p % RING], qb[:, u], ALU.mult).then_inc(multiplied, 1)

                def body(N, kv):
                    for s in range(U):
                        for p in KPAGES[s % H]:
                            multiply(N * 2 + s // H, s // H, p)
                        w, k = width(FRONT[s - s % 4]), N * NSTICK + s // 4
                        if s % 4 == 1:
                            eng.wait_ge(z_copied, k + 1)
                            if not (zero(N) and s < 4):
                                eng.wait_ge(scan_done, k)
                            eng.sem_inc(pool_steps, 1)
                            eng.tensor_scalar(rl[:, 0:w], zs[:, 0:w], 0.0, None, ALU.max).then_inc(relu_done, 1)
                        if s % 4 == 3:
                            eng.wait_ge(scan_done, k + 1)
                            eng.tensor_tensor(dd[:, 0:w], zs[:, 0:w], dd[:, 0:w], ALU.subtract).then_inc(logw_ready, 1)
                turns(eng, body, lambda s: None)

            @block.tensor
            def _(eng):
                eng.wait_ge(const_loaded, 16 * 11)
                eng.wait_ge(consts_set, 1)

                def scores(N, kv, s):
                    u, t, kind, lo, tiles = FRONT[s]
                    if s % H == 0:
                        eng.wait_ge(head_loaded[u], N * 64 + 64)
                    if not (zero(N) and s < 2):
                        f = s - 2
                        if f % 4 == 0:
                            eng.wait_ge(z_copied, N * NSTICK + f // 4 + 1)
                        else:
                            eng.wait_ge(exp_done, N * NSOFT + soft(f) + 1)
                    q = (qs if kind == "sb" else qn)[:, u, t * P:(t + 1) * P]
                    if kind == "cmp":
                        kc = kcTp[:, bass.ds(kv, 1), :].rearrange("p o c -> p (o c)")
                        eng.matmul(S[:, s % 2, 0:NCP], q, kc, start=True, stop=False)
                        eng.matmul(S[:, s % 2, 0:NCP], identb[:, :], cmask[:, t, 0:NCP], start=False, stop=True).then_inc(qk_done, 1)
                        return
                    w = tiles * P
                    edges = [((tiles - 1) * P, 1 if kind == "sb" else 0)]
                    if kind == "win" and t >= 4:
                        edges.append((0, 2))
                    for a in range(0, w, 512):
                        e = min(w, a + 512)
                        if kind == "sb":
                            k = ks[:, u, a:e]
                        else:
                            k = kT[:, 0 if kind == "sel" else 1, bass.ds(kv, 1), lo * P + a:lo * P + e].rearrange("p o c -> p (o c)")
                        own = [x for x in edges if a <= x[0] < e]
                        mm = eng.matmul(S[:, s % 2, a:e], q, k, start=True, stop=not own)
                        for z, (at, m) in enumerate(own):
                            mm = eng.matmul(S[:, s % 2, at:at + P], identb[:, :], masks[:, m, :], start=False, stop=z == len(own) - 1)
                    mm.then_inc(qk_done, 1)

                def transposes(N, m):
                    u, t, kind, lo, tiles = BACK[m % U]
                    f = front_of(m)
                    src = prs if kind == "sb" else pr[:, f % 2]
                    if kind == "sb":
                        eng.wait_ge(stick_done, N * NSTICK + m // 4 + 1)
                    else:
                        eng.wait_ge(exp_done, N * NSOFT + soft(f) + 1)
                    base, first = (m // U) * G, G0[m % U]
                    for b in range(first, G0[m % U + 1]):
                        if not (zero(N) and b < 2 and m >= 0):
                            eng.wait_ge(saved[b % 2], N * (G // 2) + (base + b) // 2)
                        if kind == "cmp":
                            eng.sem_inc(steps, 1)
                        for c in range(4 * (b - first), min(tiles, 4 * (b - first) + 4)):
                            w = min(P, width(BACK[m % U]) - c * P)
                            mm = eng.transpose(PT[0:w, b % 2, (c % 4) * P:(c % 4 + 1) * P], src[:, c * P:c * P + w], ident[:, :])
                        mm.then_inc(turned, 1)

                def product(N, kv, m):
                    u, t, kind, lo, tiles = BACK[m % U]
                    base = (m // U) * G
                    for b in range(G0[m % U], G0[m % U + 1]):
                        eng.wait_ge(saved[b % 2], N * (G // 2) + (base + b) // 2 + 1)
                    if not (zero(N) and m == 0):
                        eng.wait_ge(out_done, N * U + m)
                    for c in range(tiles):
                        if kind == "cmp":
                            l, r = prT[0:NCP, m % 2, 0, :], vcp[0:NCP, bass.ds(kv, 1), :].rearrange("p o d -> p (o d)")
                        elif kind == "sb":
                            l, r = prT[:, m % 2, c, :], vs[:, u, c, :]
                        else:
                            l, r = prT[:, m % 2, c, :], vx[:, 0 if kind == "sel" else 1, lo + c, bass.ds(kv, 1), :].rearrange("p o d -> p (o d)")
                        mm = eng.matmul(O[:, 0:HD if kind == "sb" else HD + 1], l, r, start=c == 0, stop=c == tiles - 1)
                    mm.then_inc(pv_done, 1)

                def sample(h, s):
                    if s == 1 and not zero(h) and not (isinstance(h, int) and h < 2):
                        eng.wait_ge(masked, h - 1)
                        eng.sem_inc(steps, 1)
                        eng.matmul(DB[0:1, :], ones[0:NH, 0:1], om[:, :], start=True, stop=True).then_inc(row_done, 1)
                    if s == 2 and not zero(h) and not (isinstance(h, int) and h > NH):
                        eng.wait_ge(sp_done, h)
                        if not (isinstance(h, int) and h < 2):
                            eng.wait_ge(row_saved, h - 1)
                        eng.matmul(DB[:, 0:NH * NPAGE], tri[:, :], rld[:, :], start=True, stop=False)
                        eng.matmul(DB[:, 0:NH * NPAGE], ones[:, :], later[:, :], start=False, stop=True).then_inc(cum_done, 1)
                    if not zero(h) and not (isinstance(h, int) and h > NH):
                        for p in VPAGES[s]:
                            if p == 0:
                                eng.wait_ge(weights_done, h)
                            eng.wait_ge(v_loaded[p % RING], h * 64 - 64 + 16 * (p // RING) + 16)
                            eng.matmul(DB[0:NH, :], aw[:, :, NPAGE - 1 - p], vr[:, p % RING], start=p == 0, stop=p == NPAGE - 1).then_inc(v_used, 1)

                def body(N, kv):
                    for s in range(U):
                        scores(N, kv, s)
                        kvb = lambda m: kv if m >= 0 else (1 if isinstance(N, int) else 0)
                        if not (zero(N) and s < 2):
                            transposes(N, s - 2)
                        if not (zero(N) and s < 3):
                            product(N, kvb(s - 3), s - 3)
                        sample(N * 2 + s // H, s % H)

                def tail(s):
                    if s < 2:
                        transposes(4, s - 2)
                    if s < 3:
                        product(4, 1, s - 3)
                    sample(NH, s)
                turns(eng, body, tail)
                sample(NH + 1, 1)

            def save_groups(eng, N, m, e):
                tiles = BACK[m % U][4]
                base, first = (m // U) * G, G0[m % U]
                for b in range(first, G0[m % U + 1]):
                    if b % 2 != e:
                        continue
                    eng.wait_ge(turned, N * G + base + b + 1)
                    if not (zero(N) and m in (0, 1)):
                        eng.wait_ge(pv_done, N * U + m - 1)
                    c = 4 * (b - first)
                    k, w = min(4, tiles - c), min(P, width(BACK[m % U]))
                    out = prT[0:w, m % 2, c:c + k, :]
                    src = PT[0:w, b % 2, 0:k * P].rearrange("p (c q) -> p c q", q=P)
                    if e == 0:
                        eng.tensor_copy(out, src).then_inc(saved[0], 1)
                    else:
                        eng.activation(out, src, ACT.Copy).then_inc(saved[1], 1)

            @block.scalar
            def _(eng):
                eng.preload_act_table_set("natural_log_exp_and_others")

                def exps(N, s):
                    x, w = FRONT[s], width(FRONT[s])
                    if x[2] == "sb":
                        return
                    eng.wait_ge(max_done, N * NSOFT + soft(s) + 1)
                    if not (zero(N) and s < 3):
                        m = back_of(s - 2) if (s - 2) % 4 else back_of(s - 3)
                        eng.wait_ge(turned, N * G + (m // U) * G + G0[m % U + 1])
                    eng.activation(pr[:, s % 2, 0:w], S[:, s % 2, 0:w], ACT.Exp, bias=nm[:, s:s + 1]).then_inc(exp_done, 1)

                def stick(N, s):
                    w, k = width(FRONT[s - s % 4]), N * NSTICK + s // 4
                    if s % 4 == 0:
                        eng.wait_ge(z_copied, k + 1)
                        if not (zero(N) and s < 4):
                            eng.wait_ge(scan_done, k)
                        eng.activation(lg[:, 0:w], zs[:, 0:w], ACT.Abs)
                    elif s % 4 == 1:
                        eng.drain()
                        eng.activation(lg[:, 0:w], lg[:, 0:w], ACT.Exp, scale=-1.0)
                    elif s % 4 == 2:
                        eng.drain()
                        eng.activation(lg[:, 0:w], lg[:, 0:w], ACT.Ln, bias=1.0).then_inc(log_done, 1)
                    else:
                        eng.wait_ge(logw_ready, k + 1)
                        if not (zero(N) and s < 4):
                            m = back_of(s - 7)
                            eng.wait_ge(turned, N * G + (m // U) * G + G0[m % U + 1])
                        eng.activation(prs[:, 0:w], dd[:, 0:w], ACT.Exp).then_inc(stick_done, 1)

                def sample(h, u, s):
                    if s == 0 and not zero(h) and not (isinstance(h, int) and h > NH):
                        eng.wait_ge(reduced, h * NPAGE)
                        z = zd[:, 1 - u, :, :].rearrange("p h n -> p (h n)")
                        eng.activation(lgd[:, :], z, ACT.Abs)
                        eng.drain()
                        eng.activation(lgd[:, :], lgd[:, :], ACT.Exp, scale=-1.0)
                        eng.drain()
                        eng.activation(lgd[:, :], lgd[:, :], ACT.Ln, bias=1.0).then_inc(logged, 1)
                    if s == 2 and not (isinstance(h, int) and h < 2):
                        eng.wait_ge(row_done, h - 1)
                        eng.wait_ge(row_stored, h * 16 - 16)
                        eng.activation(orow[:, :], DB[0:1, :], ACT.Copy).then_inc(row_saved, 1)
                    if s == 3 and not zero(h) and not (isinstance(h, int) and h > NH):
                        eng.wait_ge(logw_done, h)
                        if not (isinstance(h, int) and h < 2):
                            eng.wait_ge(v_used, h * NPAGE - NPAGE)
                        eng.activation(aw[:, :, :].rearrange("p h n -> p (h n)"), ddd[:, :], ACT.Exp).then_inc(weights_done, 1)

                def body(N, kv):
                    for s in range(U):
                        exps(N, s)
                        if not (zero(N) and s < 2):
                            save_groups(eng, N, s - 2, 1)
                        stick(N, s)
                        sample(N * 2 + s // H, s // H, s % H)

                def tail(s):
                    if s < 2:
                        save_groups(eng, 4, s - 2, 1)
                    sample(NH, 0, s)
                turns(eng, body, tail)
                sample(NH + 1, 1, 2)

            @block.vector
            def _(eng):
                eng.memset(ones[:, :], 1.0)
                eng.memset(keep[:, :, 1:NPAGE], 1.0)
                eng.memset(keep[:, :, 0:1], 0.0)
                eng.wait_ge(const_loaded, 16 * 11)
                eng.memset(vx[:, :, :, :, HD:HD + 1], 1.0)
                eng.tensor_copy(identb[:, :], ident[:, :])
                eng.tensor_copy(masks[:, :, :], masksf[:, :, :])
                eng.tensor_copy(cmask[:, :, :], cmaskf[:, :, :]).then_inc(consts_set, 1)

                def stat(N, s):
                    x, w = FRONT[s], width(FRONT[s])
                    z = S[:, s % 2, 0:w]
                    eng.wait_ge(qk_done, N * U + s + 1)
                    if x[2] != "sb":
                        eng.tensor_reduce(nm[:, s:s + 1], z, AX.X, ALU.max, negate=True).then_inc(max_done, 1)
                        return
                    if not (zero(N) and s < 4):
                        eng.wait_ge(logw_ready, N * NSTICK + s // 4)
                    eng.tensor_copy(zs[:, 0:w], z).then_inc(z_copied, 1)

                def scan(N, s):
                    w, k = width(FRONT[s - s % 4]), N * NSTICK + s // 4
                    rev = lambda a: a[:, w - 1::-1]
                    eng.wait_ge(log_done, k + 1)
                    eng.wait_ge(relu_done, k + 1)
                    if not (zero(N) and s < 4):
                        eng.wait_ge(stick_done, k)
                    eng.tensor_tensor_scan(rev(dd), rev(lg), rev(rl), 0.0, ALU.add, ALU.add).then_inc(scan_done, 1)

                def out(N, m):
                    u, t, kind, lo, tiles = BACK[m % U]
                    o, h = O[:, 0:HD], N * 2 + (u if m >= 0 else u - 2)
                    eng.wait_ge(pv_done, N * U + m + 1)
                    if kind == "sb":
                        eng.tensor_copy(mix[:, t, bass.ds(h * HD + 512, HD)], o).then_inc(out_done, 1)
                        return
                    br = ("cmp", "sel", "win").index(kind)
                    f, f2 = fac[:, m % U, 0:1], fac[:, m % U, 1:2]
                    eng.reciprocal(f, O[:, HD:HD + 1])
                    eng.drain()
                    eng.tensor_tensor(f2, f, gates[:, t, bass.ds(h * 3 + br, 1)], ALU.mult)
                    eng.drain()
                    if kind == "cmp" and t == 0:
                        eng.tensor_tensor(f2, f2, rowok[:, :], ALU.mult)
                        eng.drain()
                    mx = mix[:, t, bass.ds(h * HD, HD)]
                    if kind == "cmp":
                        eng.tensor_scalar(mx, o, f2, None, ALU.mult).then_inc(out_done, 1)
                    else:
                        eng.scalar_tensor_tensor(mx, o, f2, mx, ALU.mult, ALU.add).then_inc(out_done, 1)

                def sample(h, u, s, keys):
                    live = not zero(h) and not (isinstance(h, int) and h > NH)
                    z = zd[:, 1 - u, :, :].rearrange("p h n -> p (h n)")
                    if s == 0 and not (isinstance(h, int) and h < 2):
                        eng.wait_ge(v_used, h * NPAGE - NPAGE)
                        eng.tensor_tensor(om[:, :], DB[0:NH, :], diag[:, :], ALU.mult).then_inc(masked, 1)
                    if s == 1 and live:
                        if not (isinstance(h, int) and h < 2):
                            eng.wait_ge(cum_done, h - 1)
                        eng.tensor_scalar(rld[:, :], z, 0.0, None, ALU.max)
                        eng.drain()
                        eng.wait_ge(logged, h)
                        eng.tensor_tensor(rld[:, :], rld[:, :], lgd[:, :], ALU.add)
                        eng.drain()
                        eng.tensor_tensor_scan(later[:, :], keep[:, :, :].rearrange("p h n -> p (h n)"), rld[:, :], 0.0, ALU.mult, ALU.add)
                        eng.drain()
                        eng.tensor_tensor(later[:, :], later[:, :], rld[:, :], ALU.subtract).then_inc(sp_done, 1)
                    if s == 2 and live:
                        if not (isinstance(h, int) and h < 2):
                            eng.wait_ge(weights_done, h - 1)
                        eng.wait_ge(cum_done, h)
                        eng.tensor_tensor(ddd[:, :], z, DB[:, 0:NH * NPAGE], ALU.subtract).then_inc(logw_done, 1)
                    for p in KPAGES[s] if keys else []:
                        eng.wait_ge(multiplied, h * NPAGE + p + 1)
                        eng.tensor_reduce(zd[:, u, :, NPAGE - 1 - p], prod[:, p % NPR].rearrange("p (h d) -> p h d", h=NH), AX.X, ALU.add).then_inc(reduced, 1)

                def body(N, kv):
                    for s in range(U):
                        stat(N, s)
                        if not (zero(N) and s < 2):
                            save_groups(eng, N, s - 2, 0)
                        if s % 4 == 2:
                            scan(N, s)
                        if not (zero(N) and s < 3):
                            out(N, s - 3)
                        sample(N * 2 + s // H, s // H, s % H, True)

                def tail(s):
                    if s < 2:
                        save_groups(eng, 4, s - 2, 0)
                    if s < 3:
                        out(4, s - 3)
                    sample(NH, 0, s, False)
                turns(eng, body, tail)
                sample(NH + 1, 1, 0, False)


def decode_nsa(nc, io, g):
    with ExitStack() as ctx:
        sb = lambda n, s, t=F32: ctx.enter_context(nc.sbuf_tensor(n, s, t))
        sem = lambda n: g["sem"](n)
        X = NB * KVH
        ident, pt = g["ident"], g["pt"]
        kcT = sb("kc_turned_d", [HD, X, NCS])
        vc = sb("vc_rows_d", [P, X, 2, HD])
        qT = sb("q_dec", [HD, NH, NB])
        oC = sb("o_cmp_dec", [GRP, X, HD])
        oS = sb("o_sel_dec", [GRP, X, HD])
        oW = sb("o_win_dec", [GRP, X, HD])
        block_id = sb("block_id", [1, X * 16], I32)
        with ExitStack() as c2:
            sb2 = lambda n, s, t=F32: c2.enter_context(nc.sbuf_tensor(n, s, t))
            ps2 = lambda n, s: c2.enter_context(nc.psum_tensor(n, s, F32))
            sc = sb2("sc_dec", [GRP, X, NCS])
            st = sb2("st_dec", [GRP, 4, X])
            pT = sb2("p_turned", [P, X * 2, GRP])
            pS = sb2("p_summed", [P, X * 2])
            pB = sb2("p_bcast", [P, X * 2, NBLK])
            ovl = sb2("overlap", [P, 2, NBLK])
            selc = sb2("sel_consts", [NBLK, 3, NBLK])
            ranks = sb2("ranks", [NBLK, 16])
            blk = sb2("blk", [NBLK, 2])
            pageof = sb2("pageof", [NPAGE, NBLK])
            pti = sb2("pt_int", [NPAGE, NB], I32)
            ptf = sb2("pt_float", [NPAGE, NB])
            ones = sb2("ones_sel", [NBLK, 2])
            R = sb2("score_rows", [NBLK, X, NBLK])
            Q1 = sb2("sel_tmp1", [NBLK, X, NBLK])
            Q2 = sb2("sel_tmp2", [NBLK, X, NBLK])
            col = sb2("score_col", [NBLK, X])
            rank = sb2("rank", [NBLK, X])
            base = sb2("block_addr", [NBLK, NB])
            OH = sb2("one_hot", [NBLK, X, 16])
            S4 = ps2("S4", [GRP, 4, 512])
            PA = ps2("PA", [P, 512])
            PB = ps2("PB", [P, 512])
            PR = ps2("PR", [NBLK, 2, 512])
            c_loaded, scored, copied, shifted, exped, probs, turned, turned_saved, summed, rows_done, bases_done, oh_done, ids_done, pt_set = map(
                lambda n: g["sem"](n),
                ("cd_loaded", "scored", "copied", "shifted", "exped", "probs", "p_turned_s", "p_turned_saved", "p_summed_s",
                 "rows_done", "bases_done", "oh_done", "ids_done", "pt_set"))
            with nc.Block() as block:
                @block.sync
                def _(eng):
                    for dst, src in ((kcT[:, :, :].rearrange("p x c -> p (x c)"), io["kcT_s"]), (vc[:, :, 0, :], io["vc_s"][:, :, 0, :]),
                                     (vc[0:P - 1, :, 1, :], io["vc_s"][0:P - 1, :, 1, :]),
                                     (qT[:, :, :], io["Ts"].rearrange("(h d) b -> d h b", d=HD)[:, 0:NH, :]), (ovl[:, :, :], io["c_ov"]),
                                     (selc[:, :, :], io["c_sel"]), (ranks[:, :], io["c_ranks"]), (blk[:, :], io["c_blk"]),
                                     (pageof[:, :], io["c_pageof"]), (pti[:, :], io["page_table"].rearrange("b n -> n b"))):
                        eng.dma_start(dst, src, allow_slow_non_contiguous=True).then_inc(c_loaded, 16)

                @block.tensor
                def _(eng):
                    eng.wait_ge(c_loaded, 16 * 10)
                    for x in range(X):
                        b, j = x // 2, x % 2
                        if x == 8:
                            eng.wait_ge(copied, 1)
                        mm = eng.matmul(S4[:, x // 2 % 4, j * NCS:(j + 1) * NCS], qT[:, GRP * j:GRP * j + GRP, b], kcT[:, x, :], start=True, stop=True)
                        if x % 8 == 7:
                            mm.then_inc(scored, 1)
                    eng.wait_ge(pt_set, 1)
                    eng.matmul(PB[0:NBLK, 0:NB], pageof[:, :], ptf[:, :], start=True, stop=True).then_inc(bases_done, 1)
                    eng.wait_ge(probs, 1)
                    for x in range(X):
                        for c in range(2):
                            w = P - c
                            mm = eng.transpose(PA[0:w, (2 * x + c) * GRP:(2 * x + c + 1) * GRP], sc[:, x, c * P:c * P + w], ident[0:GRP, 0:GRP])
                    mm.then_inc(turned, 1)
                    eng.wait_ge(turned_saved, 1)
                    for x in range(X):
                        for c in range(2):
                            w = P - c
                            mm = eng.matmul(S4[:, x // 8, x % 8 * HD:(x % 8 + 1) * HD], pT[0:w, 2 * x + c, :], vc[0:w, x, c, :], start=c == 0, stop=c == 1)
                    mm.then_inc(scored, 1)
                    eng.wait_ge(summed, 1)
                    for x in range(X):
                        for c in range(2):
                            w = P - c
                            mm = eng.matmul(PR[:, x // 8, x % 8 * HD:(x % 8 + 1) * HD], pB[0:w, 2 * x + c, :], ovl[0:w, c, :], start=c == 0, stop=c == 1)
                    mm.then_inc(rows_done, 1)
                    eng.wait_ge(oh_done, 1)
                    eng.matmul(PB[0:1, 0:X * 16], ones[:, 0:1], OH[:, :, :].rearrange("p x r -> p (x r)"), start=True, stop=True).then_inc(ids_done, 1)

                @block.scalar
                def _(eng):
                    eng.wait_ge(shifted, 1)
                    scf = sc[:, :, :].rearrange("p x c -> p (x c)")
                    eng.activation(scf, scf, ACT.Exp).then_inc(exped, 1)

                @block.vector
                def _(eng):
                    eng.memset(ones[:, :], 1.0)
                    eng.memset(pT[96:P, :, :], 0.0)
                    eng.wait_ge(c_loaded, 16 * 10)
                    eng.tensor_copy(ptf[:, :], pti[:, :]).then_inc(pt_set, 1)
                    for h in range(2):
                        eng.wait_ge(scored, h + 1)
                        eng.tensor_copy(sc[:, 8 * h:8 * h + 8, :].rearrange("p (a j) c -> p a (j c)", j=2), S4[:, :, 0:2 * NCS]).then_inc(copied, 1)
                    eng.drain()
                    bc = lambda a: a.unsqueeze(2).broadcast_to([GRP, X, NCS])
                    eng.tensor_reduce(st[:, 0, :], sc[:, :, :], AX.X, ALU.max)
                    eng.drain()
                    eng.tensor_tensor(sc[:, :, :], sc[:, :, :], bc(st[:, 0, :]), ALU.subtract).then_inc(shifted, 1)
                    eng.wait_ge(exped, 1)
                    eng.tensor_reduce(st[:, 1, :], sc[:, :, :], AX.X, ALU.add)
                    eng.drain()
                    eng.reciprocal(st[:, 2, :], st[:, 1, :])
                    eng.drain()
                    eng.tensor_tensor(sc[:, :, :], sc[:, :, :], bc(st[:, 2, :]), ALU.mult).then_inc(probs, 1)
                    eng.wait_ge(turned, 1)
                    pa = PA[:, 0:2 * X * GRP].rearrange("p (x c h) -> p x c h", c=2, h=GRP)
                    pt4 = pT[:, :, :].rearrange("p (x c) h -> p x c h", c=2)
                    eng.tensor_copy(pt4[:, :, 0, :], pa[:, :, 0, :])
                    eng.tensor_copy(pt4[0:P - 1, :, 1, :], pa[0:P - 1, :, 1, :]).then_inc(turned_saved, 1)
                    eng.drain()
                    eng.tensor_reduce(pS[:, :], pT[:, :, :], AX.X, ALU.add)
                    eng.drain()
                    eng.tensor_copy(pB[:, :, :], pS[:, :].unsqueeze(2).broadcast_to([P, 2 * X, NBLK])).then_inc(summed, 1)
                    eng.wait_ge(scored, 3)
                    eng.tensor_copy(oC[:, :, :].rearrange("p (a x) d -> p a (x d)", a=2), S4[:, 0:2, :])
                    eng.wait_ge(bases_done, 1)
                    eng.tensor_scalar(base[:, :], PB[0:NBLK, 0:NB], 2.0, None, ALU.mult)
                    eng.drain()
                    eng.tensor_scalar(base[:, :], base[:, :], blk[:, 1:2], None, ALU.add)
                    eng.wait_ge(rows_done, 1)
                    over = lambda a, n=NBLK: a.unsqueeze(1).broadcast_to([NBLK, X, n])
                    each = lambda a, n=NBLK: a.unsqueeze(2).broadcast_to([NBLK, X, n])
                    eng.tensor_tensor(R[:, :, :], PR[:, :, :].rearrange("p a (x j) -> p (a x) j", j=NBLK), over(selc[:, 2, :]), ALU.add)
                    eng.drain()
                    eng.tensor_tensor(Q1[:, :, :], R[:, :, :], over(selc[:, 0, :]), ALU.mult)
                    eng.drain()
                    eng.tensor_reduce(col[:, :], Q1[:, :, :], AX.X, ALU.add)
                    eng.drain()
                    eng.tensor_tensor(Q1[:, :, :], R[:, :, :], each(col[:, :]), ALU.is_gt)
                    eng.tensor_tensor(Q2[:, :, :], R[:, :, :], each(col[:, :]), ALU.is_equal)
                    eng.drain()
                    eng.tensor_tensor(Q2[:, :, :], Q2[:, :, :], over(selc[:, 1, :]), ALU.mult)
                    eng.drain()
                    eng.tensor_tensor(Q1[:, :, :], Q1[:, :, :], Q2[:, :, :], ALU.add)
                    eng.drain()
                    eng.tensor_reduce(rank[:, :], Q1[:, :, :], AX.X, ALU.add)
                    eng.drain()
                    eng.tensor_tensor(OH[:, :, :], each(rank[:, :], 16), over(ranks[:, :], 16), ALU.is_equal)
                    eng.drain()
                    b4 = base[:, :].unsqueeze(2).broadcast_to([NBLK, NB, 32])
                    o4 = OH[:, :, :].rearrange("p (b j) r -> p b (j r)", j=2)
                    eng.tensor_tensor(o4, o4, b4, ALU.mult).then_inc(oh_done, 1)
                    eng.wait_ge(ids_done, 1)
                    eng.tensor_copy(block_id[:, :], PB[0:1, 0:X * 16])

        ps = lambda n, s: ctx.enter_context(nc.psum_tensor(n, s, F32))
        kv = sb("kv_sel", [P, 2, 8, 2, HD])
        wk = sb("kv_win", [P, 2, 5, 256])
        qst = sb("q_now", [HD, 2, GRP])
        ksb = sb("keys_turned", [HD, 2, 1536])
        pd = sb("probs_dec", [GRP, 1536])
        nmx = sb("nmx_dec", [GRP, 2])
        sums = sb("sums_dec", [GRP, 4])
        pTs = sb("probs_dec_turned", [P, 13, GRP])
        KT = ps("KT", [HD, 2, 512])
        SD = ps("SD", [GRP, 4, 512])
        PT = ps("PTd", [P, 512])
        OD = ps("OD", [GRP, 512])
        kv_loaded = [sem("kv_loaded0"), sem("kv_loaded1")]
        odd_loaded = [sem("odd_loaded0"), sem("odd_loaded1")]
        wk_loaded = sem("wk_loaded")
        names = ("q_staged", "k_turned", "k_saved", "scores_done", "max_done", "exps_done", "pd_turned", "pd_saved", "od_done", "od_saved")
        q_staged, k_turned, k_saved, scores_done, max_done, exps_done, pd_turned, pd_saved, od_done, od_saved = map(sem, names)
        o_stored, steps = sem("o_stored"), sem("steps_d")
        NS, NW = NSEL * 64 + 1, WINDOW + 1
        KEYT = [(c, 64 * c * 2, P) for c in range(7)] + [(7, 896, 65)]

        def turns(eng, body):
            for j in range(2):
                body(0, j)
            with eng.Fori(1, NB) as b:
                for j in range(2):
                    body(b, j)

        def selected_blocks(eng, b, j, odd):
            x = b * 2 + j
            if not isinstance(b, int):
                eng.wait_ge(od_done, x - 1)
            for r in range(odd, NSEL, 2):
                bid = eng.value_load(block_id[0:1, bass.ds(x * 16 + r, 1)], min_val=0, max_val=2 * NPOOL - 1)
                src = io["cache_blocks"][bass.ds(bid, 1)].rearrange("o s u d -> (o s) u d")[:, 4 + j:8:2, :]
                eng.dma_start(kv[64 * odd:64 * odd + 64, j, r // 2], src).then_inc((kv_loaded, odd_loaded)[odd][j], 16)

        with nc.Block() as block:
            @block.gpsimd
            def _(eng):
                turns(eng, lambda b, j: selected_blocks(eng, b, j, 1))

            @block.sync
            def _(eng):
                def body(b, j):
                    selected_blocks(eng, b, j, 0)
                    new = io["nsa_s"][bass.ds(b, 1), :].rearrange("o (u d) -> o u d", d=HD)[:, 4 + j:8:2, :]
                    eng.dma_start(kv[64:65, j, 7], new).then_inc(kv_loaded[j], 16)
                    eng.dma_start(wk[:, j, 0:4, :], io["state"][bass.ds(b, 1)].rearrange("o (t p) e -> p (o t) e", p=P)).then_inc(kv_loaded[j], 16)
                    eng.dma_start(wk[0:1, j, 4, :], io["win_new"][bass.ds(b, 1), :]).then_inc(kv_loaded[j], 16)
                turns(eng, body)
                eng.wait_ge(od_saved, 2 * X)
                for br, o in enumerate((oC, oS, oW)):
                    dst = io["o_s"][br].rearrange("b (j h d) -> h (b j) d", j=2, h=GRP)
                    eng.dma_start(dst, o[:, :, :]).then_inc(o_stored, 16)
                eng.dma_start(io["win_s_out"][:, 0:WINDOW - 1, :], io["state"][:, 1:WINDOW, :]).then_inc(o_stored, 16)
                eng.dma_start(io["win_s_out"][:, WINDOW - 1, :], io["win_new"]).then_inc(o_stored, 16)
                eng.wait_ge(o_stored, 80)

            @block.tensor
            def _(eng):
                def steady(eng):
                    eng.sem_inc(steps, 1)

                def body(b, j):
                    first = isinstance(b, int)
                    x = b * 2 + j
                    eng.wait_ge(odd_loaded[j], b * 16 * 7 + 16 * 7)
                    eng.wait_ge(kv_loaded[j], b * 16 * 11 + 16 * 11)
                    for go in range(4):
                        k = x * 4 + go
                        if first and j == 0 and go < 2:
                            pass
                        else:
                            eng.wait_ge(k_saved, k - 1)
                        steady(eng)
                        if go < 2:
                            for c in range(4 * go, 4 * go + 4):
                                w = P if c < 7 else 65
                                mm = eng.transpose(KT[:, go % 2, c % 4 * P:c % 4 * P + w], kv[0:w, j, c, 0, :], ident[0:w, 0:w])
                        elif go == 2:
                            for c in range(4):
                                mm = eng.transpose(KT[:, 0, c * P:(c + 1) * P], wk[:, j, c, j * HD:(j + 1) * HD], ident[:, :])
                        else:
                            mm = eng.transpose(KT[:, 1, 0:1], wk[0:1, j, 4, j * HD:(j + 1) * HD], ident[0:1, 0:1])
                        mm.then_inc(k_turned, 1)
                    eng.wait_ge(k_saved, x * 4 + 4)
                    eng.wait_ge(q_staged, x + 1)
                    if not (first and j == 0):
                        eng.wait_ge(exps_done, x * 2)
                    steady(eng)
                    for a, e in ((0, 512), (512, NS), (1024, 1536)):
                        eng.matmul(SD[:, a // 512, 0:e - a], qst[:, j], ksb[:, j, a:e], start=True, stop=True)
                    eng.matmul(SD[:, 3, 0:1], qst[:, j], ksb[:, j, 1000:1001], start=True, stop=True).then_inc(scores_done, 1)
                    eng.wait_ge(exps_done, x * 2 + 2)
                    if not (first and j == 0):
                        eng.wait_ge(pd_saved, x)
                    steady(eng)
                    for c in range(13):
                        a, w = (c * P, P if c < 7 else 65) if c < 8 else (1000 + (c - 8) * P, P if c < 12 else 1)
                        mm = eng.transpose(PT[0:w, c * GRP:(c + 1) * GRP], pd[:, a:a + w], ident[0:GRP, 0:GRP])
                    mm.then_inc(pd_turned, 1)
                    eng.wait_ge(pd_saved, x + 1)
                    if not (first and j == 0):
                        eng.wait_ge(od_saved, x * 2)
                    steady(eng)
                    for c in range(8):
                        w = P if c < 7 else 65
                        eng.matmul(OD[:, 0:HD], pTs[0:w, c, :], kv[0:w, j, c, 1, :], start=c == 0, stop=c == 7)
                    for c in range(5):
                        w = P if c < 4 else 1
                        mm = eng.matmul(OD[:, HD:2 * HD], pTs[0:w, 8 + c, :], wk[0:w, j, c, (2 + j) * HD:(3 + j) * HD], start=c == 0, stop=c == 4)
                    mm.then_inc(od_done, 1)
                turns(eng, body)

            @block.vector
            def _(eng):
                eng.memset(pTs[:, :, :], 0.0)

                def body(b, j):
                    first = isinstance(b, int)
                    x = b * 2 + j
                    if not first:
                        eng.wait_ge(scores_done, x - 1)
                    eng.tensor_copy(qst[:, j], qT[:, GRP * j:GRP * j + GRP, bass.ds(b, 1)].rearrange("p h o -> p (h o)")).then_inc(q_staged, 1)
                    for go, (a, e) in enumerate(((0, 512), (512, NS), (1024, 1536), (1000, 1001))):
                        eng.wait_ge(k_turned, x * 4 + go + 1)
                        eng.tensor_copy(ksb[:, j, a:e], KT[:, go % 2, 0:e - a]).then_inc(k_saved, 1)
                    eng.wait_ge(scores_done, x + 1)
                    if not (first and j == 0):
                        eng.wait_ge(exps_done, x * 2)
                    eng.tensor_reduce(nmx[:, 0:1], SD[:, 0:2, :].rearrange("p a c -> p (a c)")[:, 0:NS], AX.X, ALU.max, negate=True)
                    eng.tensor_reduce(nmx[:, 1:2], SD[:, 2:4, :].rearrange("p a c -> p (a c)")[:, 0:NW], AX.X, ALU.max, negate=True).then_inc(max_done, 1)
                    eng.wait_ge(pd_turned, x + 1)
                    if not (first and j == 0):
                        eng.wait_ge(od_done, x)
                    p3 = PT[:, 0:13 * GRP].rearrange("p (c h) -> p c h", h=GRP)
                    eng.tensor_copy(pTs[:, 0:7, :], p3[:, 0:7, :])
                    eng.tensor_copy(pTs[0:65, 7, :], p3[0:65, 7, :])
                    eng.tensor_copy(pTs[:, 8:12, :], p3[:, 8:12, :])
                    eng.drain()
                    eng.tensor_copy(pTs[0:1, 12, :], p3[0:1, 12, :]).then_inc(pd_saved, 1)
                    eng.reciprocal(sums[:, 2:4], sums[:, 0:2])
                    eng.drain()
                    eng.wait_ge(od_done, x + 1)
                    for k, o in enumerate((oS, oW)):
                        eng.tensor_scalar(o[:, bass.ds(x, 1), :].rearrange("p o d -> p (o d)"), OD[:, k * HD:(k + 1) * HD], sums[:, 2 + k:3 + k], None, ALU.mult).then_inc(od_saved, 1)
                turns(eng, body)

            @block.scalar
            def _(eng):
                def body(b, j):
                    first = isinstance(b, int)
                    x = b * 2 + j
                    eng.wait_ge(max_done, x + 1)
                    if not (first and j == 0):
                        eng.wait_ge(pd_turned, x)
                        eng.wait_ge(od_saved, x * 2)
                    eng.activation(pd[:, 0:NS], SD[:, 0:2, :].rearrange("p a c -> p (a c)")[:, 0:NS], ACT.Exp, bias=nmx[:, 0:1], accum_out=sums[:, 0:1]).then_inc(exps_done, 1)
                    eng.activation(pd[:, 1000:1000 + NW], SD[:, 2:4, :].rearrange("p a c -> p (a c)")[:, 0:NW], ACT.Exp, bias=nmx[:, 1:2], accum_out=sums[:, 1:2]).then_inc(exps_done, 1)
                turns(eng, body)


def mix_out(nc, io, g):
    with ExitStack() as ctx:
        sb = lambda n, s, t=F32: ctx.enter_context(nc.sbuf_tensor(n, s, t))
        ps = lambda n, s, t=F32: ctx.enter_context(nc.psum_tensor(n, s, t))
        sem = lambda n: g["sem"](n)
        NTILE = TILES + 1
        rows = lambda n: P if n < TILES else NB
        mix, ident, gates = g["mix"], g["ident"], g["gates"]
        hT = g["late"][:, 0:KT * TOK].rearrange("p (k t) -> p k t", k=KT)
        w = sb("w_out_sb", [P, KT, D])
        gout = sb("g_out_rows", [P, D])
        gffn = sb("g_ffn_col", [P, KT])
        x = sb("x_again", [P, 2, D])
        h = sb("h_rows", [P, 2, D])
        sq = sb("mix_squares", [P, D])
        junk = sb("h_squares", [P, D])
        half = sb("minus_half2", [P, 16])
        s16 = sb("mix_ss", [P, 2, 16])
        ss = sb("h_ss", [P, 2, 2])
        mn = sb("mix_normed", [P, 2, D])
        mT = sb("mix_turned", [P, 2, KT, P])
        hn = sb("h_normed", [P, 2, D])
        o3 = sb("o_dec_rows", [NB, 3, 512])
        px = ps("px2", [P, 2, 512])
        py = ps("py2", [P, 2, 512])
        ph = ps("ph2", [P, 2, 2, 512])
        c_loaded, dec_loaded = map(sem, ("c_loaded2", "dec_loaded"))
        w_loaded = [sem("w_out_loaded0"), sem("w_out_loaded1")]
        x_loaded = [sem("x_again0"), sem("x_again1")]
        stored = [sem("h_stored0"), sem("h_stored1")]
        names = ("mix_ready", "squared", "summed2", "rstd16", "mix_normed_s", "mix_turned_s", "mix_saved", "projected",
                 "h_done", "h_squared", "h_rstd", "h_normed_s", "h_turned", "h_saved")
        mix_ready, squared, summed, rstd16, normed, turned, mT_saved, projected, h_done, h_squared, h_rstd, h_normed, h_turned, h_saved = map(sem, names)

        with nc.Block() as block:
            @block.sync
            def _(eng):
                def store(eng, n):
                    R, u = rows(n), n % 2
                    eng.wait_ge(h_done, n + 1)
                    eng.dma_start(io["h_s"][n * P:n * P + R, :], h[0:R, u, :]).then_inc(stored[u], 16)

                eng.dma_start(gout[:, 0:512], io["g_out_nsa"][0].rearrange("h d -> (h d)").partition_broadcast(P)).then_inc(c_loaded, 16)
                eng.dma_start(gout[:, 512:D], io["g_out_sb"][0].rearrange("h d -> (h d)").partition_broadcast(P)).then_inc(c_loaded, 16)
                eng.dma_start(gffn[:, :], io["g_ffn"].rearrange("a (k p) -> p (a k)", p=P), allow_slow_non_contiguous=True).then_inc(c_loaded, 16)
                eng.dma_start(o3[:, :, :], io["o_s"].rearrange("c b n -> b c n")).then_inc(dec_loaded, 16)
                eng.dma_start(mix[0:NB, TILES, 512:D], io["osb_s"]).then_inc(dec_loaded, 16)
                for c in range(2):
                    cols = slice(c * 512, (c + 1) * 512)
                    eng.dma_start(w[:, :, cols], io["w_out"][0].rearrange("(k p) n -> p k n", p=P)[:, :, cols]).then_inc(w_loaded[c], 16)
                for n in range(NTILE):
                    R, u = rows(n), n % 2
                    if n >= 2:
                        eng.wait_ge(h_done, n - 1)
                    src = io["x_prompt"][0, n * P:(n + 1) * P, :] if n < TILES else io["x_sample"].rearrange("b t d -> (b t) d")
                    eng.dma_start(x[0:R, u, :], src).then_inc(x_loaded[u], 16)
                    if n >= 1:
                        store(eng, n - 1)
                store(eng, TILES)
                eng.wait_ge(stored[0], 80)
                eng.wait_ge(stored[1], 64)

            @block.gpsimd
            def _(eng):
                eng.memset(half[:, :], -0.5)
                eng.drain()
                for n in range(NTILE + 1):
                    if n < NTILE:
                        R, u = rows(n), n % 2
                        eng.wait_ge(summed, n + 1)
                        eng.tensor_scalar(s16[0:R, u, :], s16[0:R, u, :], 1.0 / HD, EPS, ALU.mult, ALU.add)
                        eng.drain()
                        eng.tensor_tensor(s16[0:R, u, :], s16[0:R, u, :], half[0:R, :], ALU.pow).then_inc(rstd16, 1)
                    if n >= 1:
                        R, u = rows(n - 1), (n - 1) % 2
                        eng.wait_ge(h_squared, n)
                        eng.tensor_scalar(ss[0:R, u, 1:2], ss[0:R, u, 0:1], 1.0 / D, EPS, ALU.mult, ALU.add)
                        eng.drain()
                        eng.tensor_tensor(ss[0:R, u, 1:2], ss[0:R, u, 1:2], half[0:R, 0:1], ALU.pow).then_inc(h_rstd, 1)

            @block.scalar
            def _(eng):
                def square_mix(n):
                    R = rows(n)
                    if n == TILES:
                        eng.wait_ge(mix_ready, 1)
                        eng.wait_ge(dec_loaded, 32)
                    if n >= 1:
                        eng.wait_ge(summed, n)
                    eng.activation(sq[0:R, :], mix[0:R, n, :], ACT.Square).then_inc(squared, 1)

                def save_mT(n):
                    R, u = rows(n), n % 2
                    if n >= 2:
                        eng.wait_ge(projected, n - 1)
                    for b in range(2):
                        eng.wait_ge(turned, 2 * n + b + 1)
                        eng.activation(mT[:, u, 4 * b:4 * b + 4, 0:R], px[:, b, :].rearrange("p (k r) -> p k r", k=4)[:, :, 0:R], ACT.Copy).then_inc(mT_saved, 1)

                square_mix(0)
                save_mT(0)
                for n in range(NTILE):
                    R, u = rows(n), n % 2
                    if n + 1 < NTILE:
                        square_mix(n + 1)
                        save_mT(n + 1)
                    eng.wait_ge(h_done, n + 1)
                    if n >= 2:
                        eng.wait_ge(h_normed, n - 1)
                    eng.drain()
                    eng.activation(junk[0:R, :], h[0:R, u, :], ACT.Square, accum_out=ss[0:R, u, 0:1]).then_inc(h_squared, 1)

            @block.tensor
            def _(eng):
                def turn(n, src, ready, bank, saved, done):
                    R, u = rows(n), n % 2
                    eng.wait_ge(ready, n + 1)
                    for b in range(2):
                        if n >= 1:
                            eng.wait_ge(saved, 2 * (n - 1) + b + 1)
                        for k in range(4):
                            c = (4 * b + k) * P
                            mm = eng.transpose(bank[:, b, k * P:k * P + R], src[0:R, u, c:c + P], ident[0:R, 0:R])
                        mm.then_inc(done, 1)

                turn(0, mn, normed, px, mT_saved, turned)
                for n in range(NTILE + 1):
                    if n < NTILE:
                        R, u = rows(n), n % 2
                        eng.wait_ge(mT_saved, 2 * n + 2)
                        if n >= 2:
                            eng.wait_ge(h_done, n - 1)
                        for c in range(2):
                            if n == 0:
                                eng.wait_ge(w_loaded[c], 16)
                            for k in range(KT):
                                mm = eng.matmul(ph[0:R, u, c, :], mT[:, u, k, 0:R], w[:, k, c * 512:(c + 1) * 512], start=k == 0, stop=k == KT - 1)
                            if c == 0 and n + 1 < NTILE:
                                turn(n + 1, mn, normed, px, mT_saved, turned)
                        mm.then_inc(projected, 1)
                    if n >= 1:
                        turn(n - 1, hn, h_normed, py, h_saved, h_turned)

            @block.vector
            def _(eng):
                eng.wait_ge(c_loaded, 48)
                eng.wait_ge(dec_loaded, 32)
                m = mix[0:NB, TILES, 0:512].rearrange("b (h d) -> b h d", h=NH)
                for br in range(3):
                    o = o3[:, br, :].rearrange("b (h d) -> b h d", h=NH)
                    gt = gates[0:NB, TILES, br:24:3].unsqueeze(2).broadcast_to([NB, NH, HD])
                    eng.tensor_tensor(o, o, gt, ALU.mult)
                eng.drain()
                o = [o3[:, br, :].rearrange("b (h d) -> b h d", h=NH) for br in range(3)]
                eng.tensor_tensor(m, o[0], o[1], ALU.add)
                eng.drain()
                eng.tensor_tensor(m, m, o[2], ALU.add).then_inc(mix_ready, 1)

                def norm_mix(n):
                    R, u = rows(n), n % 2
                    eng.wait_ge(squared, n + 1)
                    if n >= 2:
                        eng.wait_ge(turned, 2 * (n - 1))
                    eng.tensor_reduce(s16[0:R, u, :], sq[0:R, :].rearrange("p (h d) -> p h d", h=16), AX.X, ALU.add).then_inc(summed, 1)
                    eng.wait_ge(rstd16, n + 1)
                    eng.drain()
                    eng.tensor_tensor(mn[0:R, u, :].rearrange("p (h d) -> p h d", h=16), mix[0:R, n, :].rearrange("p (h d) -> p h d", h=16),
                                      s16[0:R, u, :].unsqueeze(2).broadcast_to([R, 16, HD]), ALU.mult)
                    eng.drain()
                    eng.tensor_tensor(mn[0:R, u, :], mn[0:R, u, :], gout[0:R, :], ALU.mult).then_inc(normed, 1)

                norm_mix(0)
                norm_mix(1)
                for n in range(NTILE + 1):
                    if n < NTILE:
                        R, u = rows(n), n % 2
                        eng.wait_ge(projected, n + 1)
                        eng.wait_ge(x_loaded[u], 16 * (n // 2) + 16)
                        if n >= 2:
                            eng.wait_ge(stored[u], 16 * (n // 2))
                            eng.wait_ge(h_squared, n - 1)
                        eng.tensor_tensor(h[0:R, u, :], ph[0:R, u, :, :].rearrange("p c n -> p (c n)"), x[0:R, u, :], ALU.add).then_inc(h_done, 1)
                        if n + 2 < NTILE:
                            norm_mix(n + 2)
                        eng.wait_ge(h_rstd, n + 1)
                        if n >= 2:
                            eng.wait_ge(h_turned, 2 * (n - 1))
                        eng.tensor_scalar(hn[0:R, u, :], h[0:R, u, :], ss[0:R, u, 1:2], None, ALU.mult).then_inc(h_normed, 1)
                    if n >= 1:
                        R = rows(n - 1)
                        for b in range(2):
                            eng.wait_ge(h_turned, 2 * (n - 1) + b + 1)
                            out = hT[:, 4 * b:4 * b + 4, (n - 1) * P:(n - 1) * P + R]
                            eng.tensor_tensor(out, py[:, b, :].rearrange("p (k r) -> p k r", k=4)[:, :, 0:R],
                                              gffn[:, 4 * b:4 * b + 4].unsqueeze(2).broadcast_to([P, 4, R]), ALU.mult).then_inc(h_saved, 1)


def swiglu(nc, io, g):
    NF, NC, CW, KH = DFF // P, 3, TOK // 3, KT // 2
    NTILE = TILES + 1
    rows = lambda n: P if n < TILES else NB
    with ExitStack() as ctx:
        sb = lambda n, s, t=F32: ctx.enter_context(nc.sbuf_tensor(n, s, t))
        late = g["late"]
        hT = late[:, 0:KT * TOK].rearrange("p (k t) -> p k t", k=KT)
        act = sb("swiglu_act", [P, NF, TOK])
        EARLY, IN_LATE = KT * TOK // 512, NF
        wd_late = late[:, 0:IN_LATE * 512].rearrange("p (m n) -> p m n", n=512)
        CUTS = [0, EARLY, 19, NF, 2 * NF]
        wd_loaded = [g["sem"](f"wd_loaded{i}") for i in range(len(CUTS) - 1)]
        wdv = io["w_down"][0].rearrange("(f p) (c n) -> c p f n", p=P, c=2)
        with ExitStack() as c2:
            sem = lambda n: g["sem"](n)
            hT_hi = c2.enter_context(nc.sbuf_tensor("h_turned_hi", [P, KT, TOK], F32R))
            hT_lo = c2.enter_context(nc.sbuf_tensor("h_turned_lo", [P, KT, TOK], F32R))
            rest = late[:, KT * TOK:]
            raw = rest[:, 0:KT * P].rearrange("p (h k f) -> p h k f", h=2, k=KH)
            sg = rest[:, KT * P:KT * P + NC * CW].rearrange("p (c t) -> p c t", c=NC)
            w_hi = c2.enter_context(nc.sbuf_tensor("w_gu_hi", [P, 2, KH, P], F32R))
            w_lo = c2.enter_context(nc.sbuf_tensor("w_gu_lo", [P, 2, KH, P], F32R))
            pg = c2.enter_context(nc.psum_tensor("pg", [P, 2, NC, 512], F32))
            w_loaded = [sem("w_gu_loaded0"), sem("w_gu_loaded1")]
            hi_done, lo_done, up_done, silu_done, act_done = map(sem, ("w_hi_done", "w_lo_done", "up_done", "silu_done", "act_done"))
            h_hi_done, h_lo_done = sem("h_hi_done"), sem("h_lo_done")

            def loop(eng, body):
                body(0, True, False)
                with eng.Fori(1, NF - 1) as f:
                    body(f, False, False)
                body(NF - 1, False, True)

            with nc.Block() as block:
                @block.sync
                def _(eng):
                    wv = io["w_gate_up"][0].rearrange("(k p) (c f) -> p k c f", p=P, c=2)

                    def body(f, first, last):
                        for e in range(2):
                            for h in range(2):
                                if not (first and e == 0):
                                    eng.wait_ge(lo_done, f * 4 + 2 * e + h - 1)
                                eng.dma_start(raw[:, h], wv[:, KH * h:KH * h + KH, e, bass.ds(f * P, P)]).then_inc(w_loaded[h], 16)
                        if first:
                            eng.wait_ge(h_lo_done, NC)
                            eng.dma_start(wd_late[:, 0:EARLY, :], wdv[0][:, 0:EARLY, :]).then_inc(wd_loaded[0], 16)
                    loop(eng, body)

                @block.tensor
                def _(eng):
                    def body(f, first, last):
                        for e in range(2):
                            for h in range(2):
                                eng.wait_ge(lo_done, f * 4 + 2 * e + h + 1)
                                for c in range(NC):
                                    if first and e == 0 and h == 0:
                                        eng.wait_ge(h_lo_done, c + 1)
                                    if not first and h == 0:
                                        eng.wait_ge((silu_done, act_done)[e], (f - 1) * NC + c + 1)
                                    cols = slice(c * CW, (c + 1) * CW)
                                    for j in range(KH):
                                        k = KH * h + j
                                        eng.matmul(pg[:, e, c, 0:CW], w_hi[:, h, j, :], hT_hi[:, k, cols], start=k == 0, stop=False)
                                        eng.matmul(pg[:, e, c, 0:CW], w_hi[:, h, j, :], hT_lo[:, k, cols], start=False, stop=False)
                                        mm = eng.matmul(pg[:, e, c, 0:CW], w_lo[:, h, j, :], hT_hi[:, k, cols], start=False, stop=k == KT - 1)
                                    mm.then_inc(up_done, 1)
                    loop(eng, body)

                @block.scalar
                def _(eng):
                    def round_unit(f, v, first=False):
                        eng.wait_ge(w_loaded[v % 2], (f * 2 + v // 2) * 16 + 16)
                        if not first:
                            eng.wait_ge(up_done, f * 4 * NC + (v - 1) * NC)
                        eng.activation(w_hi[:, v % 2], raw[:, v % 2], ACT.Copy).then_inc(hi_done, 1)

                    def round_rows(c):
                        cols = slice(c * CW, (c + 1) * CW)
                        eng.activation(hT_hi[:, :, cols], hT[:, :, cols], ACT.Copy).then_inc(h_hi_done, 1)

                    def body(f, first, last):
                        if first:
                            round_unit(0, 0, True)
                            round_rows(0)
                            round_unit(0, 1, True)
                            round_rows(1)
                            round_rows(2)
                        round_unit(f, 2)
                        round_unit(f, 3)
                        for c in range(NC):
                            eng.wait_ge(up_done, f * 4 * NC + NC + c + 1)
                            if not first:
                                eng.wait_ge(act_done, (f - 1) * NC + c + 1)
                            eng.activation(sg[:, c, :], pg[:, 0, c, 0:CW], ACT.Silu).then_inc(silu_done, 1)
                        if not last:
                            round_unit(f, 4)
                            round_unit(f, 5)
                    loop(eng, body)

                @block.vector
                def _(eng):
                    def rest_of_unit(f, v):
                        eng.wait_ge(hi_done, f * 4 + v + 1)
                        eng.tensor_tensor(w_lo[:, v % 2], raw[:, v % 2], w_hi[:, v % 2].bitcast(F32), ALU.subtract).then_inc(lo_done, 1)

                    def rest_of_rows(c):
                        cols = slice(c * CW, (c + 1) * CW)
                        eng.wait_ge(h_hi_done, c + 1)
                        eng.tensor_tensor(hT_lo[:, :, cols], hT[:, :, cols], hT_hi[:, :, cols].bitcast(F32), ALU.subtract).then_inc(h_lo_done, 1)

                    def body(f, first, last):
                        if first:
                            rest_of_unit(0, 0)
                            rest_of_rows(0)
                            rest_of_unit(0, 1)
                            rest_of_rows(1)
                            rest_of_rows(2)
                        rest_of_unit(f, 2)
                        rest_of_unit(f, 3)
                        if not last:
                            rest_of_unit(f, 4)
                            rest_of_unit(f, 5)
                        for c in range(NC):
                            eng.wait_ge(silu_done, f * NC + c + 1)
                            eng.wait_ge(up_done, f * 4 * NC + 3 * NC + c + 1)
                            out = act[:, bass.ds(f, 1), c * CW:(c + 1) * CW].rearrange("p o t -> p (o t)")
                            eng.tensor_tensor(out, sg[:, c, :], pg[:, 1, c, 0:CW], ALU.mult).then_inc(act_done, 1)
                    loop(eng, body)
        with ExitStack() as c2:
            sem = lambda n: g["sem"](n)
            py = c2.enter_context(nc.psum_tensor("py3", [P, 4, 512], F32))
            wd_last = c2.enter_context(nc.sbuf_tensor("w_down_last", [P, 2 * NF - IN_LATE, 512], F32))
            hr = c2.enter_context(nc.sbuf_tensor("h_back", [P, 4, 512], F32))
            y = c2.enter_context(nc.sbuf_tensor("y_rows", [P, 2, 512], F32))
            h_loaded = [sem(f"h_back{r}") for r in range(4)]
            down_done, y_done = sem("down_done"), sem("y_done")
            stored = [sem("y_stored0"), sem("y_stored1")]
            jobs = [(c, n) for c in range(2) for n in range(NTILE)]

            def wd(m0, m1):
                for a, e, t in ((0, IN_LATE, wd_late), (IN_LATE, 2 * NF, wd_last)):
                    if a <= m0 and m1 <= e:
                        return t[:, m0 - a:m1 - a, :]

            def load_h(eng, m):
                c, n = jobs[m]
                R = rows(n)
                if m >= 4:
                    eng.wait_ge(y_done, m - 3)
                eng.dma_start(hr[0:R, m % 4], io["h_s"][n * P:n * P + R, c * 512:c * 512 + 512]).then_inc(h_loaded[m % 4], 16)

            with nc.Block() as block:
                @block.sync
                def _(eng):
                    for i, (a, e) in enumerate(zip(CUTS, CUTS[1:])):
                        if i:
                            eng.dma_start(wd(a, e), wdv[a // NF][:, a % NF:a % NF + e - a, :]).then_inc(wd_loaded[i], 16)
                        if i == 2:
                            load_h(eng, 0)
                    for m in range(1, len(jobs)):
                        load_h(eng, m)

                @block.scalar
                def _(eng):
                    for m, (c, n) in enumerate(jobs):
                        R = rows(n)
                        dst = io["y_prompt"][n * P:(n + 1) * P] if n < TILES else io["y_sample"]
                        eng.wait_ge(y_done, m + 1)
                        eng.dma_start(dst[:, c * 512:c * 512 + 512], y[0:R, m % 2]).then_inc(stored[m % 2], 16)
                    for s in stored:
                        eng.wait_ge(s, 16 * len(jobs) // 2)

                @block.tensor
                def _(eng):
                    for m, (c, n) in enumerate(jobs):
                        R = rows(n)
                        if m >= 4:
                            eng.wait_ge(y_done, m - 3)
                        for f in range(NF):
                            if n == 0 and c * NF + f in CUTS:
                                eng.wait_ge(wd_loaded[CUTS.index(c * NF + f)], 16)
                            row = c * NF + f
                            w = wd(row, row + 1).rearrange("p o n -> p (o n)")
                            mm = eng.matmul(py[0:R, m % 4, :], act[:, f, n * P:n * P + R], w, start=f == 0, stop=f == NF - 1)
                        mm.then_inc(down_done, 1)

                @block.vector
                def _(eng):
                    for m, (c, n) in enumerate(jobs):
                        R = rows(n)
                        eng.wait_ge(down_done, m + 1)
                        eng.wait_ge(h_loaded[m % 4], 16 * (m // 4) + 16)
                        if m >= 2:
                            eng.wait_ge(stored[m % 2], 16 * (m // 2))
                        eng.tensor_tensor(y[0:R, m % 2], py[0:R, m % 4], hr[0:R, m % 4], ALU.add).then_inc(y_done, 1)


_INS = ["x_prompt", "x_sample", "cache_nsa_kv", "cache_sb_kv", "state_nsa_window", "page_table", "g_attn", "w_in",
        "g_q", "g_k", "w_cmp1_k", "w_cmp2_k", "pe_cmp_k", "w_cmp1_v", "w_cmp2_v", "pe_cmp_v", "g_out_nsa",
        "g_out_sb", "w_out", "g_ffn", "w_gate_up", "w_down"]

_OUTS = [("y_prompt", (1, SEQ, D)), ("y_sample", (NB, 1, D)), ("nsa_p", (1, 1, SEQ, 4, KVH, HD)), ("nsa_s", (1, NB, 1, 4, KVH, HD)),
         ("sb_p", (1, 1, SEQ, 2, NH, HD)), ("sb_s", (1, NB, 1, 2, NH, HD)),
         ("win_p_out", (1, 1, WINDOW, 2, KVH, HD)), ("win_s_out", (1, NB, WINDOW, 2, KVH, HD))]


def build(nc, io):
    with ExitStack() as ctx:
        sb = lambda n, s, t=F32: ctx.enter_context(nc.sbuf_tensor(n, s, t))
        taken = []

        def new_sem(name):
            taken.append(nc.alloc_semaphore(name))
            return taken[-1]

        def give_back():
            nc.all_engine_barrier()
            nc.clear_and_free_semaphores(taken)
            nc.all_engine_barrier()
            taken.clear()

        g = {"sem": new_sem, "ident": sb("ident", [P, P]), "gates": sb("gates", [P, TILES + 1, 24])}
        loaded = nc.alloc_semaphore("ident_loaded")
        with nc.Block() as block:
            @block.sync
            def _(eng):
                eng.dma_start(g["ident"][:, :], io["c_ident"]).then_inc(loaded, 16)
                eng.wait_ge(loaded, 16)
        project(nc, io, g)
        g["late"] = sb("late", [P, DFF // P * 512])
        with ExitStack() as mid:
            sm = lambda n, s, t=F32: mid.enter_context(nc.sbuf_tensor(n, s, t))
            g["mix"] = sm("mix", [P, TILES + 1, D])
            with ExitStack() as inner:
                si = lambda n, s, t=F32: inner.enter_context(nc.sbuf_tensor(n, s, t))
                g.update({"pt": si("page_table_sb", [1, NB * NPAGE], I32),
                          "kcTp": si("kc_prompt", [HD, KVH, NCP]), "vcp": si("vc_prompt", [64, KVH, HD + 1])})
                compress(nc, io, g)
                give_back()
                attend(nc, io, g)
                give_back()
                decode_nsa(nc, io, g)
                give_back()
            mix_out(nc, io, g)
        swiglu(nc, io, g)


def kernel(**inputs):
    import concourse.bacc as _bacc
    from concourse.bass_utils import run_bass_kernel_spmd as _run

    nc = _bacc.Bacc("TRN2", target_bir_lowering=False, num_devices=1)
    arrays, io = {}, {}
    for name in _INS:
        a = np.ascontiguousarray(inputs[name])
        if a.dtype.kind in "iu":
            a = a.astype(np.int32)
        arrays["in_" + name] = a
        io[name] = nc.dram_tensor("in_" + name, a.shape, mybir.dt.from_np(a.dtype), kind="ExternalInput").ap()
    for name, a in constants().items():
        arrays[name] = np.ascontiguousarray(a)
        io[name] = nc.dram_tensor(name, a.shape, F32, kind="ExternalInput").ap()
    outs = {n: nc.dram_tensor("out_" + n, s, F32, kind="ExternalOutput").ap() for n, s in _OUTS}
    flat = lambda ap: ap.rearrange("a b t c j d -> (a b t) (c j d)")
    for n in ("nsa_p", "nsa_s", "sb_p", "sb_s"):
        io[n] = flat(outs[n])
    io["y_prompt"] = outs["y_prompt"][0]
    io["y_sample"] = outs["y_sample"].rearrange("b t d -> (b t) d")
    io["win_p_out"] = flat(outs["win_p_out"])
    io["win_s_out"] = outs["win_s_out"][0].rearrange("b t c j d -> b t (c j d)")
    scratch = lambda n, s: nc.dram_tensor("scratch_" + n, s, F32, kind="Internal").ap()
    io["win_p"] = scratch("win_p", (SEQ, 256))
    io["win_new"] = scratch("win_new", (NB, 256))
    io["T"] = scratch("T", (NT * HD, SEQ))
    io["Ts"] = scratch("Ts", (NT * HD, NB))
    io["sbq_s"] = scratch("sbq_s", (NB, 512))
    io["osb_s"] = scratch("osb_s", (NB, 512))
    io["h_s"] = scratch("h_s", (TOK, D))
    io["cache_blocks"] = io["cache_nsa_kv"][0].rearrange("n (a s) f j d -> (n a) s (f j) d", a=2)
    io["o_s"] = scratch("o_s", (3, NB, 512))
    io["kcT_s"] = scratch("kcT_s", (HD, NB * KVH * NCS))
    io["vc_s"] = scratch("vc_s", (P, NB * KVH, 2, HD))
    io["T3"] = io["T"].rearrange("(h d) t -> h d t", d=HD)
    io["cache_nsa"] = io["cache_nsa_kv"][0].rearrange("n (s r) f j d -> (n s) r (f j d)", r=2)
    io["cache_sb"] = io["cache_sb_kv"][0].rearrange("n s c h d -> (n s) c (h d)")
    io["state"] = io["state_nsa_window"][0].rearrange("b t c j d -> b t (c j d)")
    nc.disable_value_cache = True
    build(nc, io)
    r = _run(nc, [arrays], core_ids=[0])
    return tuple(r.results[0]["out_" + n] for n, _ in _OUTS)
```

```python
import math
from contextlib import ExitStack

import numpy as np
import concourse.bass as bass
from concourse import mybir

F32 = mybir.dt.float32
F32R = mybir.dt.float32r
BF16 = mybir.dt.bfloat16
I32 = mybir.dt.int32
U32 = mybir.dt.uint32
ALU = mybir.AluOpType
ACT = mybir.ActivationFunctionType
AX = mybir.AxisListType

P = 128
D = 1024
SEQ = 1024
NB = 8
PAST = 4096
PAGE = 128
NPAGE = PAST // PAGE
NPOOL = NB * NPAGE * 5 // 4
HD = 64
NH = 8
KVH = 2
GRP = NH // KVH
WINDOW = 512
DFF = 2816
PROJ = 2840
KT = D // P
TILES = SEQ // P
NCP = (SEQ - 32) // 16 + 1
NCS = (PAST + 1 - 32) // 16 + 1
NBLK = PAST // 64
NSEL = 15
EPS = 1e-6
NEG = -1e30
SCALE = HD ** -0.5

COLS = [(0, 512), (512, 1024), (1024, 1304), (1304, 1816), (1816, 2328), (2328, 2840)]
GATE0, SBQ0, SBK0 = 1280, 1304, 1816
T_QN, T_KS, T_KW, T_QS, T_KB = 0, 8, 10, 12, 20
NT = 28
TOK = SEQ + NB


def constants():
    inv = np.exp(-math.log(10000.0) * np.arange(0, HD, 2, dtype=np.float32) / HD).astype(np.float32)
    pos = np.concatenate([np.arange(SEQ), np.full(P, PAST)]).astype(np.float32)
    ang = pos[:, None] * inv[None, :]
    rot = np.stack([np.cos(ang), np.sin(ang)], 1).astype(np.float32)
    i, j = np.arange(P)[:, None], np.arange(P)[None, :]
    masks = np.zeros((P, 3, P), np.float32)
    masks[:, 0] = np.where(j > i, NEG, 0)
    masks[:, 1] = np.where(j >= i, NEG, 0)
    masks[:, 2] = np.where(j < i, NEG, 0)
    cend = np.arange(64) * 16 + 31
    cmask = np.where(cend[None, :] <= np.arange(SEQ)[:, None], 0, NEG).astype(np.float32)
    cmask = cmask.reshape(TILES, P, 64).transpose(1, 0, 2)
    rowok = (np.arange(P) >= 31).astype(np.float32)[:, None]
    c = np.arange(256)[:, None] * 16
    b = np.arange(NBLK)[None, :] * 64
    ov = ((c < b + 64) & (c + 32 > b)).astype(np.float32)
    ov[NCS:] = 0
    ov = ov.reshape(2, P, NBLK).transpose(1, 0, 2)
    k, r = np.arange(NBLK), np.arange(16)
    sel = np.zeros((NBLK, 3, NBLK), np.float32)
    sel[:, 0] = np.eye(NBLK)
    sel[:, 1] = (k[None, :] < k[:, None])
    sel[:, 2] = np.where((k == 0) | (k == NBLK - 1), 1e30, 0)[None, :]
    ranks = np.broadcast_to(r, (NBLK, 16)).astype(np.float32)
    blk = np.stack([(k // 2), (k % 2)], 1).astype(np.float32)
    pageof = (np.arange(NPAGE)[:, None] == (k // 2)[None, :]).astype(np.float32)
    off = np.stack([(np.arange(P) < 64), (np.arange(P) >= 64), (np.arange(P) % 64) * 8], 1).astype(np.float32)
    tri = (i >= j).astype(np.float32)
    diag = np.zeros((NH, NH, HD), np.float32)
    for h in range(NH):
        diag[h, h] = 1
    return {
        "c_rot": rot.reshape(TILES + 1, P, 64), "c_ident": np.eye(P, dtype=np.float32),
        "c_masks": masks, "c_cmask": cmask, "c_rowok": rowok, "c_ov": ov, "c_sel": sel,
        "c_ranks": ranks, "c_blk": blk, "c_pageof": pageof, "c_off": off, "c_tri": tri, "c_diag": diag,
    }


def project(nc, io, g):
    with ExitStack() as ctx:
        sb = lambda n, s, t=F32: ctx.enter_context(nc.sbuf_tensor(n, s, t))
        ps = lambda n, s, t=F32: ctx.enter_context(nc.psum_tensor(n, s, t))
        sem = lambda n: g["sem"](n)
        w = sb("w_in_sb", [P, KT, PROJ])
        x = sb("x_sb", [P, 2, D])
        xn = sb("xn_sb", [P, 2, D])
        xT = sb("xT_sb", [P, 2, KT, P])
        pj = sb("proj_sb", [P, 2, PROJ])
        junk = sb("squares_sb", [P, D])
        ss = sb("ss_sb", [P, 2, 2])
        half = sb("minus_half", [P, 16])
        rot = sb("rot_sb", [P, 2, 64])
        gat = sb("g_attn_col", [P, KT])
        gqk = sb("g_qk_sb", [P, 14, HD])
        sq = sb("qk_squares", [P, 14, HD])
        hss = sb("head_ss", [P, 2, 16])
        r1 = sb("normed", [P, 14, HD])
        ra = sb("rot_a", [P, 14, HD])
        rb = sb("rot_b", [P, 14, HD])
        ro = sb("roped", [P, 2, 14, HD])
        kvo = sb("kv_out", [P, 2, 6, P])
        ts_hi = sb("turned_hi", [P, 2, 14, P], F32R)
        ts_lo = sb("turned_lo", [P, 2, 14, P], F32R)
        ts = sb("turned_sample", [P, 14, NB])
        sbq = sb("sb_q_scaled", [NB, 512])
        px = ps("px", [P, 2, 512])
        pp = ps("pp", [P, 4, 512])
        pt = ps("pt", [P, 2, 512])
        w_loaded = [sem(f"w_loaded{c}") for c in range(6)]
        c_loaded = sem("c_loaded")
        x_loaded = [sem("x_loaded0"), sem("x_loaded1")]
        x_squared, x_rstd, x_normed, x_turned, x_ready = map(sem, ("x_squared", "x_rstd", "x_normed", "x_turned", "x_ready"))
        proj_done, proj_saved = map(sem, ("proj_done", "proj_saved"))
        qk_squared, qk_summed, qk_rstd, roped, kv_copied = map(sem, ("qk_squared", "qk_summed", "qk_rstd", "roped", "kv_copied"))
        turned, turned_saved, sbq_scaled = map(sem, ("turned", "turned_saved", "sbq_scaled"))
        stored = [sem("stored0"), sem("stored1")]
        NTILE = TILES + 1
        rows = lambda n: P if n < TILES else NB
        ident = g["ident"]

        with nc.Block() as block:
            @block.sync
            def _(eng):
                eng.dma_start(gat[:, :], io["g_attn"].rearrange("a (k p) -> p (a k)", p=P), allow_slow_non_contiguous=True).then_inc(c_loaded, 16)
                for h in range(8):
                    eng.dma_start(gqk[:, h, :], io["g_q"][0].partition_broadcast(P)).then_inc(c_loaded, 16)
                for r in range(3):
                    for j in range(2):
                        eng.dma_start(gqk[:, 8 + 2 * r + j, :], io["g_k"][0, r].partition_broadcast(P)).then_inc(c_loaded, 16)
                def load(n):
                    R, u = rows(n), n % 2
                    if n >= 2:
                        eng.wait_ge(x_normed, n - 1)
                        eng.wait_ge(roped, n - 1)
                    src = io["x_prompt"][0, n * P:(n + 1) * P, :] if n < TILES else io["x_sample"].rearrange("b t d -> (b t) d")
                    eng.dma_start(x[0:R, u, :], src).then_inc(x_loaded[u], 16)
                    eng.dma_start(rot[0:R, u, :], io["c_rot"][n, 0:R]).then_inc(x_loaded[u], 16)

                def store(n):
                    R, u, t0 = rows(n), n % 2, n * P
                    k4 = kvo[0:R, u, 0:4, :].rearrange("p r e -> p (r e)")
                    k2 = kvo[0:R, u, 4:6, :].rearrange("p r e -> p (r e)")
                    last = n == TILES
                    eng.wait_ge(kv_copied, n + 1)
                    eng.dma_start(io["nsa_s"] if last else io["nsa_p"][t0:t0 + R, :], k4).then_inc(stored[u], 16)
                    eng.dma_start(io["win_new"] if last else io["win_p"][t0:t0 + R, :], k2).then_inc(stored[u], 16)
                    eng.wait_ge(proj_saved, 6 * n + 6)
                    eng.dma_start(io["sb_s"] if last else io["sb_p"][t0:t0 + R, :], pj[0:R, u, SBK0:PROJ]).then_inc(stored[u], 16)
                    eng.wait_ge(turned_saved, 4 * n + 4)
                    if last:
                        eng.dma_start(io["Ts"].rearrange("(m p) t -> p m t", p=P), ts[:, :, :], allow_slow_non_contiguous=True).then_inc(stored[u], 16)
                        eng.wait_ge(sbq_scaled, 1)
                        eng.dma_start(io["sbq_s"], sbq[:, :]).then_inc(stored[u], 16)
                    else:
                        for name, part in (("T_hi", ts_hi), ("T_lo", ts_lo)):
                            eng.dma_start(io[name].rearrange("(m p) t -> p m t", p=P)[:, :, t0:t0 + R], part[:, u, :, :].bitcast(F32)).then_inc(stored[u], 16)

                load(0)
                wv = io["w_in"][0].rearrange("(k p) n -> p k n", p=P)
                for c, (a, b) in enumerate(COLS):
                    eng.dma_start(w[:, :, a:b], wv[:, :, a:b]).then_inc(w_loaded[c], 16)
                load(1)
                for n in range(NTILE):
                    if n + 2 < NTILE:
                        load(n + 2)
                    store(n)
                eng.wait_ge(stored[0], 80 * 5)
                eng.wait_ge(stored[1], 80 * 4)

            @block.gpsimd
            def _(eng):
                eng.memset(half[:, :], -0.5)
                eng.drain()

                def head_norm(n):
                    R, u = rows(n), n % 2
                    eng.wait_ge(qk_summed, n + 1)
                    eng.tensor_scalar(hss[0:R, u, 0:14], hss[0:R, u, 0:14], 1.0 / HD, EPS, ALU.mult, ALU.add)
                    eng.drain()
                    eng.tensor_tensor(hss[0:R, u, 0:14], hss[0:R, u, 0:14], half[0:R, 0:14], ALU.pow).then_inc(qk_rstd, 1)

                def join_rows(n):
                    R, u = rows(n), n % 2
                    eng.wait_ge(roped, n + 1)
                    eng.wait_ge(proj_saved, 6 * n + 6)
                    if n >= 2:
                        eng.wait_ge(stored[u], 80 * (n // 2))
                    rv = ro[0:R, u, 8:14, :].rearrange("p (r j) d -> p r (j d)", j=2)
                    kv = kvo[0:R, u, :, :].rearrange("p (r c) e -> p r c e", c=2)
                    pv = pj[0:R, u, 512:1280].rearrange("p (r c e) -> p r c e", r=3, c=2)
                    eng.tensor_copy(kv[:, :, 0, :], rv)
                    eng.tensor_copy(kv[:, :, 1, :], pv[:, :, 1, :]).then_inc(kv_copied, 1)

                for n in range(NTILE):
                    R, u = rows(n), n % 2
                    eng.wait_ge(x_squared, n + 1)
                    eng.tensor_scalar(ss[0:R, u, 1:2], ss[0:R, u, 0:1], 1.0 / D, EPS, ALU.mult, ALU.add)
                    eng.drain()
                    eng.tensor_tensor(ss[0:R, u, 1:2], ss[0:R, u, 1:2], half[0:R, 0:1], ALU.pow).then_inc(x_rstd, 1)
                    if n >= 1:
                        head_norm(n - 1)
                        join_rows(n - 1)
                head_norm(TILES)
                join_rows(TILES)

            @block.scalar
            def _(eng):
                def square(n):
                    R, u = rows(n), n % 2
                    eng.wait_ge(x_loaded[u], 32 * (n // 2 + 1))
                    eng.drain()
                    eng.activation(junk[0:R, :], x[0:R, u, :], ACT.Square, accum_out=ss[0:R, u, 0:1]).then_inc(x_squared, 1)
                square(0)
                for n in range(NTILE):
                    R, u = rows(n), n % 2
                    if n + 1 < NTILE:
                        if n >= 1:
                            eng.wait_ge(x_normed, n)
                        square(n + 1)
                    for c, (a, b) in enumerate(COLS):
                        if n >= 2 and c == 0:
                            eng.wait_ge(stored[u], 80 * (n // 2))
                            eng.wait_ge(turned, 4 * (n - 1))
                            eng.wait_ge(roped, n - 1)
                        eng.wait_ge(proj_done, 6 * n + c + 1)
                        eng.activation(pj[0:R, u, a:b], pp[0:R, (6 * n + c) % 4, 0:b - a], ACT.Copy).then_inc(proj_saved, 1)
                    eng.drain()
                    if n >= 1:
                        eng.wait_ge(qk_summed, n)
                    eng.activation(sq[0:R, 0:8, :].rearrange("p h d -> p (h d)"), pj[0:R, u, 0:512], ACT.Square)
                    kk = pj[0:R, u, 512:1280].rearrange("p (r c e) -> p r c e", r=3, c=2)[:, :, 0, :]
                    eng.activation(sq[0:R, 8:14, :].rearrange("p (r j) d -> p r (j d)", j=2), kk, ACT.Square).then_inc(qk_squared, 1)
                    eng.activation(g["gates"][0:R, n, :], pj[0:R, u, GATE0:GATE0 + 24], ACT.Sigmoid)
                    if n == TILES:
                        eng.activation(sbq[:, :], pj[0:R, u, SBQ0:SBK0], ACT.Copy, scale=SCALE).then_inc(sbq_scaled, 1)

            @block.tensor
            def _(eng):
                def x_transposes(n):
                    R, u = rows(n), n % 2
                    eng.wait_ge(x_normed, n + 1)
                    for b in range(2):
                        if n >= 1:
                            eng.wait_ge(x_ready, 2 * (n - 1) + b + 1)
                        for k in range(4):
                            mm = eng.transpose(px[:, b, k * P:k * P + R], xn[0:R, u, (4 * b + k) * P:(4 * b + k + 1) * P], ident[0:R, 0:R])
                        mm.then_inc(x_turned, 1)

                def head_transposes(n, groups):
                    R, u = rows(n), n % 2
                    eng.wait_ge(roped, n + 1)
                    for b in groups:
                        m = 4 * n + b
                        if m >= 2:
                            eng.wait_ge(turned_saved, m - 1)
                        for k in range(4 * b, min(4 * b + 4, 14)):
                            if k < 4:
                                src = ro[0:R, u, 2 * k:2 * k + 2, :]
                            elif k < 6:
                                src = ro[0:R, u, 2 * k + 2:2 * k + 4, :]
                            else:
                                a = SBQ0 + (k - 6) * P
                                src = pj[0:R, u, a:a + P]
                            if k < 6:
                                src = src.rearrange("p h d -> p (h d)")
                            mm = eng.transpose(pt[:, m % 2, (k % 4) * P:(k % 4) * P + R], src, ident[0:R, 0:R])
                        mm.then_inc(turned, 1)

                for n in range(NTILE):
                    R, u = rows(n), n % 2
                    x_transposes(n) if n == 0 else None
                    for c, (a, b) in enumerate(COLS):
                        m = 6 * n + c
                        if c == 0:
                            eng.wait_ge(x_ready, 2 * n + 2)
                        if c == 3 and n >= 1:
                            head_transposes(n - 1, (0, 1))
                        if c == 4 and n >= 1:
                            head_transposes(n - 1, (2, 3))
                        if c == 4 and n + 1 < NTILE:
                            x_transposes(n + 1)
                        if n == 0:
                            eng.wait_ge(w_loaded[c], 16)
                        if m >= 4:
                            eng.wait_ge(proj_saved, m - 3)
                        for k in range(KT):
                            mm = eng.matmul(pp[0:R, m % 4, 0:b - a], xT[:, u, k, 0:R], w[:, k, a:b], start=(k == 0), stop=(k == KT - 1))
                        mm.then_inc(proj_done, 1)
                head_transposes(TILES, range(4))

            @block.vector
            def _(eng):
                eng.wait_ge(c_loaded, 16 * 15)

                def norm_x(n):
                    R, u = rows(n), n % 2
                    eng.wait_ge(x_rstd, n + 1)
                    if n >= 2:
                        eng.wait_ge(x_turned, 2 * (n - 1))
                    eng.tensor_scalar(xn[0:R, u, :], x[0:R, u, :], ss[0:R, u, 1:2], None, ALU.mult).then_inc(x_normed, 1)

                def save_xT(n):
                    R, u = rows(n), n % 2
                    if n >= 2:
                        eng.wait_ge(proj_done, 6 * (n - 1))
                    for b in range(2):
                        eng.wait_ge(x_turned, 2 * n + b + 1)
                        eng.tensor_tensor(xT[:, u, 4 * b:4 * b + 4, 0:R], px[:, b, :].rearrange("p (k r) -> p k r", k=4)[:, :, 0:R],
                                          gat[:, 4 * b:4 * b + 4].to_broadcast([P, 4, R]), ALU.mult).then_inc(x_ready, 1)

                def rotate(n):
                    R, u = rows(n), n % 2
                    eng.wait_ge(qk_squared, n + 1)
                    eng.tensor_reduce(hss[0:R, u, 0:14], sq[0:R, :, :], AX.X, ALU.add).then_inc(qk_summed, 1)
                    eng.wait_ge(qk_rstd, n + 1)
                    rs = hss[0:R, u, 0:14].to_broadcast([R, 14, HD])
                    kk = pj[0:R, u, 512:1280].rearrange("p (r c j d) -> p r c j d", r=3, c=2, j=2)
                    eng.tensor_tensor(r1[0:R, 0:8, :], pj[0:R, u, 0:512].rearrange("p (h d) -> p h d", d=HD), rs[:, 0:8, :], ALU.mult)
                    for r in range(3):
                        eng.tensor_tensor(r1[0:R, 8 + 2 * r:10 + 2 * r, :], kk[:, r, 0, :, :], rs[:, 8 + 2 * r:10 + 2 * r, :], ALU.mult)
                    eng.drain()
                    eng.tensor_tensor(r1[0:R], r1[0:R], gqk[0:R], ALU.mult)
                    eng.drain()
                    cos = rot[0:R, u:u + 1, 0:32].to_broadcast([R, 14, 32])
                    sin = rot[0:R, u:u + 1, 32:64].to_broadcast([R, 14, 32])
                    for o in (0, 32):
                        eng.tensor_tensor(ra[0:R, :, o:o + 32], r1[0:R, :, o:o + 32], cos, ALU.mult)
                        eng.tensor_tensor(rb[0:R, :, o:o + 32], r1[0:R, :, 32 - o:64 - o], sin, ALU.mult)
                    if n >= 2:
                        eng.wait_ge(turned, 4 * (n - 1))
                        eng.wait_ge(kv_copied, n - 1)
                    eng.drain()
                    eng.tensor_tensor(ro[0:R, u, :, 0:32], ra[0:R, :, 0:32], rb[0:R, :, 0:32], ALU.subtract)
                    eng.tensor_tensor(ro[0:R, u, :, 32:64], ra[0:R, :, 32:64], rb[0:R, :, 32:64], ALU.add).then_inc(roped, 1)

                def save_turned(n):
                    R, u = rows(n), n % 2
                    if n >= 2:
                        eng.wait_ge(stored[u], 80 * (n // 2))
                    for b in range(4):
                        eng.wait_ge(turned, 4 * n + b + 1)
                        cnt = min(4, 14 - 4 * b)
                        for a, e, s in ([(0, 4, SCALE)], [(0, 2, 1.0), (2, 4, SCALE)], [(0, 2, SCALE), (2, 4, 1.0)], [(0, 2, 1.0)])[b]:
                            src = pt[:, b % 2, :].rearrange("p (k r) -> p k r", k=4)[:, a:e, 0:R]
                            out = slice(4 * b + a, 4 * b + e)
                            if n == TILES:
                                ins = eng.tensor_scalar(ts[:, out, :], src, s, None, ALU.mult)
                                continue
                            eng.tensor_scalar(ts_hi[:, u, out, :], src, s, None, ALU.mult)
                            eng.drain()
                            ins = eng.scalar_tensor_tensor(ts_lo[:, u, out, :], src, s, ts_hi[:, u, out, :].bitcast(F32), ALU.mult, ALU.subtract)
                        ins.then_inc(turned_saved, 1)

                norm_x(0)
                save_xT(0)
                for n in range(NTILE):
                    if n + 1 < NTILE:
                        norm_x(n + 1)
                    if n >= 1:
                        save_turned(n - 1)
                    if n + 1 < NTILE:
                        save_xT(n + 1)
                    rotate(n)
                save_turned(TILES)


def compress(nc, io, g):
    with ExitStack() as ctx:
        sb = lambda n, s, t=F32: ctx.enter_context(nc.sbuf_tensor(n, s, t))
        ps = lambda n, s, t=F32: ctx.enter_context(nc.psum_tensor(n, s, t))
        sem = lambda n: g["sem"](n)
        RING, PAIRS = 8, NPAGE // 2
        w1 = sb("w_cmp1", [P, 2, 2, 8, P])
        w2 = sb("w_cmp2", [P, 2, HD])
        pe = sb("pe_rows", [16, 2, P])
        peT = sb("pe_cols", [P, 2, 16])
        peb = sb("pe_bias", [P, 2])
        pg = g["late"][:, 0:RING * 512].rearrange("p (s r e) -> p s r e", s=RING, r=2)
        xt = sb("rows_turned", [P, 2, 4, PAST // 2])
        hid = sb("hidden", [P, 2, 2 * NCS])
        px = ps("px_c", [P, 2, 512])
        ph = ps("ph_c", [P, 2, 512])
        pk = ps("pk_c", [HD, 512])
        pv = ps("pv_c", [P, 512])
        w_loaded = sem("cmp_w_loaded")
        table_ready = sem("page_table_loaded")
        pair_loaded = [sem(f"pair_loaded{r}") for r in range(RING)]
        second_loaded = [sem(f"second_loaded{r}") for r in range(RING)]
        turned, hidden_done, gelu_done, block_done, keys_saved, values_saved = map(
            sem, ("rows_turned_s", "hidden_done", "gelu_done", "block_done", "keys_saved", "values_saved"))
        saved = [sem("turned_saved_v"), sem("turned_saved_a")]
        pe_turned, pe_saved, bias_saved = map(sem, ("pe_turned", "pe_saved", "bias_saved"))
        ident, pt, kcp_hi, kcp_lo, vcp = (g[k] for k in ("ident", "pt", "kcp_hi", "kcp_lo", "vcp"))
        kcT = sb("kc_turned", [HD, NB * KVH, NCS])
        vc = sb("vc_rows", [P, NB * KVH, 2, HD])
        parked = sem("compressed_parked")

        def load_pages(eng, a):
            with eng.Fori(0, NB) as b:
                for q in range(PAIRS):
                    slot = (4 + q) % RING
                    if q >= 4:
                        eng.wait_ge(turned, b * PAIRS + q - 3)
                    else:
                        eng.wait_ge(turned, b * PAIRS + 1)
                    page = eng.value_load(pt[0:1, bass.ds(b * NPAGE + 2 * q + a, 1)], min_val=0, max_val=NPOOL - 1)
                    rows = io["cache_nsa"][bass.ds(page * (PAGE // 2), PAGE // 2), :, 0:256]
                    eng.dma_start(pg[64 * a:64 * a + 64, slot], rows).then_inc((pair_loaded, second_loaded)[a][slot], 16)

        with nc.Block() as block:
            @block.gpsimd
            def _(eng):
                eng.wait_ge(table_ready, 16)
                load_pages(eng, 1)

            @block.sync
            def _(eng):
                for kk, s in enumerate("kv"):
                    eng.dma_start(pe[:, kk, :], io[f"pe_cmp_{s}"][0].rearrange("(m r) d -> m (r d)", r=2)).then_inc(w_loaded, 16)
                    eng.dma_start(w1[:, kk], io[f"w_cmp1_{s}"][0].rearrange("(a j p) n -> p a j n", a=2, p=P)).then_inc(w_loaded, 16)
                    eng.dma_start(w2[:, kk], io[f"w_cmp2_{s}"][0]).then_inc(w_loaded, 16)
                eng.dma_start(pt[:, :], io["page_table"].rearrange("b (o n) -> o (b n)", o=1)).then_inc(table_ready, 16)
                for q in range(4):
                    for a in range(2):
                        rows = io["nsa_p"][(2 * q + a) * P:(2 * q + a + 1) * P, 0:256].rearrange("(p r) e -> p r e", r=2)
                        eng.dma_start(pg[64 * a:64 * a + 64, q], rows).then_inc(pair_loaded[q], 16)
                eng.wait_ge(table_ready, 16)
                load_pages(eng, 0)
                eng.wait_ge(keys_saved, NB + 1)
                eng.dma_start(io["kcT_s"], kcT[:, :, :].rearrange("p x c -> p (x c)")).then_inc(parked, 16)
                eng.wait_ge(values_saved, NB + 1)
                eng.dma_start(io["vc_s"][:, :, 0, :], vc[:, :, 0, :]).then_inc(parked, 16)
                eng.dma_start(io["vc_s"][0:P - 1, :, 1, :], vc[0:P - 1, :, 1, :]).then_inc(parked, 16)
                eng.wait_ge(parked, 48)

            def phases(eng, first, phase, last):
                first()
                phase(None, 1, 0, 0, False)
                phase(0, 0, 1, 1, None)
                with eng.Fori(0, NB // 2 - 1) as i:
                    for u in (1, 0):
                        b = i * 2 + 2 - u
                        phase(b, u, b + 1, 1 - u, b - 1)
                phase(NB - 1, 1, None, None, NB - 2)
                last(NB - 1)

            blocks_of = lambda b: NCP if b is None else NCS

            @block.tensor
            def _(eng):
                eng.wait_ge(w_loaded, 16 * 6)
                for kk in range(2):
                    mm = eng.transpose(pv[:, kk * 16:kk * 16 + 16], pe[:, kk, :], ident[0:16, 0:16])
                mm.then_inc(pe_turned, 1)
                eng.wait_ge(pe_saved, 1)
                for kk in range(2):
                    for m in range(16):
                        mm = eng.matmul(ph[:, 0, kk:kk + 1], w1[:, kk, m // 8, m % 8, :], peT[:, kk, m:m + 1], start=(m == 0), stop=(m == 15))
                mm.then_inc(hidden_done, 1)
                eng.wait_ge(bias_saved, 1)

                def turn_pair(b, q):
                    slot = q if b is None else (4 + q) % RING
                    if b is None:
                        eng.wait_ge(pair_loaded[slot], 32)
                    else:
                        k = b * 32 + 16 * ((4 + q) // RING + (0 if slot < 4 else 1))
                        eng.wait_ge(pair_loaded[slot], k + (32 if slot < 4 else 0))
                        eng.wait_ge(second_loaded[slot], k)
                    if not (b is None and q < 2):
                        eng.wait_ge(saved[q % 2], 1 if b is None else b * 8 + 2 + q // 2)
                    for v in range(4):
                        mm = eng.transpose(px[:, q % 2, v * P:(v + 1) * P], pg[:, slot, v % 2, (v // 2) * P:(v // 2 + 1) * P], ident[:, :])
                    mm.then_inc(turned, 1)

                def keys_product(b):
                    n = 2 * blocks_of(b)
                    eng.wait_ge(gelu_done, 1 if b is None else b * 2 + 3)
                    if b is not None:
                        eng.wait_ge(keys_saved, b + 1)
                    eng.matmul(pk[:, 0:n], w2[:, 0, :], hid[:, 0, 0:n], start=True, stop=True).then_inc(block_done, 1)

                def values_product(b):
                    blocks = blocks_of(b)
                    eng.wait_ge(gelu_done, 2 if b is None else b * 2 + 4)
                    if b is not None:
                        eng.wait_ge(values_saved, b + 1)
                    for v in range(2):
                        for c in range((blocks + P - 1) // P):
                            r = min(P, blocks - c * P)
                            mm = eng.matmul(pv[0:r, (2 * v + c) * HD:(2 * v + c + 1) * HD], hid[:, 1, v * blocks + c * P:v * blocks + c * P + r], w2[:, 1, :], start=True, stop=True)
                    mm.then_inc(block_done, 1)

                def phase(b, u, nb, nu, before):
                    blocks = blocks_of(b)
                    for kk in range(2):
                        for e in range(2):
                            eng.wait_ge(saved[e], 2 if b is None else b * 8 + 10)
                        if b is not None:
                            eng.wait_ge(gelu_done, b * 2 + kk + 1)
                        out = ph[:, kk, 0:2 * blocks].rearrange("p (v c) -> p v c", v=2)
                        for m in range(16):
                            half, j = m // 8, m % 8
                            src = xt[:, u, 2 * kk:2 * kk + 2, :].rearrange("p v (c j) -> p v c j", j=8)[:, :, half:half + blocks, j]
                            mm = eng.matmul(out, w1[:, kk, half, j, :], src, start=(m == 0), stop=(m == 15))
                            if m == 15:
                                mm.then_inc(hidden_done, 1)
                            if m % 2 == 1 and nb is not None:
                                turn_pair(nb, 8 * kk + m // 2)
                            if (kk, m) == (0, 3) and before is not False:
                                values_product(before)
                            if (kk, m) == (1, 7):
                                keys_product(b)

                def first():
                    for q in range(4):
                        turn_pair(None, q)
                phases(eng, first, phase, values_product)

            def save_pair(eng, b, u, q):
                eng.wait_ge(turned, (q if b is None else b * PAIRS + 4 + q) + 1)
                if q < 2 and b is not None:
                    eng.wait_ge(hidden_done, b * 2 + 1)
                for r in range(2):
                    for j in range(2):
                        out = xt[64 * r:64 * r + 64, u, j:4:2, q * P:(q + 1) * P]
                        src = px[64 * j:64 * j + 64, q % 2, :].rearrange("p (k r c) -> p k r c", k=2, r=2)[:, :, r, :]
                        ins = eng.tensor_copy(out, src) if q % 2 == 0 else eng.activation(out, src, ACT.Copy)
                ins.then_inc(saved[q % 2], 1)

            @block.vector
            def _(eng):
                eng.memset(vcp[:, :, HD:HD + 1], 1.0)
                for part in (kcp_hi, kcp_lo):
                    eng.tensor_scalar(part[:, :, NCP:64], g["ident"][0:HD, 0:KVH].unsqueeze(2), 0.0, None, ALU.mult)
                eng.wait_ge(pe_turned, 1)
                eng.tensor_copy(peT[:, :, :], pv[:, 0:32].rearrange("p (k m) -> p k m", k=2)).then_inc(pe_saved, 1)
                eng.wait_ge(hidden_done, 1)
                eng.tensor_copy(peb[:, :], ph[:, 0, 0:2]).then_inc(bias_saved, 1)

                def save_keys(b):
                    eng.wait_ge(block_done, 1 if b is None else b * 2 + 3)
                    keys = pk[:, 0:2 * blocks_of(b)].rearrange("p (v c) -> p v c", v=2)
                    if b is None:
                        eng.tensor_copy(kcp_hi[:, :, 0:NCP], keys)
                        eng.drain()
                        eng.tensor_tensor(kcp_lo[:, :, 0:NCP], keys, kcp_hi[:, :, 0:NCP].bitcast(F32), ALU.subtract).then_inc(keys_saved, 1)
                    else:
                        eng.tensor_copy(kcT[:, bass.ds(b * 2, 2), :], keys).then_inc(keys_saved, 1)

                def save_values(b):
                    eng.wait_ge(block_done, 2 if b is None else b * 2 + 4)
                    if b is None:
                        src = pv[0:NCP, 0:256].rearrange("p (v c d) -> p v c d", v=2, c=2)[:, :, 0, :]
                        eng.tensor_copy(vcp[0:NCP, :, 0:HD], src).then_inc(values_saved, 1)
                    else:
                        vals = pv[:, 0:256].rearrange("p (v c d) -> p v c d", v=2, c=2)
                        eng.tensor_copy(vc[:, bass.ds(b * 2, 2), 0, :], vals[:, :, 0, :])
                        eng.tensor_copy(vc[0:P - 1, bass.ds(b * 2, 2), 1, :], vals[0:P - 1, :, 1, :]).then_inc(values_saved, 1)

                def phase(b, u, nb, nu, before):
                    for q in range(0, PAIRS, 2):
                        if nb is not None:
                            save_pair(eng, nb, nu, q)
                        if q == 0 and before is not False:
                            save_values(before)
                        if q == 10:
                            save_keys(b)

                def first():
                    for q in (0, 2):
                        save_pair(eng, None, 1, q)
                phases(eng, first, phase, save_values)

            @block.scalar
            def _(eng):
                eng.wait_ge(bias_saved, 1)

                def phase(b, u, nb, nu, before):
                    for q in range(1, PAIRS, 2):
                        if nb is not None:
                            save_pair(eng, nb, nu, q)
                        if q in (7, 15):
                            kk, n = q // 8, 2 * blocks_of(b)
                            eng.wait_ge(hidden_done, 2 + kk if b is None else b * 2 + 4 + kk)
                            if b is not None:
                                eng.wait_ge(block_done, b * 2 + 1 + kk)
                            eng.activation(hid[:, kk, 0:n], ph[:, kk, 0:n], ACT.Gelu_apprx_tanh, bias=peb[:, kk:kk + 1]).then_inc(gelu_done, 1)

                def first():
                    for q in (1, 3):
                        save_pair(eng, None, 1, q)
                phases(eng, first, phase, lambda b: None)


def attend(nc, io, g):
    with ExitStack() as ctx:
        sb = lambda n, s, t=F32: ctx.enter_context(nc.sbuf_tensor(n, s, t))
        ps = lambda n, s, t=F32: ctx.enter_context(nc.psum_tensor(n, s, t))
        sem = g["sem"]
        RING, NPR = 4, 4
        kT = sb("kT_sel_win", [P, 2, KVH, SEQ], F32R)
        vx = sb("v_sel_win", [P, 2, TILES, KVH, HD + 1])
        qn = sb("q_nsa_hi_twice", [P, 2, SEQ], F32R)
        qs = sb("q_sb_hi_twice", [P, 2, SEQ], F32R)
        qn_lo = sb("q_nsa_lo", [HD, 2, SEQ], F32R)
        qs_lo = sb("q_sb_lo", [HD, 2, SEQ], F32R)
        ks = sb("k_sb", [P, 2, SEQ], F32R)
        vs = sb("v_sb", [P, 2, TILES, HD])
        masksf = sb("masks_f", [P, 3, P])
        cmaskf = sb("cmask_f", [P, TILES, 64])
        masks = sb("masks_b", [P, 3, P], BF16)
        cmask = sb("cmask_b", [P, TILES, 64], BF16)
        identb = sb("ident_b", [P, P], BF16)
        rowok = sb("rowok", [P, 1])
        nm = sb("minus_max", [P, 64])
        pr = sb("probs", [P, 2, SEQ])
        prs = sb("stick_weights", [P, SEQ])
        prT = sb("probs_turned", [P, 2, TILES, P])
        fac = sb("factor", [P, 64, 2])
        S = ps("scores", [P, 2, 1024])
        PT = ps("turned_ps", [P, 2, 512])
        O = ps("out_ps", [P, 512])
        DB = ps("decode_ps", [P, 512])

        late = g["late"]
        kr = late[:, 0:2048].rearrange("p (r n) -> p r n", r=RING)
        vr = late[:, 2048:4096].rearrange("p (r n) -> p r n", r=RING)
        zs, lg, rl, dd = (late[:, 4096 + i * SEQ:4096 + (i + 1) * SEQ] for i in range(4))
        PER = 16 * NPAGE // RING
        prod = late[:, 8192:10240].rearrange("p (r n) -> p r n", r=NPR)
        qb = late[:, 10240:11264].rearrange("p (r n) -> p r n", r=2)
        zd = sb("z_dec", [P, 2, NH, NPAGE])
        lgd = sb("log_dec", [P, NH * NPAGE])
        rld = sb("relu_dec", [P, NH * NPAGE])
        later = sb("later_pages", [P, NH * NPAGE])
        keep = sb("keep", [P, NH, NPAGE])
        ddd = sb("logw_dec", [P, NH * NPAGE])
        aw = sb("weights_dec", [P, NH, NPAGE])
        tri = sb("tri", [P, P])
        ones = sb("ones_dec", [P, P])
        diag = sb("diag", [NH, 512])
        om = sb("o_masked", [NH, 512])
        orow = sb("o_row", [1, 512])
        const_loaded, consts_set, pool_steps = sem("const_loaded"), sem("consts_set"), sem("pool_steps")
        head_loaded = [sem("head_loaded0"), sem("head_loaded1")]
        values_loaded = [sem("values_loaded0"), sem("values_loaded1")]
        keys_loaded = sem("sel_win_keys_loaded")
        names = ("qk_done", "max_done_a", "z_copied", "log_done", "relu_done", "scan_done", "logw_ready", "exp_done", "stick_done",
                 "turned_a", "pv_done", "out_done", "steps_a")
        qk_done, max_done, z_copied, log_done, relu_done, scan_done, logw_ready, exp_done, stick_done, turned, pv_done, out_done, steps = map(sem, names)
        saved = [sem("p_saved_v"), sem("p_saved_a")]
        k_loaded = [sem(f"k_loaded{r}") for r in range(RING)]
        v_loaded = [sem(f"v_loaded{r}") for r in range(RING)]
        q_loaded = [sem("q_loaded0"), sem("q_loaded1")]
        names = ("multiplied", "reduced", "logged", "softplus_done", "cum_done", "logw_done", "weights_done",
                 "v_used", "o_masked_s", "o_row_done", "o_row_saved", "row_stored")
        multiplied, reduced, logged, sp_done, cum_done, logw_done, weights_done, v_used, masked, row_done, row_saved, row_stored = map(sem, names)
        ident, gates, mix, kcp_hi, kcp_lo, vcp, pt = (g[k] for k in ("ident", "gates", "mix", "kcp_hi", "kcp_lo", "vcp", "pt"))

        FRONT = []
        for u in range(2):
            for t in range(TILES):
                for kind in ("sb", "cmp", "sel", "win"):
                    lo = max(0, t - 4) if kind == "win" else 0
                    FRONT.append((u, t, kind, lo, 1 if kind == "cmp" else t + 1 - lo))
        U = len(FRONT)
        H = U // 2
        front_of = lambda m: m + 1 if m % 4 < 3 else m - 3
        back_of = lambda f: f - 1 if f % 4 else f + 3
        BACK = [FRONT[front_of(m)] for m in range(U)]
        G0 = [0]
        for x in BACK:
            G0.append(G0[-1] + (x[4] + 3) // 4)
        G = G0[-1]
        assert G % 2 == 0
        soft = lambda f: f - (f // 4 + 1)
        NSOFT, NSTICK = U * 3 // 4, U // 4
        width = lambda x: NCP if x[2] == "cmp" else x[4] * P

        def spread(counts):
            ends = [sum(counts[:s // 4]) + -(-counts[s // 4] * (s % 4 + 1) // 4) for s in range(H)]
            return [list(range(([0] + ends)[s], ends[s])) for s in range(H)]
        KPAGES, VPAGES = spread((2, 2, 3, 4, 5, 5, 5, 6)), spread((0, 3, 3, 4, 5, 5, 6, 6))
        zero = lambda N: isinstance(N, int) and N == 0

        def turns(eng, body, tail):
            body(0, 0)
            with eng.Fori(1, 3) as i:
                body(i, i - 1)
            body(3, 1)
            for s in range(H):
                tail(s)

        with nc.Block() as block:
            @block.sync
            def _(eng):
                def load_values(h, u):
                    v = io["sb_p"].rearrange("(t p) (c h d) -> c p t h d", p=P, c=2, h=NH)[1][:, :, bass.ds(h, 1), :]
                    eng.dma_start(vs[:, u], v.rearrange("p t o d -> p t (o d)")).then_inc(values_loaded[u], 16)

                eng.dma_start(masksf[:, :, :], io["c_masks"]).then_inc(const_loaded, 16)
                eng.dma_start(cmaskf[:, :, :], io["c_cmask"]).then_inc(const_loaded, 16)
                eng.dma_start(rowok[:, :], io["c_rowok"]).then_inc(const_loaded, 16)
                load_values(0, 0)
                for j in range(2):
                    eng.dma_start(vx[:, 0, :, j, 0:HD], io["nsa_p"].rearrange("(t p) e -> p t e", p=P)[:, :, 384 + j * HD:448 + j * HD]).then_inc(const_loaded, 16)
                    eng.dma_start(vx[:, 1, :, j, 0:HD], io["win_p"].rearrange("(t p) e -> p t e", p=P)[:, :, 128 + j * HD:192 + j * HD]).then_inc(const_loaded, 16)
                eng.dma_start(tri[:, :], io["c_tri"]).then_inc(const_loaded, 16)
                eng.dma_start(diag[:, :], io["c_diag"].rearrange("a h d -> a (h d)")).then_inc(const_loaded, 16)
                load_values(1, 1)
                eng.dma_start(io["win_p_out"], io["win_p"][SEQ - WINDOW:SEQ, :]).then_inc(row_stored, 16)

                def key_page(h, u, p):
                    if p == 0:
                        if not zero(h // 2 if isinstance(h, int) else h):
                            eng.wait_ge(reduced, h * NPAGE - NPAGE)
                        eng.dma_start(qb[:, u], io["sbq_s"][bass.ds(h, 1), :].rearrange("o n -> (o n)").partition_broadcast(P)).then_inc(q_loaded[u], 16)
                    if not (zero(h) and p < RING):
                        eng.wait_ge(multiplied, h * NPAGE + p - RING + 1)
                    page = eng.value_load(pt[0:1, bass.ds(h * NPAGE + p, 1)], min_val=0, max_val=NPOOL - 1)
                    eng.dma_start(kr[:, p % RING], io["cache_sb"][bass.ds(page * P, P), 0, :]).then_inc(k_loaded[p % RING], 16)

                def value_page(b, p):
                    if not (zero(b) and p < RING):
                        eng.wait_ge(v_used, b * NPAGE + p - RING + 1)
                    page = eng.value_load(pt[0:1, bass.ds(b * NPAGE + p, 1)], min_val=0, max_val=NPOOL - 1)
                    eng.dma_start(vr[:, p % RING], io["cache_sb"][bass.ds(page * P, P), 1, :]).then_inc(v_loaded[p % RING], 16)

                def store_row(b):
                    eng.wait_ge(row_saved, b + 1)
                    eng.dma_start(io["osb_s"][bass.ds(b, 1), :], orow[:, :]).then_inc(row_stored, 16)

                def body(N, kv):
                    for u in range(2):
                        h = N * 2 + u
                        for p in range(NPAGE):
                            key_page(h, u, p)
                            if not zero(h):
                                value_page(h - 1, p)
                            if p == 5 and not zero(N):
                                store_row(h - 2)
                            if p == 6 and not zero(h) and not (isinstance(h, int) and h == NH - 1):
                                eng.wait_ge(pv_done, h * H)
                                load_values(h + 1, 1 - u)

                def tail(s):
                    value_page(NH - 1, s)
                    if s == 5:
                        store_row(NH - 2)

                turns(eng, body, tail)
                store_row(NH - 1)
                eng.wait_ge(row_stored, 16 * (NH + 1))

            @block.gpsimd
            def _(eng):
                heads = {part: io[part].rearrange("(h d) t -> h d t", d=HD) for part in ("T_hi", "T_lo")}
                turned_rows = {part: io[part].rearrange("(h d) t -> d h t", d=HD) for part in ("T_hi", "T_lo")}

                def load_head(h, u, parts=slice(0, 8)):
                    for dst, part, t in ((qs[0:HD], "T_hi", T_QS), (qs[HD:P], "T_hi", T_QS), (qs_lo, "T_lo", T_QS),
                                         (ks[0:HD], "T_hi", T_KB), (ks[HD:P], "T_lo", T_KB),
                                         (qn[0:HD], "T_hi", T_QN), (qn[HD:P], "T_hi", T_QN), (qn_lo, "T_lo", T_QN))[parts]:
                        eng.dma_start(dst[:, u], heads[part][bass.ds(h + t, 1)].rearrange("o d t -> d (o t)")).then_inc(head_loaded[u], 16)

                load_head(0, 0)
                for i, t in enumerate((T_KS, T_KW)):
                    eng.dma_start(kT[0:HD, i], turned_rows["T_hi"][:, t:t + 2, :]).then_inc(keys_loaded, 16)
                    eng.dma_start(kT[HD:P, i], turned_rows["T_lo"][:, t:t + 2, :]).then_inc(keys_loaded, 16)
                load_head(1, 1)

                def multiply(h, u, p):
                    if p == 0:
                        eng.wait_ge(q_loaded[u], (h - u) * 8 + 16)
                    eng.wait_ge(k_loaded[p % RING], h * PER + 16 * (p // RING) + 16)
                    if not (zero(h) and p < NPR):
                        eng.wait_ge(reduced, h * NPAGE + p - NPR + 1)
                    eng.tensor_tensor(prod[:, p % NPR], kr[:, p % RING], qb[:, u], ALU.mult).then_inc(multiplied, 1)

                def body(N, kv):
                    for s in range(U):
                        for p in KPAGES[0] + KPAGES[1] if s % H == 0 else (KPAGES + [[]])[s % H + 1]:
                            multiply(N * 2 + s // H, s // H, p)
                        if 6 <= s % H < 14 and not (zero(N) and s < H) and not (isinstance(N, int) and N == 3 and s > H):
                            h, i = N * 2 + s // H, s % H - 6
                            if i == 0:
                                eng.wait_ge(pv_done, h * H)
                            load_head(h + 1, 1 - s // H, slice(i, i + 1))
                        w, k = width(FRONT[s - s % 4]), N * NSTICK + s // 4
                        if s % 4 == 1:
                            eng.wait_ge(z_copied, k + 1)
                            if not (zero(N) and s < 4):
                                eng.wait_ge(scan_done, k)
                            eng.sem_inc(pool_steps, 1)
                            eng.tensor_scalar(rl[:, 0:w], zs[:, 0:w], 0.0, None, ALU.max).then_inc(relu_done, 1)
                        if s % 4 == 3:
                            eng.wait_ge(scan_done, k + 1)
                            eng.tensor_tensor(dd[:, 0:w], zs[:, 0:w], dd[:, 0:w], ALU.subtract).then_inc(logw_ready, 1)
                turns(eng, body, lambda s: None)

            @block.tensor
            def _(eng):
                eng.wait_ge(const_loaded, 16 * 9)
                eng.wait_ge(keys_loaded, 16 * 4)
                eng.wait_ge(consts_set, 1)

                def scores(N, kv, s):
                    u, t, kind, lo, tiles = FRONT[s]
                    if s % H == 0:
                        eng.wait_ge(head_loaded[u], N * 128 + 128)
                        eng.wait_ge(values_loaded[u], N * 16 + 16)
                    if not (zero(N) and s < 2):
                        f = s - 2
                        if f % 4 == 0:
                            eng.wait_ge(z_copied, N * NSTICK + f // 4 + 1)
                        else:
                            eng.wait_ge(exp_done, N * NSOFT + soft(f) + 1)
                    q = (qs if kind == "sb" else qn)[:, u, t * P:(t + 1) * P]
                    q_lo = (qs_lo if kind == "sb" else qn_lo)[:, u, t * P:(t + 1) * P]
                    if kind == "cmp":
                        c_hi, c_lo = (x[:, bass.ds(kv, 1), :].rearrange("p o c -> p (o c)") for x in (kcp_hi, kcp_lo))
                        eng.matmul(S[:, s % 2, 0:64], q[0:HD], c_hi, start=True, stop=False)
                        eng.matmul(S[:, s % 2, 0:64], q[0:HD], c_lo, start=False, stop=False)
                        eng.matmul(S[:, s % 2, 0:64], q_lo, c_hi, start=False, stop=False)
                        eng.matmul(S[:, s % 2, 0:64], identb[:, :], cmask[:, t, :], start=False, stop=True).then_inc(qk_done, 1)
                        return
                    w = tiles * P
                    edges = [((tiles - 1) * P, 1 if kind == "sb" else 0)]
                    if kind == "win" and t >= 4:
                        edges.append((0, 2))
                    for a in range(0, w, 512):
                        e = min(w, a + 512)
                        if kind == "sb":
                            k = ks[:, u, a:e]
                        else:
                            k = kT[:, 0 if kind == "sel" else 1, bass.ds(kv, 1), lo * P + a:lo * P + e].rearrange("p o c -> p (o c)")
                        own = [x for x in edges if a <= x[0] < e]
                        eng.matmul(S[:, s % 2, a:e], q, k, start=True, stop=False)
                        mm = eng.matmul(S[:, s % 2, a:e], q_lo, k[0:HD], start=False, stop=not own)
                        for z, (at, m) in enumerate(own):
                            mm = eng.matmul(S[:, s % 2, at:at + P], identb[:, :], masks[:, m, :], start=False, stop=z == len(own) - 1)
                    mm.then_inc(qk_done, 1)

                def transposes(N, m):
                    u, t, kind, lo, tiles = BACK[m % U]
                    f = front_of(m)
                    src = prs if kind == "sb" else pr[:, f % 2]
                    if kind == "sb":
                        eng.wait_ge(stick_done, N * NSTICK + m // 4 + 1)
                    else:
                        eng.wait_ge(exp_done, N * NSOFT + soft(f) + 1)
                    base, first = (m // U) * G, G0[m % U]
                    for b in range(first, G0[m % U + 1]):
                        if not (zero(N) and b < 2 and m >= 0):
                            eng.wait_ge(saved[b % 2], N * (G // 2) + (base + b) // 2)
                        if kind == "cmp":
                            eng.sem_inc(steps, 1)
                        for c in range(4 * (b - first), min(tiles, 4 * (b - first) + 4)):
                            w = min(P, width(BACK[m % U]) - c * P)
                            mm = eng.transpose(PT[0:w, b % 2, (c % 4) * P:(c % 4 + 1) * P], src[:, c * P:c * P + w], ident[:, :])
                        mm.then_inc(turned, 1)

                def product(N, kv, m):
                    u, t, kind, lo, tiles = BACK[m % U]
                    base = (m // U) * G
                    for b in range(G0[m % U], G0[m % U + 1]):
                        eng.wait_ge(saved[b % 2], N * (G // 2) + (base + b) // 2 + 1)
                    if not (zero(N) and m == 0):
                        eng.wait_ge(out_done, N * U + m)
                    for c in range(tiles):
                        if kind == "cmp":
                            l, r = prT[0:NCP, m % 2, 0, :], vcp[0:NCP, bass.ds(kv, 1), :].rearrange("p o d -> p (o d)")
                        elif kind == "sb":
                            l, r = prT[:, m % 2, c, :], vs[:, u, c, :]
                        else:
                            l, r = prT[:, m % 2, c, :], vx[:, 0 if kind == "sel" else 1, lo + c, bass.ds(kv, 1), :].rearrange("p o d -> p (o d)")
                        mm = eng.matmul(O[:, 0:HD if kind == "sb" else HD + 1], l, r, start=c == 0, stop=c == tiles - 1)
                    mm.then_inc(pv_done, 1)

                def sample(h, s):
                    if s == 1 and not zero(h) and not (isinstance(h, int) and h < 2):
                        eng.wait_ge(masked, h - 1)
                        eng.sem_inc(steps, 1)
                        eng.matmul(DB[0:1, :], ones[0:NH, 0:1], om[:, :], start=True, stop=True).then_inc(row_done, 1)
                    if s == 2 and not zero(h) and not (isinstance(h, int) and h > NH):
                        eng.wait_ge(sp_done, h)
                        if not (isinstance(h, int) and h < 2):
                            eng.wait_ge(row_saved, h - 1)
                        eng.matmul(DB[:, 0:NH * NPAGE], tri[:, :], rld[:, :], start=True, stop=False)
                        eng.matmul(DB[:, 0:NH * NPAGE], ones[:, :], later[:, :], start=False, stop=True).then_inc(cum_done, 1)
                    if not zero(h) and not (isinstance(h, int) and h > NH):
                        for p in VPAGES[s]:
                            if p == 0:
                                eng.wait_ge(weights_done, h)
                            eng.wait_ge(v_loaded[p % RING], h * PER - PER + 16 * (p // RING) + 16)
                            eng.matmul(DB[0:NH, :], aw[:, :, NPAGE - 1 - p], vr[:, p % RING], start=p == 0, stop=p == NPAGE - 1).then_inc(v_used, 1)

                def body(N, kv):
                    for s in range(U):
                        scores(N, kv, s)
                        kvb = lambda m: kv if m >= 0 else (1 if isinstance(N, int) else 0)
                        if not (zero(N) and s < 2):
                            transposes(N, s - 2)
                        if not (zero(N) and s < 3):
                            product(N, kvb(s - 3), s - 3)
                        sample(N * 2 + s // H, s % H)

                def tail(s):
                    if s < 2:
                        transposes(4, s - 2)
                    if s < 3:
                        product(4, 1, s - 3)
                    sample(NH, s)
                turns(eng, body, tail)
                sample(NH + 1, 1)

            def save_groups(eng, N, m, e):
                tiles = BACK[m % U][4]
                base, first = (m // U) * G, G0[m % U]
                for b in range(first, G0[m % U + 1]):
                    if b % 2 != e:
                        continue
                    eng.wait_ge(turned, N * G + base + b + 1)
                    if not (zero(N) and m in (0, 1)):
                        eng.wait_ge(pv_done, N * U + m - 1)
                    c = 4 * (b - first)
                    k, w = min(4, tiles - c), min(P, width(BACK[m % U]))
                    out = prT[0:w, m % 2, c:c + k, :]
                    src = PT[0:w, b % 2, 0:k * P].rearrange("p (c q) -> p c q", q=P)
                    if e == 0:
                        eng.tensor_copy(out, src).then_inc(saved[0], 1)
                    else:
                        eng.activation(out, src, ACT.Copy).then_inc(saved[1], 1)

            @block.scalar
            def _(eng):
                eng.preload_act_table_set("natural_log_exp_and_others")

                def exps(N, s):
                    x, w = FRONT[s], width(FRONT[s])
                    if x[2] == "sb":
                        return
                    eng.wait_ge(max_done, N * NSOFT + soft(s) + 1)
                    if not (zero(N) and s < 3):
                        m = back_of(s - 2) if (s - 2) % 4 else back_of(s - 3)
                        eng.wait_ge(turned, N * G + (m // U) * G + G0[m % U + 1])
                    eng.activation(pr[:, s % 2, 0:w], S[:, s % 2, 0:w], ACT.Exp, bias=nm[:, s:s + 1]).then_inc(exp_done, 1)

                def stick(N, s):
                    w, k = width(FRONT[s - s % 4]), N * NSTICK + s // 4
                    if s % 4 == 0:
                        eng.wait_ge(z_copied, k + 1)
                        if not (zero(N) and s < 4):
                            eng.wait_ge(scan_done, k)
                        eng.activation(lg[:, 0:w], zs[:, 0:w], ACT.Abs)
                    elif s % 4 == 1:
                        eng.drain()
                        eng.activation(lg[:, 0:w], lg[:, 0:w], ACT.Exp, scale=-1.0)
                    elif s % 4 == 2:
                        eng.drain()
                        eng.activation(lg[:, 0:w], lg[:, 0:w], ACT.Ln, bias=1.0).then_inc(log_done, 1)
                    else:
                        eng.wait_ge(logw_ready, k + 1)
                        if not (zero(N) and s < 4):
                            m = back_of(s - 7)
                            eng.wait_ge(turned, N * G + (m // U) * G + G0[m % U + 1])
                        eng.activation(prs[:, 0:w], dd[:, 0:w], ACT.Exp).then_inc(stick_done, 1)

                def sample(h, u, s):
                    if s == 0 and not zero(h) and not (isinstance(h, int) and h > NH):
                        eng.wait_ge(reduced, h * NPAGE)
                        z = zd[:, 1 - u, :, :].rearrange("p h n -> p (h n)")
                        eng.activation(lgd[:, :], z, ACT.Abs)
                        eng.drain()
                        eng.activation(lgd[:, :], lgd[:, :], ACT.Exp, scale=-1.0)
                        eng.drain()
                        eng.activation(lgd[:, :], lgd[:, :], ACT.Ln, bias=1.0).then_inc(logged, 1)
                    if s == 2 and not (isinstance(h, int) and h < 2):
                        eng.wait_ge(row_done, h - 1)
                        eng.wait_ge(row_stored, h * 16 - 16)
                        eng.activation(orow[:, :], DB[0:1, :], ACT.Copy).then_inc(row_saved, 1)
                    if s == 3 and not zero(h) and not (isinstance(h, int) and h > NH):
                        eng.wait_ge(logw_done, h)
                        if not (isinstance(h, int) and h < 2):
                            eng.wait_ge(v_used, h * NPAGE - NPAGE)
                        eng.activation(aw[:, :, :].rearrange("p h n -> p (h n)"), ddd[:, :], ACT.Exp).then_inc(weights_done, 1)

                def body(N, kv):
                    for s in range(U):
                        exps(N, s)
                        if not (zero(N) and s < 2):
                            save_groups(eng, N, s - 2, 1)
                        stick(N, s)
                        sample(N * 2 + s // H, s // H, s % H)

                def tail(s):
                    if s < 2:
                        save_groups(eng, 4, s - 2, 1)
                    sample(NH, 0, s)
                turns(eng, body, tail)
                sample(NH + 1, 1, 2)

            @block.vector
            def _(eng):
                eng.memset(ones[:, :], 1.0)
                eng.memset(keep[:, :, 1:NPAGE], 1.0)
                eng.memset(keep[:, :, 0:1], 0.0)
                eng.wait_ge(const_loaded, 16 * 9)
                eng.memset(vx[:, :, :, :, HD:HD + 1], 1.0)
                eng.tensor_copy(identb[:, :], ident[:, :])
                eng.tensor_copy(masks[:, :, :], masksf[:, :, :])
                eng.tensor_copy(cmask[:, :, :], cmaskf[:, :, :]).then_inc(consts_set, 1)

                def stat(N, s):
                    x, w = FRONT[s], width(FRONT[s])
                    z = S[:, s % 2, 0:w]
                    eng.wait_ge(qk_done, N * U + s + 1)
                    if x[2] != "sb":
                        eng.tensor_reduce(nm[:, s:s + 1], z, AX.X, ALU.max, negate=True).then_inc(max_done, 1)
                        return
                    if not (zero(N) and s < 4):
                        eng.wait_ge(logw_ready, N * NSTICK + s // 4)
                    eng.tensor_copy(zs[:, 0:w], z).then_inc(z_copied, 1)

                def scan(N, s):
                    w, k = width(FRONT[s - s % 4]), N * NSTICK + s // 4
                    rev = lambda a: a[:, w - 1::-1]
                    eng.wait_ge(log_done, k + 1)
                    eng.wait_ge(relu_done, k + 1)
                    if not (zero(N) and s < 4):
                        eng.wait_ge(stick_done, k)
                    eng.tensor_tensor_scan(rev(dd), rev(lg), rev(rl), 0.0, ALU.add, ALU.add).then_inc(scan_done, 1)

                def out(N, m):
                    u, t, kind, lo, tiles = BACK[m % U]
                    o, h = O[:, 0:HD], N * 2 + (u if m >= 0 else u - 2)
                    eng.wait_ge(pv_done, N * U + m + 1)
                    if kind == "sb":
                        eng.tensor_copy(mix[:, t, bass.ds(h * HD + 512, HD)], o).then_inc(out_done, 1)
                        return
                    br = ("cmp", "sel", "win").index(kind)
                    f, f2 = fac[:, m % U, 0:1], fac[:, m % U, 1:2]
                    eng.reciprocal(f, O[:, HD:HD + 1])
                    eng.drain()
                    eng.tensor_tensor(f2, f, gates[:, t, bass.ds(h * 3 + br, 1)], ALU.mult)
                    eng.drain()
                    if kind == "cmp" and t == 0:
                        eng.tensor_tensor(f2, f2, rowok[:, :], ALU.mult)
                        eng.drain()
                    mx = mix[:, t, bass.ds(h * HD, HD)]
                    if kind == "cmp":
                        eng.tensor_scalar(mx, o, f2, None, ALU.mult).then_inc(out_done, 1)
                    else:
                        eng.scalar_tensor_tensor(mx, o, f2, mx, ALU.mult, ALU.add).then_inc(out_done, 1)

                def sample(h, u, s, keys):
                    live = not zero(h) and not (isinstance(h, int) and h > NH)
                    z = zd[:, 1 - u, :, :].rearrange("p h n -> p (h n)")
                    if s == 0 and not (isinstance(h, int) and h < 2):
                        eng.wait_ge(v_used, h * NPAGE - NPAGE)
                        eng.tensor_tensor(om[:, :], DB[0:NH, :], diag[:, :], ALU.mult).then_inc(masked, 1)
                    if s == 1 and live:
                        if not (isinstance(h, int) and h < 2):
                            eng.wait_ge(cum_done, h - 1)
                        eng.tensor_scalar(rld[:, :], z, 0.0, None, ALU.max)
                        eng.drain()
                        eng.wait_ge(logged, h)
                        eng.tensor_tensor(rld[:, :], rld[:, :], lgd[:, :], ALU.add)
                        eng.drain()
                        eng.tensor_tensor_scan(later[:, :], keep[:, :, :].rearrange("p h n -> p (h n)"), rld[:, :], 0.0, ALU.mult, ALU.add)
                        eng.drain()
                        eng.tensor_tensor(later[:, :], later[:, :], rld[:, :], ALU.subtract).then_inc(sp_done, 1)
                    if s == 2 and live:
                        if not (isinstance(h, int) and h < 2):
                            eng.wait_ge(weights_done, h - 1)
                        eng.wait_ge(cum_done, h)
                        eng.tensor_tensor(ddd[:, :], z, DB[:, 0:NH * NPAGE], ALU.subtract).then_inc(logw_done, 1)
                    for p in KPAGES[s] if keys else []:
                        eng.wait_ge(multiplied, h * NPAGE + p + 1)
                        eng.tensor_reduce(zd[:, u, :, NPAGE - 1 - p], prod[:, p % NPR].rearrange("p (h d) -> p h d", h=NH), AX.X, ALU.add).then_inc(reduced, 1)

                def body(N, kv):
                    for s in range(U):
                        stat(N, s)
                        if not (zero(N) and s < 2):
                            save_groups(eng, N, s - 2, 0)
                        if not (zero(N) and s < 3):
                            out(N, s - 3)
                        if s % 4 == 2:
                            scan(N, s)
                        sample(N * 2 + s // H, s // H, s % H, True)

                def tail(s):
                    if s < 2:
                        save_groups(eng, 4, s - 2, 0)
                    if s < 3:
                        out(4, s - 3)
                    sample(NH, 0, s, False)
                turns(eng, body, tail)
                sample(NH + 1, 1, 0, False)


def decode_nsa(nc, io, g):
    with ExitStack() as ctx:
        sb = lambda n, s, t=F32: ctx.enter_context(nc.sbuf_tensor(n, s, t))
        sem = lambda n: g["sem"](n)
        X = NB * KVH
        ident, pt = g["ident"], g["pt"]
        kcT = sb("kc_turned_d", [HD, X, NCS])
        vc = sb("vc_rows_d", [P, X, 2, HD])
        qT = sb("q_dec", [HD, NH, NB])
        oC = sb("o_cmp_dec", [GRP, X, HD])
        oS = sb("o_sel_dec", [GRP, X, HD])
        oW = sb("o_win_dec", [GRP, X, HD])
        block_id = sb("block_id", [1, X * 16], I32)
        with ExitStack() as c2:
            sb2 = lambda n, s, t=F32: c2.enter_context(nc.sbuf_tensor(n, s, t))
            ps2 = lambda n, s: c2.enter_context(nc.psum_tensor(n, s, F32))
            sc = sb2("sc_dec", [GRP, X, NCS])
            st = sb2("st_dec", [GRP, 4, X])
            pT = sb2("p_turned", [P, X * 2, GRP])
            pS = sb2("p_summed", [P, X * 2])
            pB = sb2("p_bcast", [P, X * 2, NBLK])
            ovl = sb2("overlap", [P, 2, NBLK])
            selc = sb2("sel_consts", [NBLK, 3, NBLK])
            ranks = sb2("ranks", [NBLK, 16])
            blk = sb2("blk", [NBLK, 2])
            pageof = sb2("pageof", [NPAGE, NBLK])
            pti = sb2("pt_int", [NPAGE, NB], I32)
            ptf = sb2("pt_float", [NPAGE, NB])
            ones = sb2("ones_sel", [NBLK, 2])
            R = sb2("score_rows", [NBLK, X, NBLK])
            Q1 = sb2("sel_tmp1", [NBLK, X, NBLK])
            Q2 = sb2("sel_tmp2", [NBLK, X, NBLK])
            col = sb2("score_col", [NBLK, X])
            rank = sb2("rank", [NBLK, X])
            base = sb2("block_addr", [NBLK, NB])
            OH = sb2("one_hot", [NBLK, X, 16])
            S4 = ps2("S4", [GRP, 4, 512])
            PA = ps2("PA", [P, 512])
            PB = ps2("PB", [P, 512])
            PR = ps2("PR", [NBLK, 2, 512])
            c_loaded, scored, copied, shifted, exped, probs, turned, turned_saved, summed, rows_done, bases_done, oh_done, ids_done, pt_set = map(
                lambda n: g["sem"](n),
                ("cd_loaded", "scored", "copied", "shifted", "exped", "probs", "p_turned_s", "p_turned_saved", "p_summed_s",
                 "rows_done", "bases_done", "oh_done", "ids_done", "pt_set"))
            with nc.Block() as block:
                @block.sync
                def _(eng):
                    for dst, src in ((kcT[:, :, :].rearrange("p x c -> p (x c)"), io["kcT_s"]), (vc[:, :, 0, :], io["vc_s"][:, :, 0, :]),
                                     (vc[0:P - 1, :, 1, :], io["vc_s"][0:P - 1, :, 1, :]),
                                     (qT[:, :, :], io["Ts"].rearrange("(h d) b -> d h b", d=HD)[:, 0:NH, :]), (ovl[:, :, :], io["c_ov"]),
                                     (selc[:, :, :], io["c_sel"]), (ranks[:, :], io["c_ranks"]), (blk[:, :], io["c_blk"]),
                                     (pageof[:, :], io["c_pageof"]), (pti[:, :], io["page_table"].rearrange("b n -> n b"))):
                        eng.dma_start(dst, src, allow_slow_non_contiguous=True).then_inc(c_loaded, 16)

                @block.tensor
                def _(eng):
                    eng.wait_ge(c_loaded, 16 * 10)
                    for x in range(X):
                        b, j = x // 2, x % 2
                        if x == 8:
                            eng.wait_ge(copied, 1)
                        mm = eng.matmul(S4[:, x // 2 % 4, j * NCS:(j + 1) * NCS], qT[:, GRP * j:GRP * j + GRP, b], kcT[:, x, :], start=True, stop=True)
                        if x % 8 == 7:
                            mm.then_inc(scored, 1)
                    eng.wait_ge(pt_set, 1)
                    eng.matmul(PB[0:NBLK, 0:NB], pageof[:, :], ptf[:, :], start=True, stop=True).then_inc(bases_done, 1)
                    eng.wait_ge(probs, 1)
                    for x in range(X):
                        for c in range(2):
                            w = P - c
                            mm = eng.transpose(PA[0:w, (2 * x + c) * GRP:(2 * x + c + 1) * GRP], sc[:, x, c * P:c * P + w], ident[0:GRP, 0:GRP])
                    mm.then_inc(turned, 1)
                    eng.wait_ge(turned_saved, 1)
                    for x in range(X):
                        for c in range(2):
                            w = P - c
                            mm = eng.matmul(S4[:, x // 8, x % 8 * HD:(x % 8 + 1) * HD], pT[0:w, 2 * x + c, :], vc[0:w, x, c, :], start=c == 0, stop=c == 1)
                    mm.then_inc(scored, 1)
                    eng.wait_ge(summed, 1)
                    for x in range(X):
                        for c in range(2):
                            w = P - c
                            mm = eng.matmul(PR[:, x // 8, x % 8 * HD:(x % 8 + 1) * HD], pB[0:w, 2 * x + c, :], ovl[0:w, c, :], start=c == 0, stop=c == 1)
                    mm.then_inc(rows_done, 1)
                    eng.wait_ge(oh_done, 1)
                    eng.matmul(PB[0:1, 0:X * 16], ones[:, 0:1], OH[:, :, :].rearrange("p x r -> p (x r)"), start=True, stop=True).then_inc(ids_done, 1)

                @block.scalar
                def _(eng):
                    eng.wait_ge(shifted, 1)
                    scf = sc[:, :, :].rearrange("p x c -> p (x c)")
                    eng.activation(scf, scf, ACT.Exp).then_inc(exped, 1)

                @block.vector
                def _(eng):
                    eng.memset(ones[:, :], 1.0)
                    eng.memset(pT[96:P, :, :], 0.0)
                    eng.wait_ge(c_loaded, 16 * 10)
                    eng.tensor_copy(ptf[:, :], pti[:, :]).then_inc(pt_set, 1)
                    for h in range(2):
                        eng.wait_ge(scored, h + 1)
                        eng.tensor_copy(sc[:, 8 * h:8 * h + 8, :].rearrange("p (a j) c -> p a (j c)", j=2), S4[:, :, 0:2 * NCS]).then_inc(copied, 1)
                    eng.drain()
                    bc = lambda a: a.unsqueeze(2).broadcast_to([GRP, X, NCS])
                    eng.tensor_reduce(st[:, 0, :], sc[:, :, :], AX.X, ALU.max)
                    eng.drain()
                    eng.tensor_tensor(sc[:, :, :], sc[:, :, :], bc(st[:, 0, :]), ALU.subtract).then_inc(shifted, 1)
                    eng.wait_ge(exped, 1)
                    eng.tensor_reduce(st[:, 1, :], sc[:, :, :], AX.X, ALU.add)
                    eng.drain()
                    eng.reciprocal(st[:, 2, :], st[:, 1, :])
                    eng.drain()
                    eng.tensor_tensor(sc[:, :, :], sc[:, :, :], bc(st[:, 2, :]), ALU.mult).then_inc(probs, 1)
                    eng.wait_ge(turned, 1)
                    pa = PA[:, 0:2 * X * GRP].rearrange("p (x c h) -> p x c h", c=2, h=GRP)
                    pt4 = pT[:, :, :].rearrange("p (x c) h -> p x c h", c=2)
                    eng.tensor_copy(pt4[:, :, 0, :], pa[:, :, 0, :])
                    eng.tensor_copy(pt4[0:P - 1, :, 1, :], pa[0:P - 1, :, 1, :]).then_inc(turned_saved, 1)
                    eng.drain()
                    eng.tensor_reduce(pS[:, :], pT[:, :, :], AX.X, ALU.add)
                    eng.drain()
                    eng.tensor_copy(pB[:, :, :], pS[:, :].unsqueeze(2).broadcast_to([P, 2 * X, NBLK])).then_inc(summed, 1)
                    eng.wait_ge(scored, 3)
                    eng.tensor_copy(oC[:, :, :].rearrange("p (a x) d -> p a (x d)", a=2), S4[:, 0:2, :])
                    eng.wait_ge(bases_done, 1)
                    eng.tensor_scalar(base[:, :], PB[0:NBLK, 0:NB], 2.0, None, ALU.mult)
                    eng.drain()
                    eng.tensor_scalar(base[:, :], base[:, :], blk[:, 1:2], None, ALU.add)
                    eng.wait_ge(rows_done, 1)
                    over = lambda a, n=NBLK: a.unsqueeze(1).broadcast_to([NBLK, X, n])
                    each = lambda a, n=NBLK: a.unsqueeze(2).broadcast_to([NBLK, X, n])
                    eng.tensor_tensor(R[:, :, :], PR[:, :, :].rearrange("p a (x j) -> p (a x) j", j=NBLK), over(selc[:, 2, :]), ALU.add)
                    eng.drain()
                    eng.tensor_tensor(Q1[:, :, :], R[:, :, :], over(selc[:, 0, :]), ALU.mult)
                    eng.drain()
                    eng.tensor_reduce(col[:, :], Q1[:, :, :], AX.X, ALU.add)
                    eng.drain()
                    eng.tensor_tensor(Q1[:, :, :], R[:, :, :], each(col[:, :]), ALU.is_gt)
                    eng.tensor_tensor(Q2[:, :, :], R[:, :, :], each(col[:, :]), ALU.is_equal)
                    eng.drain()
                    eng.tensor_tensor(Q2[:, :, :], Q2[:, :, :], over(selc[:, 1, :]), ALU.mult)
                    eng.drain()
                    eng.tensor_tensor(Q1[:, :, :], Q1[:, :, :], Q2[:, :, :], ALU.add)
                    eng.drain()
                    eng.tensor_reduce(rank[:, :], Q1[:, :, :], AX.X, ALU.add)
                    eng.drain()
                    eng.tensor_tensor(OH[:, :, :], each(rank[:, :], 16), over(ranks[:, :], 16), ALU.is_equal)
                    eng.drain()
                    b4 = base[:, :].unsqueeze(2).broadcast_to([NBLK, NB, 32])
                    o4 = OH[:, :, :].rearrange("p (b j) r -> p b (j r)", j=2)
                    eng.tensor_tensor(o4, o4, b4, ALU.mult).then_inc(oh_done, 1)
                    eng.wait_ge(ids_done, 1)
                    eng.tensor_copy(block_id[:, :], PB[0:1, 0:X * 16])

        ps = lambda n, s: ctx.enter_context(nc.psum_tensor(n, s, F32))
        kv = sb("kv_sel", [P, 4, 8, 2, HD])
        wk = sb("kv_win", [P, 2, 5, 256])
        qst = sb("q_now", [HD, 2, GRP])
        ksb = sb("keys_turned", [HD, 2, 1536])
        pd = sb("probs_dec", [GRP, 1536])
        nmx = sb("nmx_dec", [GRP, 2])
        sums = sb("sums_dec", [GRP, 4])
        pTs = sb("probs_dec_turned", [P, 13, GRP])
        KT = ps("KT", [HD, 2, 512])
        SD = ps("SD", [GRP, 4, 512])
        PT = ps("PTd", [P, 512])
        OD = ps("OD", [GRP, 512])
        kv_loaded = [sem(f"kv_loaded{u}") for u in range(4)]
        others_loaded = [sem(f"others_loaded{u}") for u in range(4)]
        SHARES = (list(range(0, 12, 2)), list(range(1, 12, 2)) + list(range(12, NSEL)))
        names = ("q_staged", "k_turned", "k_saved", "scores_done", "max_done", "exps_done", "pd_turned", "pd_saved", "od_done", "od_saved")
        q_staged, k_turned, k_saved, scores_done, max_done, exps_done, pd_turned, pd_saved, od_done, od_saved = map(sem, names)
        o_stored, steps = sem("o_stored"), sem("steps_d")
        NS, NW = NSEL * 64 + 1, WINDOW + 1
        KEYT = [(c, 64 * c * 2, P) for c in range(7)] + [(7, 896, 65)]

        def sequences(eng, body, ends):
            body(0, 0, 0, False)
            body(1, 1, 0, False)
            with eng.Fori(1, NB // 2 - ends) as i:
                for r in range(2):
                    body(i * 2 + r, r, i, False)
            if ends:
                body(NB - 2, 0, NB // 2 - 1, False)
                body(NB - 1, 1, NB // 2 - 1, True)

        def turns(eng, body):
            def both(b, r, uses, last):
                for j in range(2):
                    body(b, j, r, uses)
            sequences(eng, both, 0)

        def turns_ahead(eng, body):
            def both(b, r, uses, last):
                body(b, 0, r, (b, 1, r, uses))
                body(b, 1, r, None if last else (b + 1, 0, 1 - r, uses + r))
            sequences(eng, both, 1)

        def selected_blocks(eng, b, j, r, queue):
            x = b * 2 + j
            if not isinstance(b, int):
                eng.wait_ge(od_done, x - 3)
            for z in SHARES[queue]:
                bid = eng.value_load(block_id[0:1, bass.ds(x * 16 + z, 1)], min_val=0, max_val=2 * NPOOL - 1)
                src = io["cache_blocks"][bass.ds(bid, 1)].rearrange("o s u d -> (o s) u d")[:, 4 + j:8:2, :]
                h = 64 * (z % 2)
                eng.dma_start(kv[h:h + 64, 2 * r + j, z // 2], src).then_inc((kv_loaded, others_loaded)[queue][2 * r + j], 16)

        with nc.Block() as block:
            @block.gpsimd
            def _(eng):
                turns(eng, lambda b, j, r, uses: selected_blocks(eng, b, j, r, 1))

            @block.sync
            def _(eng):
                def body(b, j, r, uses):
                    x, u = b * 2 + j, 2 * r + j
                    selected_blocks(eng, b, j, r, 0)
                    new = io["nsa_s"][bass.ds(b, 1), :].rearrange("o (u d) -> o u d", d=HD)[:, 4 + j:8:2, :]
                    eng.dma_start(kv[64:65, u, 7], new).then_inc(kv_loaded[u], 16)
                    if j == 0:
                        if not isinstance(b, int):
                            eng.wait_ge(od_done, x - 2)
                        eng.dma_start(wk[:, r, 0:4, :], io["state"][bass.ds(b, 1)].rearrange("o (t p) e -> p (o t) e", p=P)).then_inc(kv_loaded[u], 16)
                        eng.dma_start(wk[0:1, r, 4, :], io["win_new"][bass.ds(b, 1), :]).then_inc(kv_loaded[u], 16)
                turns(eng, body)
                eng.wait_ge(od_saved, 2 * X)
                for br, o in enumerate((oC, oS, oW)):
                    dst = io["o_s"][br].rearrange("b (j h d) -> h (b j) d", j=2, h=GRP)
                    eng.dma_start(dst, o[:, :, :]).then_inc(o_stored, 16)
                eng.dma_start(io["win_s_out"][:, 0:WINDOW - 1, :], io["state"][:, 1:WINDOW, :]).then_inc(o_stored, 16)
                eng.dma_start(io["win_s_out"][:, WINDOW - 1, :], io["win_new"]).then_inc(o_stored, 16)
                eng.wait_ge(o_stored, 80)

            @block.tensor
            def _(eng):
                def steady(eng):
                    eng.sem_inc(steps, 1)

                def turn_keys(b, j, r, uses):
                    x, u = b * 2 + j, 2 * r + j
                    own = len(SHARES[0]) + (3 if j == 0 else 1)
                    eng.wait_ge(others_loaded[u], uses * 16 * len(SHARES[1]) + 16 * len(SHARES[1]))
                    eng.wait_ge(kv_loaded[u], uses * 16 * own + 16 * own)
                    for go in range(4):
                        if not (isinstance(b, int) and x == 0 and go < 2):
                            eng.wait_ge(k_saved, x * 4 + go - 1)
                        steady(eng)
                        if go < 2:
                            for c in range(4 * go, 4 * go + 4):
                                w = P if c < 7 else 65
                                mm = eng.transpose(KT[:, go % 2, c % 4 * P:c % 4 * P + w], kv[0:w, u, c, 0, :], ident[0:w, 0:w])
                        elif go == 2:
                            for c in range(4):
                                mm = eng.transpose(KT[:, 0, c * P:(c + 1) * P], wk[:, r, c, j * HD:(j + 1) * HD], ident[:, :])
                        else:
                            mm = eng.transpose(KT[:, 1, 0:1], wk[0:1, r, 4, j * HD:(j + 1) * HD], ident[0:1, 0:1])
                        mm.then_inc(k_turned, 1)

                def body(b, j, r, after):
                    first = isinstance(b, int) and b == 0
                    x = b * 2 + j
                    eng.wait_ge(k_saved, x * 4 + 4)
                    eng.wait_ge(q_staged, x + 1)
                    if not (first and j == 0):
                        eng.wait_ge(exps_done, x * 2)
                    steady(eng)
                    for a, e in ((0, 512), (512, NS), (1024, 1536)):
                        eng.matmul(SD[:, a // 512, 0:e - a], qst[:, j], ksb[:, j, a:e], start=True, stop=True)
                    eng.matmul(SD[:, 3, 0:1], qst[:, j], ksb[:, j, 1000:1001], start=True, stop=True).then_inc(scores_done, 1)
                    if after is not None:
                        turn_keys(*after)
                    eng.wait_ge(exps_done, x * 2 + 2)
                    if not (first and j == 0):
                        eng.wait_ge(pd_saved, x)
                    steady(eng)
                    for c in range(13):
                        a, w = (c * P, P if c < 7 else 65) if c < 8 else (1000 + (c - 8) * P, P if c < 12 else 1)
                        mm = eng.transpose(PT[0:w, c * GRP:(c + 1) * GRP], pd[:, a:a + w], ident[0:GRP, 0:GRP])
                    mm.then_inc(pd_turned, 1)
                    eng.wait_ge(pd_saved, x + 1)
                    if not (first and j == 0):
                        eng.wait_ge(od_saved, x * 2)
                    steady(eng)
                    for c in range(8):
                        w = P if c < 7 else 65
                        eng.matmul(OD[:, 0:HD], pTs[0:w, c, :], kv[0:w, 2 * r + j, c, 1, :], start=c == 0, stop=c == 7)
                    for c in range(5):
                        w = P if c < 4 else 1
                        mm = eng.matmul(OD[:, HD:2 * HD], pTs[0:w, 8 + c, :], wk[0:w, r, c, (2 + j) * HD:(3 + j) * HD], start=c == 0, stop=c == 4)
                    mm.then_inc(od_done, 1)
                turn_keys(0, 0, 0, 0)
                turns_ahead(eng, body)

            @block.vector
            def _(eng):
                eng.memset(pTs[:, :, :], 0.0)

                def save_keys(b, j, r, uses):
                    x = b * 2 + j
                    if not (isinstance(b, int) and b == 0):
                        eng.wait_ge(scores_done, x - 1)
                    eng.tensor_copy(qst[:, j], qT[:, GRP * j:GRP * j + GRP, bass.ds(b, 1)].rearrange("p h o -> p (h o)")).then_inc(q_staged, 1)
                    for go, (a, e) in enumerate(((0, 512), (512, NS), (1024, 1536), (1000, 1001))):
                        eng.wait_ge(k_turned, x * 4 + go + 1)
                        eng.tensor_copy(ksb[:, j, a:e], KT[:, go % 2, 0:e - a]).then_inc(k_saved, 1)

                def body(b, j, r, after):
                    first = isinstance(b, int) and b == 0
                    x = b * 2 + j
                    eng.wait_ge(scores_done, x + 1)
                    if not (first and j == 0):
                        eng.wait_ge(exps_done, x * 2)
                    eng.tensor_reduce(nmx[:, 0:1], SD[:, 0:2, :].rearrange("p a c -> p (a c)")[:, 0:NS], AX.X, ALU.max, negate=True).then_inc(max_done, 1)
                    eng.tensor_reduce(nmx[:, 1:2], SD[:, 2:4, :].rearrange("p a c -> p (a c)")[:, 0:NW], AX.X, ALU.max, negate=True).then_inc(max_done, 1)
                    if after is not None:
                        save_keys(*after)
                    eng.wait_ge(pd_turned, x + 1)
                    if not (first and j == 0):
                        eng.wait_ge(od_done, x)
                    p3 = PT[:, 0:13 * GRP].rearrange("p (c h) -> p c h", h=GRP)
                    eng.tensor_copy(pTs[:, 0:7, :], p3[:, 0:7, :])
                    eng.tensor_copy(pTs[0:65, 7, :], p3[0:65, 7, :])
                    eng.tensor_copy(pTs[:, 8:12, :], p3[:, 8:12, :])
                    eng.drain()
                    eng.tensor_copy(pTs[0:1, 12, :], p3[0:1, 12, :]).then_inc(pd_saved, 1)
                    eng.reciprocal(sums[:, 2:4], sums[:, 0:2])
                    eng.drain()
                    eng.wait_ge(od_done, x + 1)
                    for k, o in enumerate((oS, oW)):
                        eng.tensor_scalar(o[:, bass.ds(x, 1), :].rearrange("p o d -> p (o d)"), OD[:, k * HD:(k + 1) * HD], sums[:, 2 + k:3 + k], None, ALU.mult).then_inc(od_saved, 1)
                save_keys(0, 0, 0, 0)
                turns_ahead(eng, body)

            @block.scalar
            def _(eng):
                def body(b, j, r, uses):
                    first = isinstance(b, int) and b == 0
                    x = b * 2 + j
                    eng.wait_ge(max_done, 2 * x + 1)
                    if not (first and j == 0):
                        eng.wait_ge(pd_turned, x)
                        eng.wait_ge(od_saved, x * 2)
                    eng.activation(pd[:, 0:NS], SD[:, 0:2, :].rearrange("p a c -> p (a c)")[:, 0:NS], ACT.Exp, bias=nmx[:, 0:1], accum_out=sums[:, 0:1]).then_inc(exps_done, 1)
                    eng.wait_ge(max_done, 2 * x + 2)
                    eng.activation(pd[:, 1000:1000 + NW], SD[:, 2:4, :].rearrange("p a c -> p (a c)")[:, 0:NW], ACT.Exp, bias=nmx[:, 1:2], accum_out=sums[:, 1:2]).then_inc(exps_done, 1)
                turns(eng, body)


def mix_out(nc, io, g):
    with ExitStack() as ctx:
        sb = lambda n, s, t=F32: ctx.enter_context(nc.sbuf_tensor(n, s, t))
        ps = lambda n, s, t=F32: ctx.enter_context(nc.psum_tensor(n, s, t))
        sem = lambda n: g["sem"](n)
        NTILE = TILES + 1
        rows = lambda n: P if n < TILES else NB
        mix, ident, gates = g["mix"], g["ident"], g["gates"]
        hT = g["late"][:, 0:KT * TOK].rearrange("p (k t) -> p k t", k=KT)
        w = sb("w_out_sb", [P, KT, D])
        gout = sb("g_out_rows", [P, D])
        gffn = sb("g_ffn_col", [P, KT])
        x = sb("x_again", [P, 2, D])
        h = sb("h_rows", [P, 2, D])
        sq = sb("mix_squares", [P, D])
        junk = sb("h_squares", [P, D])
        half = sb("minus_half2", [P, 16])
        s16 = sb("mix_ss", [P, 2, 16])
        ss = sb("h_ss", [P, 2, 2])
        mn = sb("mix_normed", [P, 2, D])
        mT = sb("mix_turned", [P, 2, KT, P])
        hn = sb("h_normed", [P, 2, D])
        o3 = sb("o_dec_rows", [NB, 3, 512])
        px = ps("px2", [P, 2, 512])
        py = ps("py2", [P, 2, 512])
        ph = ps("ph2", [P, 2, 2, 512])
        c_loaded, dec_loaded = map(sem, ("c_loaded2", "dec_loaded"))
        w_loaded = [sem("w_out_loaded0"), sem("w_out_loaded1")]
        x_loaded = [sem("x_again0"), sem("x_again1")]
        stored = [sem("h_stored0"), sem("h_stored1")]
        names = ("mix_ready", "squared", "summed2", "rstd16", "mix_normed_s", "mix_turned_s", "mix_saved", "projected",
                 "h_done", "h_squared", "h_rstd", "h_normed_s", "h_turned", "h_saved")
        mix_ready, squared, summed, rstd16, normed, turned, mT_saved, projected, h_done, h_squared, h_rstd, h_normed, h_turned, h_saved = map(sem, names)

        with nc.Block() as block:
            @block.sync
            def _(eng):
                def store(eng, n):
                    R, u = rows(n), n % 2
                    eng.wait_ge(h_done, n + 1)
                    eng.dma_start(io["h_s"][n * P:n * P + R, :], h[0:R, u, :]).then_inc(stored[u], 16)

                eng.dma_start(gout[:, 0:512], io["g_out_nsa"][0].rearrange("h d -> (h d)").partition_broadcast(P)).then_inc(c_loaded, 16)
                eng.dma_start(gout[:, 512:D], io["g_out_sb"][0].rearrange("h d -> (h d)").partition_broadcast(P)).then_inc(c_loaded, 16)
                eng.dma_start(gffn[:, :], io["g_ffn"].rearrange("a (k p) -> p (a k)", p=P), allow_slow_non_contiguous=True).then_inc(c_loaded, 16)
                eng.dma_start(o3[:, :, :], io["o_s"].rearrange("c b n -> b c n")).then_inc(dec_loaded, 16)
                eng.dma_start(mix[0:NB, TILES, 512:D], io["osb_s"]).then_inc(dec_loaded, 16)
                for c in range(2):
                    cols = slice(c * 512, (c + 1) * 512)
                    eng.dma_start(w[:, :, cols], io["w_out"][0].rearrange("(k p) n -> p k n", p=P)[:, :, cols]).then_inc(w_loaded[c], 16)
                for n in range(NTILE):
                    R, u = rows(n), n % 2
                    if n >= 2:
                        eng.wait_ge(h_done, n - 1)
                    src = io["x_prompt"][0, n * P:(n + 1) * P, :] if n < TILES else io["x_sample"].rearrange("b t d -> (b t) d")
                    eng.dma_start(x[0:R, u, :], src).then_inc(x_loaded[u], 16)
                    if n >= 1:
                        store(eng, n - 1)
                store(eng, TILES)
                eng.wait_ge(stored[0], 80)
                eng.wait_ge(stored[1], 64)

            @block.gpsimd
            def _(eng):
                eng.memset(half[:, :], -0.5)
                eng.drain()

                def mix_power(n):
                    R, u = rows(n), n % 2
                    eng.wait_ge(summed, n + 1)
                    eng.tensor_scalar(s16[0:R, u, :], s16[0:R, u, :], 1.0 / HD, EPS, ALU.mult, ALU.add)
                    eng.drain()
                    eng.tensor_tensor(s16[0:R, u, :], s16[0:R, u, :], half[0:R, :], ALU.pow).then_inc(rstd16, 1)

                mix_power(0)
                mix_power(1)
                for n in range(NTILE):
                    if n + 2 < NTILE:
                        mix_power(n + 2)
                    R, u = rows(n), n % 2
                    eng.wait_ge(h_squared, n + 1)
                    eng.tensor_scalar(ss[0:R, u, 1:2], ss[0:R, u, 0:1], 1.0 / D, EPS, ALU.mult, ALU.add)
                    eng.drain()
                    eng.tensor_tensor(ss[0:R, u, 1:2], ss[0:R, u, 1:2], half[0:R, 0:1], ALU.pow).then_inc(h_rstd, 1)

            @block.scalar
            def _(eng):
                def square_mix(n):
                    R = rows(n)
                    if n == TILES:
                        eng.wait_ge(mix_ready, 1)
                        eng.wait_ge(dec_loaded, 32)
                    if n >= 1:
                        eng.wait_ge(summed, n)
                    eng.activation(sq[0:R, :], mix[0:R, n, :], ACT.Square).then_inc(squared, 1)

                def save_mT(n):
                    R, u = rows(n), n % 2
                    if n >= 2:
                        eng.wait_ge(projected, n - 1)
                    for b in range(2):
                        eng.wait_ge(turned, 2 * n + b + 1)
                        eng.activation(mT[:, u, 4 * b:4 * b + 4, 0:R], px[:, b, :].rearrange("p (k r) -> p k r", k=4)[:, :, 0:R], ACT.Copy).then_inc(mT_saved, 1)

                square_mix(0)
                square_mix(1)
                save_mT(0)
                for n in range(NTILE):
                    R, u = rows(n), n % 2
                    if n + 2 < NTILE:
                        square_mix(n + 2)
                    if n + 1 < NTILE:
                        save_mT(n + 1)
                    eng.wait_ge(h_done, n + 1)
                    if n >= 2:
                        eng.wait_ge(h_normed, n - 1)
                    eng.drain()
                    eng.activation(junk[0:R, :], h[0:R, u, :], ACT.Square, accum_out=ss[0:R, u, 0:1]).then_inc(h_squared, 1)

            @block.tensor
            def _(eng):
                def turn(n, src, ready, bank, saved, done):
                    R, u = rows(n), n % 2
                    eng.wait_ge(ready, n + 1)
                    for b in range(2):
                        if n >= 1:
                            eng.wait_ge(saved, 2 * (n - 1) + b + 1)
                        for k in range(4):
                            c = (4 * b + k) * P
                            mm = eng.transpose(bank[:, b, k * P:k * P + R], src[0:R, u, c:c + P], ident[0:R, 0:R])
                        mm.then_inc(done, 1)

                turn(0, mn, normed, px, mT_saved, turned)
                for n in range(NTILE + 1):
                    if n < NTILE:
                        R, u = rows(n), n % 2
                        eng.wait_ge(mT_saved, 2 * n + 2)
                        if n >= 2:
                            eng.wait_ge(h_done, n - 1)
                        for c in range(2):
                            if n == 0:
                                eng.wait_ge(w_loaded[c], 16)
                            for k in range(KT):
                                mm = eng.matmul(ph[0:R, u, c, :], mT[:, u, k, 0:R], w[:, k, c * 512:(c + 1) * 512], start=k == 0, stop=k == KT - 1)
                            if c == 0 and n + 1 < NTILE:
                                turn(n + 1, mn, normed, px, mT_saved, turned)
                        mm.then_inc(projected, 1)
                    if n >= 1:
                        turn(n - 1, hn, h_normed, py, h_saved, h_turned)

            @block.vector
            def _(eng):
                eng.wait_ge(c_loaded, 48)
                eng.wait_ge(dec_loaded, 32)
                m = mix[0:NB, TILES, 0:512].rearrange("b (h d) -> b h d", h=NH)
                for br in range(3):
                    o = o3[:, br, :].rearrange("b (h d) -> b h d", h=NH)
                    gt = gates[0:NB, TILES, br:24:3].unsqueeze(2).broadcast_to([NB, NH, HD])
                    eng.tensor_tensor(o, o, gt, ALU.mult)
                eng.drain()
                o = [o3[:, br, :].rearrange("b (h d) -> b h d", h=NH) for br in range(3)]
                eng.tensor_tensor(m, o[0], o[1], ALU.add)
                eng.drain()
                eng.tensor_tensor(m, m, o[2], ALU.add).then_inc(mix_ready, 1)

                def norm_mix(n):
                    R, u = rows(n), n % 2
                    eng.wait_ge(squared, n + 1)
                    if n >= 2:
                        eng.wait_ge(turned, 2 * (n - 1))
                    eng.tensor_reduce(s16[0:R, u, :], sq[0:R, :].rearrange("p (h d) -> p h d", h=16), AX.X, ALU.add).then_inc(summed, 1)
                    eng.wait_ge(rstd16, n + 1)
                    eng.drain()
                    eng.tensor_tensor(mn[0:R, u, :].rearrange("p (h d) -> p h d", h=16), mix[0:R, n, :].rearrange("p (h d) -> p h d", h=16),
                                      s16[0:R, u, :].unsqueeze(2).broadcast_to([R, 16, HD]), ALU.mult)
                    eng.drain()
                    eng.tensor_tensor(mn[0:R, u, :], mn[0:R, u, :], gout[0:R, :], ALU.mult).then_inc(normed, 1)

                norm_mix(0)
                norm_mix(1)
                for n in range(NTILE + 1):
                    if n + 2 < NTILE:
                        norm_mix(n + 2)
                    if n < NTILE:
                        R, u = rows(n), n % 2
                        eng.wait_ge(projected, n + 1)
                        eng.wait_ge(x_loaded[u], 16 * (n // 2) + 16)
                        if n >= 2:
                            eng.wait_ge(stored[u], 16 * (n // 2))
                            eng.wait_ge(h_squared, n - 1)
                        eng.tensor_tensor(h[0:R, u, :], ph[0:R, u, :, :].rearrange("p c n -> p (c n)"), x[0:R, u, :], ALU.add).then_inc(h_done, 1)
                        eng.wait_ge(h_rstd, n + 1)
                        if n >= 2:
                            eng.wait_ge(h_turned, 2 * (n - 1))
                        eng.tensor_scalar(hn[0:R, u, :], h[0:R, u, :], ss[0:R, u, 1:2], None, ALU.mult).then_inc(h_normed, 1)
                    if n >= 1:
                        R = rows(n - 1)
                        for b in range(2):
                            eng.wait_ge(h_turned, 2 * (n - 1) + b + 1)
                            out = hT[:, 4 * b:4 * b + 4, (n - 1) * P:(n - 1) * P + R]
                            eng.tensor_tensor(out, py[:, b, :].rearrange("p (k r) -> p k r", k=4)[:, :, 0:R],
                                              gffn[:, 4 * b:4 * b + 4].unsqueeze(2).broadcast_to([P, 4, R]), ALU.mult).then_inc(h_saved, 1)


def swiglu(nc, io, g):
    NF, NC, CW, KH = DFF // P, 3, TOK // 3, KT // 2
    NTILE = TILES + 1
    rows = lambda n: P if n < TILES else NB
    with ExitStack() as ctx:
        sb = lambda n, s, t=F32: ctx.enter_context(nc.sbuf_tensor(n, s, t))
        late = g["late"]
        hT = late[:, 0:KT * TOK].rearrange("p (k t) -> p k t", k=KT)
        act = sb("swiglu_act", [P, NF, TOK])
        QW = D // 4
        wd_raw = late[:, 0:2 * NF * QW].rearrange("p (u f n) -> p u f n", u=2, f=NF)
        wd_loaded = [g["sem"](f"wd_loaded{q}") for q in range(4)]
        wdv = io["w_down"][0].rearrange("(f p) (q n) -> q p f n", p=P, q=4)
        with ExitStack() as c2:
            sem = lambda n: g["sem"](n)
            hT_hi = c2.enter_context(nc.sbuf_tensor("h_turned_hi", [P, KT, TOK], F32R))
            hT_lo = c2.enter_context(nc.sbuf_tensor("h_turned_lo", [P, KT, TOK], F32R))
            rest = late[:, KT * TOK:]
            raw = rest[:, 0:KT * P].rearrange("p (h k f) -> p h k f", h=2, k=KH)
            sg = rest[:, KT * P:KT * P + NC * CW].rearrange("p (c t) -> p c t", c=NC)
            w_hi = c2.enter_context(nc.sbuf_tensor("w_gu_hi", [P, 2, KH, P], F32R))
            w_lo = c2.enter_context(nc.sbuf_tensor("w_gu_lo", [P, 2, KH, P], F32R))
            pg = c2.enter_context(nc.psum_tensor("pg", [P, 2, NC, 512], F32))
            w_loaded = [sem("w_gu_loaded0"), sem("w_gu_loaded1")]
            hi_done, lo_done, up_done, silu_done, act_done = map(sem, ("w_hi_done", "w_lo_done", "up_done", "silu_done", "act_done"))
            h_hi_done, h_lo_done = sem("h_hi_done"), sem("h_lo_done")

            def loop(eng, body):
                body(0, True, False)
                with eng.Fori(1, NF - 1) as f:
                    body(f, False, False)
                body(NF - 1, False, True)

            with nc.Block() as block:
                @block.sync
                def _(eng):
                    wv = io["w_gate_up"][0].rearrange("(k p) (c f) -> p k c f", p=P, c=2)

                    def body(f, first, last):
                        for e in range(2):
                            for h in range(2):
                                if not (first and e == 0):
                                    eng.wait_ge(lo_done, f * 4 + 2 * e + h - 1)
                                eng.dma_start(raw[:, h], wv[:, KH * h:KH * h + KH, e, bass.ds(f * P, P)]).then_inc(w_loaded[h], 16)
                        if first:
                            eng.wait_ge(h_lo_done, NC)
                            eng.dma_start(wd_raw[:, 0], wdv[0]).then_inc(wd_loaded[0], 16)
                    loop(eng, body)

                @block.tensor
                def _(eng):
                    def body(f, first, last):
                        for e in range(2):
                            for h in range(2):
                                eng.wait_ge(lo_done, f * 4 + 2 * e + h + 1)
                                for c in range(NC):
                                    if first and e == 0 and h == 0:
                                        eng.wait_ge(h_lo_done, c + 1)
                                    if not first and h == 0:
                                        eng.wait_ge((silu_done, act_done)[e], (f - 1) * NC + c + 1)
                                    cols = slice(c * CW, (c + 1) * CW)
                                    for j in range(KH):
                                        k = KH * h + j
                                        eng.matmul(pg[:, e, c, 0:CW], w_hi[:, h, j, :], hT_hi[:, k, cols], start=k == 0, stop=False)
                                        eng.matmul(pg[:, e, c, 0:CW], w_hi[:, h, j, :], hT_lo[:, k, cols], start=False, stop=False)
                                        mm = eng.matmul(pg[:, e, c, 0:CW], w_lo[:, h, j, :], hT_hi[:, k, cols], start=False, stop=k == KT - 1)
                                    mm.then_inc(up_done, 1)
                    loop(eng, body)

                @block.scalar
                def _(eng):
                    def round_unit(f, v, first=False):
                        eng.wait_ge(w_loaded[v % 2], (f * 2 + v // 2) * 16 + 16)
                        if not first:
                            eng.wait_ge(up_done, f * 4 * NC + (v - 1) * NC)
                        eng.activation(w_hi[:, v % 2], raw[:, v % 2], ACT.Copy).then_inc(hi_done, 1)

                    def round_rows(c):
                        cols = slice(c * CW, (c + 1) * CW)
                        eng.activation(hT_hi[:, :, cols], hT[:, :, cols], ACT.Copy).then_inc(h_hi_done, 1)

                    def body(f, first, last):
                        if first:
                            round_unit(0, 0, True)
                            round_rows(0)
                            round_unit(0, 1, True)
                            round_rows(1)
                            round_rows(2)
                        round_unit(f, 2)
                        round_unit(f, 3)
                        for c in range(NC):
                            eng.wait_ge(up_done, f * 4 * NC + NC + c + 1)
                            if not first:
                                eng.wait_ge(act_done, (f - 1) * NC + c + 1)
                            eng.activation(sg[:, c, :], pg[:, 0, c, 0:CW], ACT.Silu).then_inc(silu_done, 1)
                        if not last:
                            round_unit(f, 4)
                            round_unit(f, 5)
                    loop(eng, body)

                @block.vector
                def _(eng):
                    def rest_of_unit(f, v):
                        eng.wait_ge(hi_done, f * 4 + v + 1)
                        eng.tensor_tensor(w_lo[:, v % 2], raw[:, v % 2], w_hi[:, v % 2].bitcast(F32), ALU.subtract).then_inc(lo_done, 1)

                    def rest_of_rows(c):
                        cols = slice(c * CW, (c + 1) * CW)
                        eng.wait_ge(h_hi_done, c + 1)
                        eng.tensor_tensor(hT_lo[:, :, cols], hT[:, :, cols], hT_hi[:, :, cols].bitcast(F32), ALU.subtract).then_inc(h_lo_done, 1)

                    def body(f, first, last):
                        if first:
                            rest_of_unit(0, 0)
                            rest_of_rows(0)
                            rest_of_unit(0, 1)
                            rest_of_rows(1)
                            rest_of_rows(2)
                        rest_of_unit(f, 2)
                        rest_of_unit(f, 3)
                        if not last:
                            rest_of_unit(f, 4)
                            rest_of_unit(f, 5)
                        for c in range(NC):
                            eng.wait_ge(silu_done, f * NC + c + 1)
                            eng.wait_ge(up_done, f * 4 * NC + 3 * NC + c + 1)
                            out = act[:, bass.ds(f, 1), c * CW:(c + 1) * CW].rearrange("p o t -> p (o t)")
                            eng.tensor_tensor(out, sg[:, c, :], pg[:, 1, c, 0:CW], ALU.mult).then_inc(act_done, 1)
                    loop(eng, body)
        with ExitStack() as c2:
            sem = lambda n: g["sem"](n)
            py = c2.enter_context(nc.psum_tensor("py3", [P, 4, 512], F32))
            HF = NF // 2
            a_hi = c2.enter_context(nc.sbuf_tensor("act_hi", [P, 2, HF, P], F32R))
            a_lo = c2.enter_context(nc.sbuf_tensor("act_lo", [P, 2, HF, P], F32R))
            wd_hi = c2.enter_context(nc.sbuf_tensor("w_down_hi", [P, NF, QW], F32R))
            wd_lo = c2.enter_context(nc.sbuf_tensor("w_down_lo", [P, NF, QW], F32R))
            hr = c2.enter_context(nc.sbuf_tensor("h_back", [P, 4, QW], F32))
            y = c2.enter_context(nc.sbuf_tensor("y_rows", [P, 2, QW], F32))
            h_loaded = [sem(f"h_back{r}") for r in range(4)]
            y_done, a_used = sem("y_done"), sem("a_used")
            a_hi_done, a_lo_done, wd_hi_done, wd_lo_done = map(sem, ("a_hi_done", "a_lo_done", "wd_hi_done", "wd_lo_done"))
            stored = [sem("y_stored0"), sem("y_stored1")]
            jobs = [(q, n) for q in range(4) for n in range(NTILE)]
            PIECES = [(0, 6), (6, HF), (HF, 17), (17, NF)]

            def load_h(eng, m):
                q, n = jobs[m]
                R = rows(n)
                if m >= 4:
                    eng.wait_ge(y_done, m - 3)
                eng.dma_start(hr[0:R, m % 4], io["h_s"][n * P:n * P + R, q * QW:(q + 1) * QW]).then_inc(h_loaded[m % 4], 16)

            with nc.Block() as block:
                @block.sync
                def _(eng):
                    eng.dma_start(wd_raw[:, 1], wdv[1]).then_inc(wd_loaded[1], 16)
                    for m, (q, n) in enumerate(jobs):
                        load_h(eng, m)
                        if n == 3 and q + 2 < 4:
                            eng.wait_ge(wd_lo_done, 4 * q + 4)
                            eng.dma_start(wd_raw[:, q % 2], wdv[q + 2]).then_inc(wd_loaded[q + 2], 16)

                @block.gpsimd
                def _(eng):
                    for m, (q, n) in enumerate(jobs):
                        R = rows(n)
                        dst = io["y_prompt"][n * P:(n + 1) * P] if n < TILES else io["y_sample"]
                        eng.wait_ge(y_done, m + 1)
                        eng.dma_start(dst[:, q * QW:(q + 1) * QW], y[0:R, m % 2]).then_inc(stored[m % 2], 16)
                    for s in stored:
                        eng.wait_ge(s, 16 * len(jobs) // 2)

                @block.tensor
                def _(eng):
                    for m, (q, n) in enumerate(jobs):
                        if m >= 4:
                            eng.wait_ge(y_done, m - 3)
                        out = py[:, m % 4, 0:QW]
                        for f in range(NF):
                            h, j = f // HF, f % HF
                            if j == 0:
                                eng.wait_ge(a_lo_done, 2 * m + h + 1)
                            for i, (a, e) in enumerate(PIECES):
                                if n == 0 and f == a:
                                    eng.wait_ge(wd_lo_done, 4 * q + i + 1)
                            eng.matmul(out, a_hi[:, h, j, :], wd_hi[:, f, :], start=f == 0, stop=False)
                            eng.matmul(out, a_hi[:, h, j, :], wd_lo[:, f, :], start=False, stop=False)
                            mm = eng.matmul(out, a_lo[:, h, j, :], wd_hi[:, f, :], start=False, stop=f == NF - 1)
                            if j == HF - 1:
                                mm.then_inc(a_used, 1)

                def unit(m, h):
                    n = jobs[m][1]
                    R = rows(n)
                    return act[:, h * HF:(h + 1) * HF, n * P:n * P + R], a_hi[:, h, :, 0:R], a_lo[:, h, :, 0:R]

                @block.scalar
                def _(eng):
                    for m, (q, n) in enumerate(jobs):
                        for h in range(2):
                            if m:
                                eng.wait_ge(a_used, 2 * m + h - 1)
                            src, hi, lo = unit(m, h)
                            eng.activation(hi, src, ACT.Copy).then_inc(a_hi_done, 1)
                            if n == 0:
                                if h == 0:
                                    eng.wait_ge(wd_loaded[q], 16)
                                for a, e in PIECES[2 * h:2 * h + 2]:
                                    eng.activation(wd_hi[:, a:e, :], wd_raw[:, q % 2, a:e, :], ACT.Copy).then_inc(wd_hi_done, 1)

                @block.vector
                def _(eng):
                    def add_row(m):
                        q, n = jobs[m]
                        R = rows(n)
                        eng.wait_ge(a_used, 2 * m + 2)
                        eng.wait_ge(h_loaded[m % 4], 16 * (m // 4) + 16)
                        if m >= 2:
                            eng.wait_ge(stored[m % 2], 16 * (m // 2))
                        eng.tensor_tensor(y[0:R, m % 2], py[0:R, m % 4, 0:QW], hr[0:R, m % 4], ALU.add).then_inc(y_done, 1)

                    for m, (q, n) in enumerate(jobs):
                        for h in range(2):
                            src, hi, lo = unit(m, h)
                            eng.wait_ge(a_hi_done, 2 * m + h + 1)
                            eng.tensor_tensor(lo, src, hi.bitcast(F32), ALU.subtract).then_inc(a_lo_done, 1)
                            if n == 0:
                                for i in (2 * h, 2 * h + 1):
                                    a, e = PIECES[i]
                                    eng.wait_ge(wd_hi_done, 4 * q + i + 1)
                                    eng.tensor_tensor(wd_lo[:, a:e, :], wd_raw[:, q % 2, a:e, :], wd_hi[:, a:e, :].bitcast(F32), ALU.subtract).then_inc(wd_lo_done, 1)
                        if m:
                            add_row(m - 1)
                    add_row(len(jobs) - 1)


_INS = ["x_prompt", "x_sample", "cache_nsa_kv", "cache_sb_kv", "state_nsa_window", "page_table", "g_attn", "w_in",
        "g_q", "g_k", "w_cmp1_k", "w_cmp2_k", "pe_cmp_k", "w_cmp1_v", "w_cmp2_v", "pe_cmp_v", "g_out_nsa",
        "g_out_sb", "w_out", "g_ffn", "w_gate_up", "w_down"]

_OUTS = [("y_prompt", (1, SEQ, D)), ("y_sample", (NB, 1, D)), ("nsa_p", (1, 1, SEQ, 4, KVH, HD)), ("nsa_s", (1, NB, 1, 4, KVH, HD)),
         ("sb_p", (1, 1, SEQ, 2, NH, HD)), ("sb_s", (1, NB, 1, 2, NH, HD)),
         ("win_p_out", (1, 1, WINDOW, 2, KVH, HD)), ("win_s_out", (1, NB, WINDOW, 2, KVH, HD))]


def build(nc, io):
    with ExitStack() as ctx:
        sb = lambda n, s, t=F32: ctx.enter_context(nc.sbuf_tensor(n, s, t))
        taken = []

        def new_sem(name):
            taken.append(nc.alloc_semaphore(name))
            return taken[-1]

        def give_back():
            nc.all_engine_barrier()
            nc.clear_and_free_semaphores(taken)
            nc.all_engine_barrier()
            taken.clear()

        g = {"sem": new_sem, "ident": sb("ident", [P, P]), "gates": sb("gates", [P, TILES + 1, 24])}
        loaded = nc.alloc_semaphore("ident_loaded")
        with nc.Block() as block:
            @block.sync
            def _(eng):
                eng.dma_start(g["ident"][:, :], io["c_ident"]).then_inc(loaded, 16)
                eng.wait_ge(loaded, 16)
        project(nc, io, g)
        g["late"] = sb("late", [P, DFF // P * 512])
        with ExitStack() as mid:
            sm = lambda n, s, t=F32: mid.enter_context(nc.sbuf_tensor(n, s, t))
            g["mix"] = sm("mix", [P, TILES + 1, D])
            with ExitStack() as inner:
                si = lambda n, s, t=F32: inner.enter_context(nc.sbuf_tensor(n, s, t))
                g.update({"pt": si("page_table_sb", [1, NB * NPAGE], I32),
                          "kcp_hi": si("kc_prompt_hi", [HD, KVH, 64], F32R), "kcp_lo": si("kc_prompt_lo", [HD, KVH, 64], F32R), "vcp": si("vc_prompt", [64, KVH, HD + 1])})
                compress(nc, io, g)
                give_back()
                attend(nc, io, g)
                give_back()
                decode_nsa(nc, io, g)
                give_back()
            mix_out(nc, io, g)
        swiglu(nc, io, g)


def kernel(**inputs):
    import concourse.bacc as _bacc
    from concourse.bass_utils import run_bass_kernel_spmd as _run

    nc = _bacc.Bacc("TRN2", target_bir_lowering=False, num_devices=1)
    arrays, io = {}, {}
    for name in _INS:
        a = np.ascontiguousarray(inputs[name])
        if a.dtype.kind in "iu":
            a = a.astype(np.int32)
        arrays["in_" + name] = a
        io[name] = nc.dram_tensor("in_" + name, a.shape, mybir.dt.from_np(a.dtype), kind="ExternalInput").ap()
    for name, a in constants().items():
        arrays[name] = np.ascontiguousarray(a)
        io[name] = nc.dram_tensor(name, a.shape, F32, kind="ExternalInput").ap()
    outs = {n: nc.dram_tensor("out_" + n, s, F32, kind="ExternalOutput").ap() for n, s in _OUTS}
    flat = lambda ap: ap.rearrange("a b t c j d -> (a b t) (c j d)")
    for n in ("nsa_p", "nsa_s", "sb_p", "sb_s"):
        io[n] = flat(outs[n])
    io["y_prompt"] = outs["y_prompt"][0]
    io["y_sample"] = outs["y_sample"].rearrange("b t d -> (b t) d")
    io["win_p_out"] = flat(outs["win_p_out"])
    io["win_s_out"] = outs["win_s_out"][0].rearrange("b t c j d -> b t (c j d)")
    scratch = lambda n, s: nc.dram_tensor("scratch_" + n, s, F32, kind="Internal").ap()
    io["win_p"] = scratch("win_p", (SEQ, 256))
    io["win_new"] = scratch("win_new", (NB, 256))
    for part in ("T_hi", "T_lo"):
        io[part] = scratch(part, (NT * HD, SEQ))
    io["Ts"] = scratch("Ts", (NT * HD, NB))
    io["sbq_s"] = scratch("sbq_s", (NB, 512))
    io["osb_s"] = scratch("osb_s", (NB, 512))
    io["h_s"] = scratch("h_s", (TOK, D))
    io["cache_blocks"] = io["cache_nsa_kv"][0].rearrange("n (a s) f j d -> (n a) s (f j) d", a=2)
    io["o_s"] = scratch("o_s", (3, NB, 512))
    io["kcT_s"] = scratch("kcT_s", (HD, NB * KVH * NCS))
    io["vc_s"] = scratch("vc_s", (P, NB * KVH, 2, HD))
    io["cache_nsa"] = io["cache_nsa_kv"][0].rearrange("n (s r) f j d -> (n s) r (f j d)", r=2)
    io["cache_sb"] = io["cache_sb_kv"][0].rearrange("n s c h d -> (n s) c (h d)")
    io["state"] = io["state_nsa_window"][0].rearrange("b t c j d -> b t (c j d)")
    nc.disable_value_cache = True
    build(nc, io)
    r = _run(nc, [arrays], core_ids=[0])
    return tuple(r.results[0]["out_" + n] for n, _ in _OUTS)
```
